# Optimizing a Trainium2 kernel written in Bass

```python
import math
import jax, jax.numpy as jnp
from jax import lax
import numpy as np

D_MODEL = 1024
BATCH = 1
SEQ = 512
DEPTH = 1

N_META = 16
CHUNK = 64
PAD = CHUNK - N_META
M_HEADS = 4
R_HEADS = 4
HEAD_DIM = D_MODEL // (M_HEADS + R_HEADS)
M_WIDTH = M_HEADS * HEAD_DIM
R_WIDTH = R_HEADS * HEAD_DIM
MIX_WIDTH = M_WIDTH + R_WIDTH
PROJ_WIDTH = 4 * M_WIDTH + 4 * R_WIDTH + 2 * M_HEADS
PEER_HEADS = 8
PEER_KEYS = 128
PEER_EXPERTS = PEER_KEYS * PEER_KEYS
PEER_TOPK = 16
PEER_QDIM = 256
PEER_TOKEN_BLOCK = 256
ROPE_BASE = 10000.0
EPS = 1e-6

kernel_name = "hymba_mlstm_retnet_peer_block"

F32 = jnp.float32

def rmsnorm(x, w):
    xf = x.astype(F32)
    y = xf * lax.rsqrt(jnp.mean(xf * xf, axis=-1, keepdims=True) + EPS) * w.astype(F32)
    return y.astype(x.dtype)

def head_norm(x, w):
    H, d = x.shape[1], x.shape[3]
    mu = jnp.mean(x, axis=-1, keepdims=True)
    xc = x - mu
    var = jnp.mean(xc * xc, axis=-1, keepdims=True)
    return xc * lax.rsqrt(var + EPS) * w.astype(F32).reshape(1, H, 1, d)

def split_heads(t, n_heads):
    B, L, _ = t.shape
    return t.reshape(B, L, n_heads, -1).transpose(0, 2, 1, 3)

def merge_heads(t):
    B, H, L, d = t.shape
    return t.transpose(0, 2, 1, 3).reshape(B, L, H * d)

def to_chunks(t):
    B, H, L, d = t.shape
    return t.reshape(B, H, L // CHUNK, CHUNK, d)

def rotary(x, pos):
    half = x.shape[-1] // 2
    inv_freq = ROPE_BASE ** (-jnp.arange(half, dtype=F32) / half)
    ang = pos[:, None] * inv_freq[None, :]
    cos, sin = jnp.cos(ang), jnp.sin(ang)
    x1, x2 = x[..., :half], x[..., half:]
    return jnp.concatenate([x1 * cos - x2 * sin, x1 * sin + x2 * cos], axis=-1)

def mlstm_heads(q, k, v, i_pre, f_pre):
    B, H, N, C, dk = k.shape
    dv = v.shape[-1]
    k = k * (dk ** -0.5)
    log_f = jax.nn.log_sigmoid(f_pre)
    log_i = i_pre
    b = jnp.cumsum(log_f, axis=-1)
    g = b[..., -1]
    a = g[..., None] - b + log_i

    def step(carry, inp):
        c_st, n_st, m_st = carry
        k_c, v_c, a_c, g_c = inp
        m_new = jnp.maximum(g_c + m_st, jnp.max(a_c, axis=-1))
        decay = jnp.exp(g_c + m_st - m_new)
        w = jnp.exp(a_c - m_new[..., None])
        kw = k_c * w[..., None]
        c_new = decay[..., None, None] * c_st + jnp.einsum('bhjk,bhjv->bhkv', kw, v_c)
        n_new = decay[..., None] * n_st + jnp.sum(kw, axis=2)
        return (c_new, n_new, m_new), (c_st, n_st, m_st)

    init = (jnp.zeros((B, H, dk, dv), F32), jnp.zeros((B, H, dk), F32), jnp.zeros((B, H), F32))
    xs = (jnp.moveaxis(k, 2, 0), jnp.moveaxis(v, 2, 0), jnp.moveaxis(a, 2, 0), jnp.moveaxis(g, 2, 0))
    _, (c_prev, n_prev, m_prev) = lax.scan(step, init, xs)
    c_prev = jnp.moveaxis(c_prev, 0, 2)
    n_prev = jnp.moveaxis(n_prev, 0, 2)
    m_prev = jnp.moveaxis(m_prev, 0, 2)

    causal = jnp.tril(jnp.ones((C, C), dtype=bool))
    d_log = b[..., :, None] - b[..., None, :] + log_i[..., None, :]
    d_log = jnp.where(causal, d_log, -jnp.inf)
    inter_log = b + m_prev[..., None]
    m_t = jnp.maximum(inter_log, jnp.max(d_log, axis=-1))
    w_inter = jnp.exp(inter_log - m_t)
    s = jnp.einsum('bhncd,bhnjd->bhncj', q, k) * jnp.exp(d_log - m_t[..., None])
    num = (w_inter[..., None] * jnp.einsum('bhncd,bhndv->bhncv', q, c_prev)
           + jnp.einsum('bhncj,bhnjv->bhncv', s, v))
    den = w_inter * jnp.einsum('bhncd,bhnd->bhnc', q, n_prev) + jnp.sum(s, axis=-1)
    return num / jnp.maximum(jnp.abs(den), jnp.exp(-m_t))[..., None]

def retention_heads(q, k, v):
    B, H, N, C, dk = k.shape
    dv = v.shape[-1]
    k = k * (dk ** -0.5)
    log_gamma = jnp.log1p(-jnp.exp2(-5.0 - jnp.arange(H, dtype=F32)))
    idx = jnp.arange(C, dtype=F32)
    rel = idx[:, None] - idx[None, :]
    causal = rel >= 0
    decay_intra = jnp.where(causal, jnp.exp(log_gamma[:, None, None] * jnp.where(causal, rel, 0.0)), 0.0)
    decay_cross = jnp.exp(log_gamma[:, None] * (idx + 1.0))
    decay_state = jnp.exp(log_gamma[:, None] * (C - 1.0 - idx))
    decay_chunk = jnp.exp(log_gamma * C)
    kz = k * decay_state[None, :, None, :, None]

    def step(r_st, inp):
        k_c, v_c = inp
        r_new = decay_chunk[None, :, None, None] * r_st + jnp.einsum('bhjk,bhjv->bhkv', k_c, v_c)
        return r_new, r_st

    _, r_prev = lax.scan(step, jnp.zeros((B, H, dk, dv), F32), (jnp.moveaxis(kz, 2, 0), jnp.moveaxis(v, 2, 0)))
    r_prev = jnp.moveaxis(r_prev, 0, 2)
    s = jnp.einsum('bhncd,bhnjd->bhncj', q, k) * decay_intra[None, :, None]
    inner = jnp.einsum('bhncj,bhnjv->bhncv', s, v)
    cross = decay_cross[None, :, None, :, None] * jnp.einsum('bhncd,bhndv->bhncv', q, r_prev)
    return inner + cross

def mixer_sublayer(h, norm_w, w_in, gate_bias, m_norm_w, r_norm_w, w_out):
    B, L, _ = h.shape
    a = rmsnorm(h, norm_w)
    a = jnp.pad(a, ((0, 0), (PAD, 0), (0, 0)))
    Lp = L + PAD
    n_chunks = Lp // CHUNK
    proj = (a @ w_in).astype(F32)
    sizes = [M_WIDTH] * 4 + [R_WIDTH] * 4
    offsets = [int(o) for o in np.cumsum(sizes)]
    mq, mk, mv, mo, rq, rk, rv, rg, gates = jnp.split(proj, offsets, axis=-1)
    gates = gates + gate_bias.astype(F32)
    gates = gates.transpose(0, 2, 1).reshape(B, 2 * M_HEADS, n_chunks, CHUNK)
    i_pre, f_pre = gates[:, :M_HEADS], gates[:, M_HEADS:]

    h_m = mlstm_heads(to_chunks(split_heads(mq, M_HEADS)), to_chunks(split_heads(mk, M_HEADS)),
                      to_chunks(split_heads(mv, M_HEADS)), i_pre, f_pre)
    h_m = h_m.reshape(B, M_HEADS, Lp, HEAD_DIM)
    out_m = merge_heads(head_norm(jax.nn.sigmoid(split_heads(mo, M_HEADS)) * h_m, m_norm_w))

    pos = jnp.arange(Lp, dtype=F32) - PAD
    rq_h = rotary(split_heads(rq, R_HEADS), pos)
    rk_h = rotary(split_heads(rk, R_HEADS), pos)
    ret = retention_heads(to_chunks(rq_h), to_chunks(rk_h), to_chunks(split_heads(rv, R_HEADS)))
    ret = ret.reshape(B, R_HEADS, Lp, HEAD_DIM)
    out_r = merge_heads(jax.nn.silu(split_heads(rg, R_HEADS)) * head_norm(ret, r_norm_w))

    y = jnp.concatenate([out_m, out_r], axis=-1)[:, PAD:].astype(h.dtype)
    return y @ w_out

def peer_ffn(x, w_query, sub_keys, w_down, w_up):
    B, L, D = x.shape
    T = B * L
    TB = PEER_TOKEN_BLOCK
    n_blk = -(-T // TB)
    t = jnp.pad(x.reshape(T, D), ((0, n_blk * TB - T), (0, 0))).reshape(n_blk, TB, D)

    def block(xb):
        q = (xb @ w_query).astype(F32).reshape(TB, PEER_HEADS, 2, PEER_QDIM // 2)
        s = jnp.einsum('thpd,pnd->thpn', q, sub_keys.astype(F32))
        s1, i1 = lax.top_k(s[:, :, 0], PEER_TOPK)
        s2, i2 = lax.top_k(s[:, :, 1], PEER_TOPK)
        cand = (s1[..., :, None] + s2[..., None, :]).reshape(TB, PEER_HEADS, PEER_TOPK * PEER_TOPK)
        cidx = (i1[..., :, None] * PEER_KEYS + i2[..., None, :]).reshape(TB, PEER_HEADS, PEER_TOPK * PEER_TOPK)
        top, sel = lax.top_k(cand, PEER_TOPK)
        eidx = jnp.take_along_axis(cidx, sel, axis=-1)
        gate = jax.nn.softmax(top, axis=-1)
        u = jnp.take(w_down, eidx, axis=0)
        act = jax.nn.gelu(jnp.einsum('thkd,td->thk', u, xb).astype(F32), approximate=False)
        vv = jnp.take(w_up, eidx, axis=0)
        return jnp.einsum('thk,thkd->td', (gate * act).astype(xb.dtype), vv)

    out = lax.map(block, t).reshape(n_blk * TB, D)[:T]
    return out.reshape(B, L, D)

def setup_inputs(seed: int = 0) -> dict:
    key = jax.random.key(seed)
    ks = jax.random.split(key, 16)
    nrm = jax.random.normal
    x = nrm(ks[0], (BATCH, SEQ, D_MODEL), F32)
    meta_tokens = nrm(ks[1], (N_META, D_MODEL), F32)
    norm1_w = 1.0 + 0.01 * nrm(ks[2], (DEPTH, D_MODEL), F32)
    w_in = nrm(ks[3], (DEPTH, D_MODEL, PROJ_WIDTH), F32) * D_MODEL ** -0.5
    i_bias = 0.1 * nrm(ks[4], (DEPTH, M_HEADS), F32)
    f_bias = jnp.linspace(3.0, 6.0, M_HEADS, dtype=F32)[None, :] + 0.01 * nrm(ks[5], (DEPTH, M_HEADS), F32)
    gate_bias = jnp.concatenate([i_bias, f_bias], axis=-1)
    m_norm_w = 1.0 + 0.01 * nrm(ks[6], (DEPTH, M_WIDTH), F32)
    r_norm_w = 1.0 + 0.01 * nrm(ks[7], (DEPTH, R_WIDTH), F32)
    w_out = nrm(ks[8], (DEPTH, MIX_WIDTH, D_MODEL), F32) * MIX_WIDTH ** -0.5
    norm2_w = 1.0 + 0.01 * nrm(ks[9], (DEPTH, D_MODEL), F32)
    peer_w_query = nrm(ks[10], (DEPTH, D_MODEL, PEER_HEADS * PEER_QDIM), F32) * D_MODEL ** -0.5
    peer_sub_keys = nrm(ks[11], (DEPTH, 2, PEER_KEYS, PEER_QDIM // 2), F32) * (PEER_QDIM // 2) ** -0.5
    peer_w_down = nrm(ks[12], (DEPTH, PEER_EXPERTS, D_MODEL), F32) * D_MODEL ** -0.5
    peer_w_up = nrm(ks[13], (DEPTH, PEER_EXPERTS, D_MODEL), F32) * PEER_HEADS ** -0.5
    final_norm_w = 1.0 + 0.01 * nrm(ks[14], (D_MODEL,), F32)
    return {"x": x, "meta_tokens": meta_tokens, "norm1_w": norm1_w, "w_in": w_in,
            "gate_bias": gate_bias, "m_norm_w": m_norm_w, "r_norm_w": r_norm_w, "w_out": w_out,
            "norm2_w": norm2_w, "peer_w_query": peer_w_query, "peer_sub_keys": peer_sub_keys,
            "peer_w_down": peer_w_down, "peer_w_up": peer_w_up, "final_norm_w": final_norm_w}

def reference(x, meta_tokens, norm1_w, w_in, gate_bias, m_norm_w, r_norm_w, w_out, norm2_w,
              peer_w_query, peer_sub_keys, peer_w_down, peer_w_up, final_norm_w):
    B = x.shape[0]
    meta = jnp.broadcast_to(meta_tokens.astype(x.dtype)[None], (B, N_META, D_MODEL))
    h = jnp.concatenate([meta, x], axis=1)
    for l in range(DEPTH):
        h = h + mixer_sublayer(h, norm1_w[l], w_in[l], gate_bias[l], m_norm_w[l], r_norm_w[l], w_out[l])
        h = h + peer_ffn(rmsnorm(h, norm2_w[l]), peer_w_query[l], peer_sub_keys[l], peer_w_down[l], peer_w_up[l])
    return rmsnorm(h, final_norm_w)[:, N_META:]


_drawn_inputs = setup_inputs


def setup_inputs(seed=0):
    import zlib

    import numpy as np

    out = dict(_drawn_inputs(seed))
    spreads = {}
    factors = {'m_norm_w': 23.843, 'r_norm_w': 41.726, 'norm2_w': 21.29, 'final_norm_w': 33.123}
    for name, (base, spread) in spreads.items():
        noise = np.random.default_rng([zlib.crc32(name.encode()), seed]).standard_normal(out[name].shape)
        drawn = base * np.exp(spread * noise) if base else spread * noise
        out[name] = __import__('jax').numpy.asarray(drawn.astype(out[name].dtype))
    for name, factor in factors.items():
        out[name] = (out[name] * factor).astype(out[name].dtype)
    return out
```

```python
import math
from contextlib import ExitStack

import concourse.bass as bass
from concourse import mybir

F32 = mybir.dt.float32
F32R = mybir.dt.float32r
F16 = mybir.dt.float16
U32 = mybir.dt.uint32
ALU = mybir.AluOpType
ACT = mybir.ActivationFunctionType
AX = mybir.AxisListType

P = 128
D = 1024
KD = D // P
SEQ = 512
META = 16
TOK = SEQ + META
TT = SEQ // P
MH, RH = 4, 4
NH = MH + RH
PH = 8
TOPK = 16
EPS = 1e-6
SCALE = P ** -0.5
GSCALE = 4096.0

B_OUT = 4 * NH
B_QUERY = B_OUT + KD
B_DOWN = B_QUERY + 2 * PH
B_UP = B_DOWN + P
B_END = B_UP + P
RING = 4
LEAD = 2

PRE = 4
PLAIN = 12
BUILD = 16
POST = P - PRE - TT * (PLAIN + BUILD)
PIECES = 8
BATCH = 4
PER_TILE = P // BATCH // BUILD

COLS = [SEQ - P * j for j in range(TT)]
S_AT = [sum(COLS[:j]) for j in range(TT + 1)]
S_WIDTH = S_AT[TT] + SEQ

T_COS, T_SIN, T_DEC = 0, TOK, 2 * TOK
T_SWAP = T_DEC + RH * TOK
T_ONE = T_SWAP + P
T_MEAN = T_ONE + P
T_SEL = T_MEAN + P
T_END = T_SEL + MH * P


def mixer_peer_kernel(nc, x, meta, w_blocks, w_gates, gate_bias, gains, final_gain, keys, ident_in, table_in, out):
    a_dram = nc.dram_tensor("act_scratch", (P, P, SEQ), F32, kind="Internal").ap()
    g_dram = nc.dram_tensor("gate_scratch", (P, P, SEQ), F32, kind="Internal").ap()

    ctx = ExitStack()
    with ctx:
        def sb(name, shape, dt=F32, scope=ctx):
            return scope.enter_context(nc.sbuf_tensor(name, shape, dt))

        def sem(name):
            return ctx.enter_context(nc.semaphore(name))

        raw = sb("raw", [P, RING, D])
        w_h = sb("w_h", [P, RING, D], F32R)
        w_l = sb("w_l", [P, RING, D], F32R)
        xt_h = sb("xt_h", [P, KD, TOK], F32R)
        xt_l = sb("xt_l", [P, KD, TOK], F32R)
        acc = sb("acc", [P, TT, D])
        ident = sb("ident", [P, P])
        keys_t = sb("keys_t", [P, 2, P])
        gain = sb("gain", [P, 2 * KD + NH])
        sums = sb("sums", [P, 16])
        rstd = sb("rstd", [P, 16])
        fence_cell = sb("fence_cell", [P, 5])

        with ExitStack() as region:
            xn = sb("xn", [P, 2, D], scope=region)
            ntmp = sb("ntmp", [P, 2, KD, P], scope=region)
            junk = sb("junk", [P, D], scope=region)
            mt = sb("mt", [META, D], scope=region)
        with ExitStack() as region:
            topv = sb("topv", [P, TT, 2, PH, TOPK], scope=region)
            topi = sb("topi", [P, TT, 2, PH, TOPK], scope=region)
            cand = sb("cand", [P, PH, TOPK * TOPK], scope=region)
            tv = sb("tv", [P, PH, TOPK], scope=region)
            ti = sb("ti", [P, PH * TOPK], U32, scope=region)
            tj = sb("tj", [P, 2, PH * TOPK], U32, scope=region)
            tf = sb("tf", [P, 2, PH * TOPK], scope=region)
            dist = sb("dist", [P, PH, TOPK], scope=region)
            expd = sb("expd", [P, PH, TOPK], scope=region)
            den8 = sb("den8", [P, 2, PH], scope=region)
            route = sb("route", [P, 3, PH * TOPK], scope=region)
            eq = sb("eq", [P, PH * TOPK, TOPK], F16, scope=region)
            pick = sb("pick", [P, PH, TOPK, TOPK], F16, scope=region)
            gh16 = sb("gh16", [P, P], F16, scope=region)
            route_t = sb("route_t", [P, 3, P], scope=region)
        y_h = sb("y_h", [P, KD, SEQ], F32R)
        y_l = sb("y_l", [P, KD, SEQ], F32R)

        with ExitStack() as region:
            table = sb("table", [P, T_END], scope=region)
            qT = sb("qT", [P, 2, SEQ], scope=region)
            kT = sb("kT", [P, 2, TOK], scope=region)
            vT = sb("vT", [P, TOK], scope=region)
            v_tok = sb("v_tok", [P, 2, TT * P], scope=region)
            v_meta = sb("v_meta", [META, 2, P], scope=region)
            og = sb("og", [P, 2, SEQ], scope=region)
            eg = sb("eg", [P, SEQ], scope=region)
            decay = sb("decay", [P, S_WIDTH], scope=region)
            probs = sb("probs", [P, S_WIDTH], scope=region)
            floor = sb("floor", [P, SEQ], scope=region)
            hden = sb("hden", [P, SEQ], scope=region)
            hx = sb("hx", [P, SEQ], scope=region)
            hxc = sb("hxc", [P, SEQ], scope=region)
            hsq = sb("hsq", [P, SEQ], scope=region)
            hy = sb("hy", [P, SEQ], scope=region)
            q_raw = sb("q_raw", [P, SEQ], scope=region)
            k_raw = sb("k_raw", [P, TOK], scope=region)
            rot = sb("rot", [P, TOK], scope=region)
            gm = sb("gm", [MH, 2, TOK], scope=region)
            u_col = sb("u_col", [P, TT + 1, MH], scope=region)
            wg = sb("wg", [P, KD * 2 * MH], scope=region)
            wg_h = sb("wg_h", [P, KD * 2 * MH], F32R, scope=region)
            wg_l = sb("wg_l", [P, KD * 2 * MH], F32R, scope=region)
            gb = sb("gb", [MH, 2], scope=region)
        with ExitStack() as region:
            qx = sb("qx", [P, 2, SEQ], scope=region)
            sc = sb("sc", [P, 2, TT, P], scope=region)
            t8v = sb("t8v", [P, TT, 2, TOPK], scope=region)
            t8i = sb("t8i", [P, TT, 2, TOPK], U32, scope=region)
            sc_rest = sb("sc_rest", [P, 2, TT, P], scope=region)
        with ExitStack() as region:
            gchunk = sb("gchunk", [P, P, P], scope=region)
            onehot = sb("onehot", [P, 2, 3, BATCH, P], F16, scope=region)
            a_out = sb("a_out", [P, 2, SEQ], scope=region)
            iota16 = sb("iota16", [P, P], F16, scope=region)
            gate_h = sb("gate_h", [P, P], scope=region)
            gate_l = sb("gate_l", [P, P], scope=region)
        with ExitStack() as region:
            a_in = sb("a_in", [P, RING, SEQ], scope=region)
            g_in = sb("g_in", [P, RING, SEQ], scope=region)
            ga = sb("ga", [P, 2, SEQ], scope=region)
            fgain = sb("fgain", [P, D], scope=region)
            junk2 = sb("junk2", [P, D], scope=region)

        ps = ctx.enter_context(nc.psum_tensor("ps", [P, 8, 512], F32))

        w_loaded = [sem(f"w_loaded{i}") for i in range(RING)]
        w_hi, w_lo, w_used = sem("w_hi"), sem("w_lo"), sem("w_used")
        x_loaded = [sem(f"x_loaded{i}") for i in range(TT + 1)]
        c_loaded = sem("c_loaded")
        t_loaded = sem("t_loaded")
        nt_r, nt_xn, nt_tr, nt_f, nt_hi, nt_lo = (sem(n) for n in ("nt_r", "nt_xn", "nt_tr", "nt_f", "nt_hi", "nt_lo"))
        act_own, dve_own = sem("act_own"), sem("dve_own")
        wg_split_h, wg_split = sem("wg_split_h"), sem("wg_split")
        g_mm, g_an, g_ln, g_u, g_ut, g_ready = (sem(n) for n in ("g_mm", "g_an", "g_ln", "g_u", "g_ut", "g_ready"))
        pj_ev, s_done, p_done, pv_done, den_abs = (sem(n) for n in ("pj_ev", "s_done", "p_done", "pv_done", "den_abs"))
        x_ready, mean_done, xc_ready, sq_ready, var_done, rstd_done = (sem(n) for n in ("x_ready", "mean_done", "xc_ready", "sq_ready", "var_done", "rstd_done"))
        y_ready, y_hi, y_lo, o_exp = (sem(n) for n in ("y_ready", "y_hi", "y_lo", "o_exp"))
        vt_done, vt_ev, bc_done, d_done, masked, sw_done, rope_done = (sem(n) for n in ("vt_done", "vt_ev", "bc_done", "d_done", "masked", "sw_done", "rope_done"))
        mix_added = sem("mix_added")
        qx_ready, sc_done, sc_ev, sc_used = (sem(n) for n in ("qx_ready", "sc_done", "sc_ev", "sc_used"))
        iota_ready = sem("iota_ready")
        chunk_free, dist_ready, exp_ready, route_ready, route_tr, oh_ready, gm_done, g_ev = (
            sem(n) for n in ("chunk_free", "dist_ready", "exp_ready", "route_ready", "route_tr", "oh_ready", "gm_done", "g_ev"))
        a_ready = sem("a_ready")
        a_stored = [sem(f"a_stored{i}") for i in range(2)]
        ag_loaded = [sem(f"ag_loaded{i}") for i in range(RING)]
        ga_done, ga_hi, ga_lo = (sem(n) for n in ("ga_done", "ga_hi", "ga_lo"))
        f_loaded, res_added, f_r, f_done, stored = (sem(n) for n in ("f_loaded", "res_added", "f_r", "f_done", "stored"))

        block = ctx.enter_context(nc.Block())

        def table_cols(at, n, rows=P):
            return table[0:rows, at:at + n]

        @block.sync
        def _(sp):
            def known(v):
                return v if isinstance(v, int) else sp.snap(v)

            def load_weights(q, u):
                b = known(q * RING + u)
                free = known(q * RING + (u - RING + 1))
                if isinstance(q, int) and q * RING + u < RING:
                    sp.dma_start(raw[:, u, :], w_blocks[b, :, :]).then_inc(w_loaded[u], 16)
                    return
                if isinstance(q, int):
                    src = w_blocks[b, :, :]
                else:
                    src = w_blocks[bass.ds(b, 1), :, :].rearrange("o p n -> p (o n)")
                sp.wait_ge(w_lo, free)
                sp.dma_start(raw[:, u, :], src).then_inc(w_loaded[u], 16)

            for t in range(TT):
                sp.dma_start(acc[:, t, :], x[0, t * P:(t + 1) * P, :]).then_inc(x_loaded[t], 16)
                if t == 0:
                    sp.dma_start(gain[:, :], gains).then_inc(c_loaded, 16)
                    sp.dma_start(ident[:, :], ident_in).then_inc(c_loaded, 16)
            sp.dma_start(mt[:, :], meta).then_inc(x_loaded[TT], 16)
            sp.dma_start(wg[:, :], w_gates).then_inc(c_loaded, 16)
            sp.dma_start(gb[:, :], gate_bias).then_inc(c_loaded, 16)
            for u in range(RING):
                load_weights(0, u)
            sp.dma_start(table[:, :], table_in).then_inc(t_loaded, 16)
            sp.dma_start(keys_t[:, :, :], keys).then_inc(t_loaded, 16)
            with sp.Fori(1, (B_DOWN + PRE) // RING) as q:
                for u in range(RING):
                    load_weights(q, u)

            def store_act(q, u):
                n = known(q * RING + u)
                ready = known(q * RING + (u + 1))
                sp.wait_ge(a_ready, ready)
                if isinstance(q, int):
                    dst = a_dram[n, :, :]
                else:
                    dst = a_dram[bass.ds(n, 1), :, :].rearrange("o p t -> p (o t)")
                sp.dma_start(dst, a_out[:, u % 2, :]).then_inc(a_stored[u % 2], 16)

            g_view = g_dram.rearrange("j p t -> p j t")

            def store_chunk(r, piece):
                js = slice(piece * P // PIECES, (piece + 1) * P // PIECES)
                if piece == 0:
                    sp.wait_ge(g_ev, known(r * (P // BATCH) + P // BATCH))
                cols = slice(r * P, (r + 1) * P) if isinstance(r, int) else bass.ds(known(r * P), P)
                sp.dma_start(g_view[:, js, cols], gchunk[:, js, :]).then_inc(chunk_free, 16)

            def down_unit(q, chunk=None, piece0=0):
                for u in range(RING):
                    b_unit = q + (B_DOWN // RING + (u + 6) // RING)
                    load_weights(b_unit, (u + 6) % RING)
                    if chunk is not None and piece0 + u < PIECES:
                        store_chunk(chunk, piece0 + u)
                    store_act(q, u)

            for u in range(2):
                load_weights((B_DOWN + PRE) // RING, u)
            with sp.Fori(0, (PRE + PLAIN + BUILD) // RING) as i:
                down_unit(i)
            with sp.Fori(1, TT) as r:
                at = r * ((PLAIN + BUILD) // RING) + PRE // RING
                for i in range(PLAIN // RING):
                    down_unit(at + i, r - 1, i * RING)
                with sp.Fori(0, BUILD // RING) as i:
                    down_unit(at + i + PLAIN // RING)

            def load_ag(q, u, first=False):
                n = known(q * RING + u)
                free = known(q * RING + (u - RING + 1))
                if isinstance(q, int):
                    a_src, g_src = a_dram[n, :, :], g_dram[n, :, :]
                else:
                    a_src = a_dram[bass.ds(n, 1), :, :].rearrange("o p t -> p (o t)")
                    g_src = g_dram[bass.ds(n, 1), :, :].rearrange("o p t -> p (o t)")
                if not first:
                    sp.wait_ge(ga_done, free)
                sp.dma_start(a_in[:, u, :], a_src).then_inc(ag_loaded[u], 16)
                sp.dma_start(g_in[:, u, :], g_src).then_inc(ag_loaded[u], 16)

            for i in range(POST // RING - 1):
                down_unit((P - POST) // RING + i, TT - 1, i * RING)
            sp.wait_ge(chunk_free, 1 + 16 * PIECES * TT)
            for slot in range(2):
                sp.wait_ge(a_stored[slot], 16 * (P - RING) // 2)
            for u in range(RING):
                load_ag(0, u, first=True)
            down_unit(P // RING - 1)
            for slot in range(2):
                sp.wait_ge(a_stored[slot], 16 * P // 2)
            sp.dma_start(fgain[:, :], final_gain).then_inc(f_loaded, 16)
            def up_unit(q, weights=True):
                for u in range(RING):
                    if weights or u < RING - 6 % RING:
                        load_weights(q + (B_UP // RING + (u + 6) // RING), (u + 6) % RING)
                    load_ag(q + 1, u)

            with sp.Fori(0, P // RING - 2) as q:
                up_unit(q)
            up_unit(P // RING - 2, weights=False)
            for t in range(TT):
                sp.wait_ge(f_done, t + 1)
                sp.dma_start(out[0, t * P:(t + 1) * P, :], acc[:, t, :]).then_inc(stored, 16)
            sp.wait_ge(stored, 16 * TT)

        @block.gpsimd
        def _(pool):
            def split_low(q, u):
                pool.wait_ge(w_hi, q * RING + (u + 1))
                nc.gpsimd.tensor_tensor(w_l[:, u, :], raw[:, u, :], w_h[:, u, :].bitcast(F32), ALU.subtract).then_inc(w_lo, 1)

            for b in range(LEAD):
                split_low(0, b)
            for h in range(NH + 1):
                for s in range(4):
                    if h < NH:
                        b = 4 * h + s + LEAD
                        split_low(b // RING, b % RING)
                    if s == 0 and 1 <= h <= MH:
                        pool.wait_ge(d_done, h)
                        for j in range(TT):
                            blk = decay[:, S_AT[j]:S_AT[j] + P]
                            last = nc.gpsimd.affine_select(out=blk, in_=blk, compare_op=ALU.is_ge, fill=0.0, base=0,
                                                           pattern=[[1, P]], channel_multiplier=-1)
                        last.then_inc(masked, 1)
            for b in range(B_OUT + LEAD, B_OUT + RING):
                split_low(b // RING, b % RING)
            pool.wait_ge(w_used, B_OUT + 1)
            nc.gpsimd.iota(iota16[:, :], [[1, P]], base=0, channel_multiplier=0,
                           allow_small_or_imprecise_dtypes=True).then_inc(iota_ready, 1)
            with pool.Fori(B_OUT // RING + 1, B_DOWN // RING) as q:
                for u in range(RING):
                    split_low(q, u)
            with pool.Fori(B_DOWN // RING, B_END // RING) as q:
                for u in range(RING):
                    split_low(q, u)

        @block.scalar
        def _(act):
            own = [0]

            def link(ins):
                own[0] += 1
                ins.then_inc(act_own, 1)
                act.wait_ge(act_own, own[0])

            def split_high(q, u, first=False):
                act.wait_ge(w_loaded[u], q * 16 + 16)
                if not first:
                    act.wait_ge(w_used, q * RING + (u - RING + 1))
                nc.scalar.copy(w_h[:, u, :], raw[:, u, :]).then_inc(w_hi, 1)

            def high(b):
                split_high(b // RING, b % RING, first=b < RING)

            def inv_rms(src, n, scratch, ready, rows=P):
                link(nc.scalar.activation(scratch, src, ACT.Square, accum_out=sums[0:rows, n:n + 1]))
                link(nc.scalar.activation(sums[0:rows, n:n + 1], sums[0:rows, n:n + 1], ACT.Ln, bias=EPS, scale=1.0 / D))
                nc.scalar.activation(rstd[0:rows, n:n + 1], sums[0:rows, n:n + 1], ACT.Exp, scale=-0.5).then_inc(ready, 1)

            def high_xt(n):
                t = n if n <= TT else n - TT - 1
                cols = slice(t * P, t * P + P) if n != TT else slice(SEQ, TOK)
                width = P if n != TT else META
                act.wait_ge(nt_f, n + 1)
                nc.scalar.copy(xt_h[:, :, cols], ntmp[:, n % 2, :, 0:width]).then_inc(nt_hi, 1)

            nc.scalar.preload_act_table_set("natural_log_exp_and_others")

            for n in range(TT + 1):
                act.wait_ge(x_loaded[n], 16)
                src = acc[:, n, :] if n < TT else mt[:, :]
                rows = P if n < TT else META
                inv_rms(src, n, junk[0:rows, :], nt_r, rows)
                if n == TT:
                    act.wait_ge(c_loaded, 64)
                    nc.scalar.copy(wg_h[:, :], wg[:, :]).then_inc(wg_split_h, 1)
                if n >= 2:
                    high_xt(n - 2)
            high(0)
            high_xt(TT - 1)
            high(1)
            high_xt(TT)

            act.wait_ge(g_an, 1)
            link(nc.scalar.activation(hxc[0:MH, :], hx[0:MH, :], ACT.Exp))
            link(nc.scalar.activation(hxc[0:MH, 0:SEQ], hxc[0:MH, 0:SEQ], ACT.Ln, bias=1.0))
            act.wait_ge(g_an, 2)
            link(nc.scalar.activation(rot[0:MH, 0:META], rot[0:MH, 0:META], ACT.Exp))
            nc.scalar.activation(rot[0:MH, 0:META], rot[0:MH, 0:META], ACT.Ln, bias=1.0).then_inc(g_ln, 1)

            for h in range(NH + 1):
                is_m = h < MH
                pair = h % 2
                if h < NH:
                    high(4 * h + LEAD)
                if h >= 1:
                    g = h - 1
                    act.wait_ge(vt_done, g + 1)
                    if g >= 2:
                        act.wait_ge(pv_done, g - 1)
                    nc.scalar.copy(v_tok[:, g % 2, :], ps[:, 7, :])
                    nc.scalar.copy(v_meta[:, g % 2, :], ps[0:META, 4, 0:P]).then_inc(vt_ev, 1)
                    if g < MH:
                        act.wait_ge(bc_done, g + 1)
                        act.wait_ge(g_ready, 1)
                        if g >= 1:
                            act.wait_ge(p_done, g)
                            act.wait_ge(x_ready, g)
                        for j in range(TT):
                            nc.scalar.activation(decay[:, S_AT[j]:S_AT[j + 1]], ps[:, 5, P * j:SEQ], ACT.Exp,
                                                 bias=u_col[:, j, g:g + 1], scale=-1.0)
                        nc.scalar.activation(decay[0:META, S_AT[TT]:S_WIDTH], ps[0:META, 5, :], ACT.Exp,
                                             bias=u_col[0:META, TT, g:g + 1], scale=-1.0)
                        nc.scalar.activation(floor[:, :], ps[:, 6, :], ACT.Exp, scale=-1.0).then_inc(d_done, 1)
                    if g >= 1:
                        act.wait_ge(y_ready, g)
                        nc.scalar.copy(y_h[:, g - 1, :], hy[:, :]).then_inc(y_hi, 1)
                if h < NH:
                    act.wait_ge(w_used, 4 * h + 1)
                    if is_m:
                        if h >= 2:
                            act.wait_ge(s_done, h - 1)
                        nc.scalar.copy(qT[:, pair, :], ps[:, 0, :]).then_inc(pj_ev, 1)
                    else:
                        if h > MH:
                            act.wait_ge(rope_done, h - MH)
                        nc.scalar.copy(q_raw[:, :], ps[:, 0, :]).then_inc(pj_ev, 1)
                    high(4 * h + 1 + LEAD)
                    act.wait_ge(w_used, 4 * h + 2)
                    dst = kT[:, pair, :] if is_m else k_raw[:, :]
                    nc.scalar.copy(dst[:, 0:SEQ], ps[:, 1, :])
                    nc.scalar.copy(dst[:, SEQ:TOK], ps[:, 2, 0:META]).then_inc(pj_ev, 1)
                if h >= 1:
                    g = h - 1
                    act.wait_ge(pv_done, g + 1)
                    if g < MH:
                        nc.scalar.activation(hden[:, :], ps[:, 3, :], ACT.Abs).then_inc(den_abs, 1)
                    else:
                        nc.scalar.copy(hx[:, :], ps[:, 7, :]).then_inc(x_ready, 1)
                if h < NH:
                    high(4 * h + 2 + LEAD)
                    act.wait_ge(w_used, 4 * h + 3)
                    nc.scalar.copy(vT[:, 0:SEQ], ps[:, 0, :])
                    nc.scalar.copy(vT[:, SEQ:TOK], ps[:, 2, META:2 * META]).then_inc(pj_ev, 1)
                if h >= 1:
                    act.wait_ge(xc_ready, h)
                    nc.scalar.activation(hsq[:, :], hxc[:, :], ACT.Square).then_inc(sq_ready, 1)
                if h < NH:
                    high(4 * h + 3 + LEAD)
                    act.wait_ge(w_used, 4 * h + 4)
                    if h >= 2:
                        act.wait_ge(y_ready, h - 1)
                    if is_m:
                        nc.scalar.activation(og[:, pair, :], ps[:, 1, :], ACT.Exp, scale=-1.0).then_inc(pj_ev, 1)
                    else:
                        nc.scalar.copy(og[:, pair, :], ps[:, 1, :]).then_inc(pj_ev, 1)
                        act.wait_ge(pj_ev, 4 * h + 4)
                        nc.scalar.activation(eg[:, :], og[:, pair, :], ACT.Exp, scale=-1.0).then_inc(o_exp, 1)
                if h >= 1:
                    act.wait_ge(var_done, h)
                    link(nc.scalar.activation(hsq[:, :], ps[:, 3, :], ACT.Ln, bias=EPS))
                    nc.scalar.activation(hsq[:, :], hsq[:, :], ACT.Exp, scale=-0.5).then_inc(rstd_done, 1)
            act.wait_ge(y_ready, NH)
            nc.scalar.copy(y_h[:, NH - 1, :], hy[:, :]).then_inc(y_hi, 1)
            for j in range(KD):
                high(B_OUT + j + LEAD)

            for n in range(TT + 1, 2 * TT + 1):
                act.wait_ge(mix_added, n - TT)
                inv_rms(acc[:, n - TT - 1, :], n, junk[:, :], nt_r)
                if n >= TT + 3:
                    high_xt(n - 2)
            high_xt(2 * TT - 1)
            high_xt(2 * TT)

            def query(i, first=False):
                for p in range(2):
                    act.wait_ge(w_used, i * 2 + (B_QUERY + p + 1))
                    if not first:
                        act.wait_ge(sc_done, i * 2 + (p - 1))
                    nc.scalar.copy(qx[:, p, :], ps[:, p, :]).then_inc(qx_ready, 1)
                for p in range(2):
                    act.wait_ge(sc_done, i * 2 + (p + 1))
                    if not first:
                        act.wait_ge(sc_used, i * 2 + (p - 1))
                    nc.scalar.copy(sc[:, p, :, :], ps[:, 2 + p, :].rearrange("p (t n) -> p t n", t=TT)).then_inc(sc_ev, 1)

            for i in range(2):
                high(B_QUERY + 2 * i + LEAD)
                high(B_QUERY + 2 * i + 1 + LEAD)
                query(i, first=i == 0)
            with act.Fori(1, PH // 2) as i2:
                for half in range(2):
                    for p in range(2):
                        split_high(i2 + (B_QUERY // RING + half), (2 * half + p + LEAD) % RING)
                    query(i2 * 2 + half)

            def gelu(q, u, first=False):
                act.wait_ge(w_used, q * RING + (B_DOWN + u + 1))
                if not first:
                    act.wait_ge(a_stored[u % 2], q * 32 + 16 * (u // 2))
                nc.scalar.activation(a_out[:, u % 2, :], ps[:, u % 2, :], ACT.Gelu).then_inc(a_ready, 1)

            def down_tile(q, u, first=False):
                split_high(q + (B_DOWN // RING + (u + LEAD) // RING), (u + LEAD) % RING)
                gelu(q, u, first)

            for u in range(RING):
                down_tile(0, u, first=u < 2)
            with act.Fori(0, TT) as r:
                with act.Fori(0, PLAIN // RING - 1) as i:
                    for u in range(RING):
                        down_tile(r * ((PLAIN + BUILD) // RING) + i + PRE // RING, u)
                act.wait_ge(dist_ready, r + 1)
                nc.scalar.activation(expd[:, :, :], dist[:, :, :], ACT.Exp).then_inc(exp_ready, 1)
                for u in range(RING):
                    down_tile(r * ((PLAIN + BUILD) // RING) + (PLAIN + PRE) // RING - 1, u)
                act.wait_ge(chunk_free, r * (16 * PIECES) + 1)
                for i in range(BUILD // RING):
                    for u in range(RING):
                        down_tile(r * ((PLAIN + BUILD) // RING) + (PLAIN + PRE) // RING + i, u)
                        for k in range(PER_TILE):
                            n = (i * RING + u) * PER_TILE + k
                            act.wait_ge(gm_done, r * (P // BATCH) + (n + 1))
                            nc.scalar.activation(gchunk[:, :, n * BATCH:(n + 1) * BATCH].rearrange("p j t -> p t j"),
                                                 ps[:, 2 + n % 2, :].rearrange("p (t j) -> p t j", t=BATCH),
                                                 ACT.Copy, scale=1.0 / GSCALE).then_inc(g_ev, 1)
            with act.Fori(0, POST // RING - 1) as i:
                for u in range(RING):
                    down_tile(i + (P - POST) // RING, u)

            def high_ga(q, u, first=False):
                act.wait_ge(ga_done, q * RING + (u + 1))
                if not first:
                    act.wait_ge(w_used, q * RING + (B_UP + u - RING + 1))
                nc.scalar.copy(y_h[:, u, :], ga[:, u % 2, :]).then_inc(ga_hi, 1)

            for u in range(RING):
                down_tile(P // RING - 1, u)
                if u >= LEAD:
                    high_ga(0, u - LEAD, first=True)

            def up_tile(q, u):
                split_high(q + (B_UP // RING + (u + LEAD) // RING), (u + LEAD) % RING)
                high_ga(q + (u + LEAD) // RING, (u + LEAD) % RING, first=isinstance(q, int) and q == 0 and u < LEAD)

            for u in range(RING):
                up_tile(0, u)
            with act.Fori(1, P // RING - 1) as q:
                for u in range(RING):
                    up_tile(q, u)
            for u in range(RING - LEAD):
                up_tile(P // RING - 1, u)

            nc.scalar.preload_act_table_set("natural_log_exp_and_others")
            for t in range(TT):
                act.wait_ge(res_added, t + 1)
                inv_rms(acc[:, t, :], 2 * TT + 1 + t, junk2[:, :], f_r)

        @block.vector
        def _(dve):
            own = [0]

            def link(ins):
                own[0] += 1
                ins.then_inc(dve_own, 1)
                dve.wait_ge(dve_own, own[0])

            def scale_rows(n):
                src = acc[:, n, :] if n < TT else (mt[:, :] if n == TT else acc[:, n - TT - 1, :])
                rows = META if n == TT else P
                dve.wait_ge(nt_r, n + 1)
                if n >= 2:
                    dve.wait_ge(nt_tr, n - 1)
                nc.vector.tensor_scalar(xn[0:rows, n % 2, :], src, rstd[0:rows, n:n + 1], None, ALU.mult).then_inc(nt_xn, 1)

            def apply_gain(n):
                width = META if n == TT else P
                g0 = 0 if n <= TT else KD
                dve.wait_ge(nt_tr, n + 1)
                if n >= 2:
                    dve.wait_ge(nt_lo, n - 1)
                src = ps[:, 2 * (n % 2):2 * (n % 2) + 2, :].rearrange("p b (k c) -> p (b k) c", c=P)
                nc.vector.tensor_tensor(ntmp[:, n % 2, :, 0:width], src[:, :, 0:width],
                                        gain[:, g0:g0 + KD].unsqueeze(2).broadcast_to([P, KD, width]),
                                        ALU.mult).then_inc(nt_f, 1)

            def low_xt(n):
                t = n if n <= TT else n - TT - 1
                cols = slice(t * P, t * P + P) if n != TT else slice(SEQ, TOK)
                width = P if n != TT else META
                dve.wait_ge(nt_hi, n + 1)
                nc.vector.tensor_tensor(xt_l[:, :, cols], ntmp[:, n % 2, :, 0:width], xt_h[:, :, cols].bitcast(F32),
                                        ALU.subtract).then_inc(nt_lo, 1)

            dve.wait_ge(c_loaded, 64)
            for n in range(TT + 1):
                scale_rows(n)
                if n == TT:
                    dve.wait_ge(wg_split_h, 1)
                    nc.vector.tensor_tensor(wg_l[:, :], wg[:, :], wg_h[:, :].bitcast(F32), ALU.subtract).then_inc(wg_split, 1)
                if n >= 1:
                    apply_gain(n - 1)
                if n >= 2:
                    low_xt(n - 2)
            apply_gain(TT)
            low_xt(TT - 1)
            low_xt(TT)

            dve.wait_ge(t_loaded, 32)
            gi, gf, gl = (probs[0:MH, k * TOK:(k + 1) * TOK] for k in range(3))
            gs, gu, g1 = (decay[0:MH, k * TOK:(k + 1) * TOK] for k in range(3))
            dve.wait_ge(g_mm, 1)
            link(nc.vector.tensor_scalar(gi[:, META:TOK], ps[0:MH, 4, :], gb[:, 0:1], None, ALU.add))
            link(nc.vector.tensor_scalar(gf[:, META:TOK], ps[0:MH, 5, :], gb[:, 1:2], None, ALU.add))
            link(nc.vector.tensor_scalar(gi[:, 0:META], ps[0:MH, 6, 0:META], gb[:, 0:1], None, ALU.add))
            link(nc.vector.tensor_scalar(gf[:, 0:META], ps[0:MH, 7, 0:META], gb[:, 1:2], None, ALU.add))
            nc.vector.scalar_tensor_tensor(hx[0:MH, :], gf[:, META:TOK], -1.0, gf[:, META:TOK], ALU.mult, ALU.min).then_inc(g_an, 1)
            nc.vector.scalar_tensor_tensor(rot[0:MH, 0:META], gf[:, 0:META], -1.0, gf[:, 0:META], ALU.mult, ALU.min).then_inc(g_an, 1)
            link(nc.vector.memset(g1, 1.0))
            dve.wait_ge(g_ln, 1)
            link(nc.vector.scalar_tensor_tensor(gl[:, META:TOK], gf[:, META:TOK], 0.0, hxc[0:MH, :], ALU.min, ALU.subtract))
            link(nc.vector.scalar_tensor_tensor(gl[:, 0:META], gf[:, 0:META], 0.0, rot[0:MH, 0:META], ALU.min, ALU.subtract))
            link(nc.vector.tensor_tensor_scan(gs, g1, gl, 0.0, ALU.mult, ALU.add))
            link(nc.vector.tensor_tensor(gu, gi, gs, ALU.subtract))
            link(nc.vector.tensor_tensor_scan(gm[:, 0, :], g1, gu, 0.0, ALU.mult, ALU.max))
            nc.vector.tensor_tensor(gm[:, 1, :], gm[:, 0, :], gs, ALU.add).then_inc(g_u, 1)
            dve.wait_ge(g_ut, 1)
            nc.vector.tensor_copy(u_col[:, 0:TT, :], ps[:, 4, 0:TT * MH].rearrange("p (t h) -> p t h", h=MH))
            nc.vector.tensor_copy(u_col[0:META, TT, :], ps[0:META, 4, TT * MH:(TT + 1) * MH]).then_inc(g_ready, 1)

            for h in range(NH + 1):
                if h >= 1:
                    g = h - 1
                    gp = g % 2
                    if g >= MH:
                        dve.wait_ge(sw_done, g - MH + 1)
                        if g >= 2:
                            dve.wait_ge(s_done, g - 1)
                        cos, sin = table_cols(T_COS, TOK), table_cols(T_SIN, TOK)
                        link(nc.vector.tensor_tensor(rot[:, 0:SEQ], ps[:, 5, :], sin[:, 0:SEQ], ALU.mult))
                        link(nc.vector.tensor_tensor(qT[:, gp, :], q_raw[:, :], cos[:, 0:SEQ], ALU.mult))
                        link(nc.vector.tensor_tensor(qT[:, gp, :], qT[:, gp, :], rot[:, 0:SEQ], ALU.add))
                        nc.vector.tensor_tensor(rot[:, 0:SEQ], ps[:, 6, :], sin[:, 0:SEQ], ALU.mult)
                        link(nc.vector.tensor_tensor(rot[:, SEQ:TOK], ps[:, 2, 32:32 + META], sin[:, SEQ:TOK], ALU.mult))
                        link(nc.vector.tensor_tensor(kT[:, gp, :], k_raw[:, :], cos, ALU.mult))
                        nc.vector.tensor_tensor(kT[:, gp, :], kT[:, gp, :], rot[:, :], ALU.add).then_inc(rope_done, 1)
                    if g >= MH:
                        dve.wait_ge(o_exp, g - MH + 1)
                        link(nc.vector.tensor_scalar(eg[:, :], eg[:, :], 1.0, None, ALU.add))
                        link(nc.vector.reciprocal(eg[:, :], eg[:, :]))
                        link(nc.vector.tensor_tensor(og[:, gp, :], og[:, gp, :], eg[:, :], ALU.mult))
                    if g >= 1:
                        dve.wait_ge(y_hi, g)
                        nc.vector.tensor_tensor(y_l[:, g - 1, :], hy[:, :], y_h[:, g - 1, :].bitcast(F32), ALU.subtract).then_inc(y_lo, 1)
                    dve.wait_ge(s_done, g + 1)
                    if g < MH:
                        dve.wait_ge(masked, g + 1)
                    if g >= 1:
                        dve.wait_ge(pv_done, g)
                    where = [(3, 0), (4, 0), (6, 0), (4, COLS[1])]
                    for j in range(TT):
                        bank, at = where[j]
                        w = COLS[j]
                        dec = decay[:, S_AT[j]:S_AT[j + 1]] if g < MH else table_cols(T_DEC + (g - MH) * TOK, w)
                        nc.vector.scalar_tensor_tensor(probs[:, S_AT[j]:S_AT[j + 1]], ps[:, bank, at:at + w], SCALE, dec,
                                                       ALU.mult, ALU.mult)
                    dec = decay[0:META, S_AT[TT]:S_WIDTH] if g < MH else table_cols(T_DEC + (g - MH) * TOK + META, SEQ, META)
                    nc.vector.scalar_tensor_tensor(probs[0:META, S_AT[TT]:S_WIDTH], ps[0:META, 5, :], SCALE, dec,
                                                   ALU.mult, ALU.mult).then_inc(p_done, 1)
                    if g < MH:
                        dve.wait_ge(den_abs, g + 1)
                        link(nc.vector.tensor_tensor(hden[:, :], hden[:, :], floor[:, :], ALU.max))
                        dve.wait_ge(pj_ev, 4 * g + 4)
                        link(nc.vector.scalar_tensor_tensor(hden[:, :], og[:, gp, :], 1.0, hden[:, :], ALU.add, ALU.mult))
                        link(nc.vector.reciprocal(hden[:, :], hden[:, :]))
                        nc.vector.tensor_tensor(hx[:, :], ps[:, 7, :], hden[:, :], ALU.mult).then_inc(x_ready, 1)
                    dve.wait_ge(mean_done, g + 1)
                    nc.vector.tensor_tensor(hxc[:, :], hx[:, :], ps[:, 4, :], ALU.subtract).then_inc(xc_ready, 1)
                    dve.wait_ge(rstd_done, g + 1)
                    head_gain = gain[:, 2 * KD + g:2 * KD + g + 1]
                    if g < MH:
                        nc.vector.scalar_tensor_tensor(hy[:, :], hxc[:, :], head_gain, hsq[:, :], ALU.mult, ALU.mult).then_inc(y_ready, 1)
                    else:
                        link(nc.vector.scalar_tensor_tensor(hxc[:, :], hxc[:, :], head_gain, hsq[:, :], ALU.mult, ALU.mult))
                        nc.vector.tensor_tensor(hy[:, :], hxc[:, :], og[:, gp, :], ALU.mult).then_inc(y_ready, 1)
            dve.wait_ge(y_hi, NH)
            nc.vector.tensor_tensor(y_l[:, NH - 1, :], hy[:, :], y_h[:, NH - 1, :].bitcast(F32), ALU.subtract).then_inc(y_lo, 1)

            dve.wait_ge(w_used, B_QUERY)
            for t in range(TT):
                for half in range(2):
                    dst = acc[:, t, half * 512:(half + 1) * 512]
                    last = nc.vector.tensor_tensor(dst, dst, ps[:, 2 * t + half, :], ALU.add)
                last.then_inc(mix_added, 1)

            for n in range(TT + 1, 2 * TT + 1):
                scale_rows(n)
                if n >= TT + 2:
                    apply_gain(n - 1)
                if n >= TT + 3:
                    low_xt(n - 2)
            apply_gain(2 * TT)
            low_xt(2 * TT - 1)
            low_xt(2 * TT)

            link(nc.vector.memset(fence_cell[:, 0:1], 0.0))

            def fence(semaphore, value, cell=0):
                dve.wait_ge(semaphore, value)
                nc.vector.tensor_copy(fence_cell[:, 1 + cell:2 + cell], fence_cell[:, 0:1])

            class Steps:

                def __init__(self, index, size):
                    self.index, self.size, self.start, self.n = index, size, own[0], 0

                def step(self, ins):
                    self.n += 1
                    ins.then_inc(dve_own, 1)

                def value(self):
                    return self.index * self.size + (self.start + self.n)

                def end(self, times):
                    assert self.n == self.size
                    own[0] += self.size * times

            with dve.Fori(0, PH) as h:
                steps = Steps(h, 8)
                for p in range(2):
                    fence(sc_ev, h * 2 + (p + 1), 1 + p)
                    for t in range(TT):
                        last = nc.vector.max(t8v[:, t, p, 0:8], sc[:, p, t, :])
                    steps.step(last)
                    fence(dve_own, steps.value())
                    for t in range(TT):
                        nc.vector.max_index(t8i[:, t, p, 0:8], t8v[:, t, p, 0:8], sc[:, p, t, :])
                    for t in range(TT):
                        last = nc.vector.match_replace(sc_rest[:, p, t, :], t8v[:, t, p, 0:8], sc[:, p, t, :], -3.0e38)
                    steps.step(last)
                    fence(dve_own, steps.value())
                    for t in range(TT):
                        last = nc.vector.max(t8v[:, t, p, 8:16], sc_rest[:, p, t, :])
                    steps.step(last)
                    fence(dve_own, steps.value())
                    for t in range(TT):
                        last = nc.vector.max_index(t8i[:, t, p, 8:16], t8v[:, t, p, 8:16], sc_rest[:, p, t, :])
                    last.then_inc(sc_used, 1)
                fence(sc_used, h * 2 + 2)
                steps.step(nc.vector.tensor_copy(topv[:, :, :, bass.ds(h, 1), :].rearrange("p t s o k -> p t s (o k)"), t8v[:, :, :, :]))
                steps.step(nc.vector.tensor_copy(topi[:, :, :, bass.ds(h, 1), :].rearrange("p t s o k -> p t s (o k)"), t8i[:, :, :, :]))
                fence(dve_own, steps.value())
            steps.end(PH)
            link(nc.vector.tensor_copy(fence_cell[:, 4:5], fence_cell[:, 0:1]))
            nc.vector.tensor_copy(fence_cell[:, 4:5], fence_cell[:, 0:1]).then_inc(chunk_free, 1)
            dve.wait_ge(iota_ready, 1)

            with dve.Fori(0, TT) as r:
                steps = Steps(r, 19)
                step = steps.step

                def behind():
                    dve.wait_ge(dve_own, steps.value())

                def of_tile(tops, s):
                    return tops[:, bass.ds(r, 1), s, :, :].rearrange("p o h k -> p (o h) k")

                cand4 = cand[:, :, :].rearrange("p h (a b) -> p h a b", b=TOPK)
                step(nc.vector.tensor_tensor(cand4, of_tile(topv, 0).unsqueeze(3).broadcast_to([P, PH, TOPK, TOPK]),
                                             of_tile(topv, 1).unsqueeze(2).broadcast_to([P, PH, TOPK, TOPK]), ALU.add))
                fence(dve_own, steps.value())
                for h in range(PH):
                    last = nc.vector.max(tv[:, h, 0:8], cand[:, h, :])
                step(last)
                fence(dve_own, steps.value())
                for h in range(PH):
                    last = nc.vector.max_index(ti[:, h * TOPK:h * TOPK + 8], tv[:, h, 0:8], cand[:, h, :])
                step(last)
                fence(dve_own, steps.value())
                for h in range(PH):
                    last = nc.vector.match_replace(cand[:, h, :], tv[:, h, 0:8], cand[:, h, :], -3.0e38)
                step(last)
                fence(dve_own, steps.value())
                for h in range(PH):
                    last = nc.vector.max(tv[:, h, 8:16], cand[:, h, :])
                step(last)
                fence(dve_own, steps.value())
                nc.vector.tensor_tensor(dist[:, :, :], tv[:, :, :], tv[:, :, 0:1].broadcast_to([P, PH, TOPK]),
                                        ALU.subtract).then_inc(dist_ready, 1)
                for h in range(PH):
                    last = nc.vector.max_index(ti[:, h * TOPK + 8:(h + 1) * TOPK], tv[:, h, 8:16], cand[:, h, :])
                step(last)
                behind()
                nc.vector.tensor_scalar(tj[:, 0, :], ti[:, :], 4, None, ALU.logical_shift_right)
                step(nc.vector.tensor_scalar(tj[:, 1, :], ti[:, :], 15, None, ALU.bitwise_and))
                behind()
                step(nc.vector.tensor_copy(tf[:, :, :], tj[:, :, :]))
                for s in range(2):
                    behind()
                    step(nc.vector.tensor_tensor(eq[:, :, :], tf[:, s, :].unsqueeze(2).broadcast_to([P, P, TOPK]),
                                                 iota16[:, 0:TOPK].unsqueeze(1).broadcast_to([P, P, TOPK]), ALU.is_equal))
                    behind()
                    step(nc.vector.tensor_tensor(pick[:, :, :, :], eq[:, :, :].rearrange("p (h k) a -> p h k a", h=PH),
                                                 of_tile(topi, s).unsqueeze(2).broadcast_to([P, PH, TOPK, TOPK]), ALU.mult))
                    behind()
                    step(nc.vector.tensor_reduce(route[:, s, :], pick[:, :, :, :].rearrange("p h k a -> p (h k) a"), AX.X, ALU.add))
                dve.wait_ge(exp_ready, r + 1)
                step(nc.vector.tensor_reduce(den8[:, 0, :], expd[:, :, :], AX.X, ALU.add))
                behind()
                step(nc.vector.reciprocal(den8[:, 1, :], den8[:, 0, :]))
                behind()
                nc.vector.scalar_tensor_tensor(route[:, 2, :].rearrange("p (h k) -> p h k", h=PH), expd[:, :, :], GSCALE,
                                               den8[:, 1, :].unsqueeze(2).broadcast_to([P, PH, TOPK]), ALU.mult, ALU.mult).then_inc(route_ready, 1)
                dve.wait_ge(route_tr, r + 1)
                nc.vector.tensor_copy(route_t[:, :, :], ps[:, 4, 0:3 * P].rearrange("p (i t) -> p i t", i=3))
                step(nc.vector.tensor_copy(gh16[:, :], ps[:, 4, 2 * P:3 * P]))
                behind()
                step(nc.vector.tensor_copy(gate_h[:, :], gh16[:, :]))
                behind()
                step(nc.vector.tensor_tensor(gate_l[:, :], route_t[:, 2, :], gate_h[:, :], ALU.subtract))
                behind()
                for n in range(P // BATCH):
                    slot = n % 2
                    if n >= 2:
                        dve.wait_ge(gm_done, r * (P // BATCH) + (n - 1))
                    for c in range(BATCH):
                        t = n * BATCH + c
                        nc.vector.tensor_scalar(onehot[:, slot, 0, c, :], iota16[:, :], route_t[:, 0, t:t + 1], None, ALU.is_equal)
                        nc.vector.tensor_scalar(onehot[:, slot, 1, c, :], iota16[:, :], route_t[:, 1, t:t + 1], gate_h[:, t:t + 1],
                                                ALU.is_equal, ALU.mult)
                        last = nc.vector.tensor_scalar(onehot[:, slot, 2, c, :], iota16[:, :], route_t[:, 1, t:t + 1], gate_l[:, t:t + 1],
                                                       ALU.is_equal, ALU.mult)
                    last.then_inc(oh_ready, 1)
            steps.end(TT)

            def weigh(q, u, first=False):
                dve.wait_ge(ag_loaded[u], q * 32 + 32)
                if not first:
                    dve.wait_ge(ga_lo, q * RING + (u - 1))
                nc.vector.tensor_tensor(ga[:, u % 2, :], a_in[:, u, :], g_in[:, u, :], ALU.mult).then_inc(ga_done, 1)
                dve.wait_ge(ga_hi, q * RING + (u + 1))
                nc.vector.tensor_tensor(y_l[:, u, :], ga[:, u % 2, :], y_h[:, u, :].bitcast(F32), ALU.subtract).then_inc(ga_lo, 1)

            for u in range(RING):
                weigh(0, u, first=u < 2)
            with dve.Fori(1, P // RING) as q:
                for u in range(RING):
                    weigh(q, u)

            dve.wait_ge(w_used, B_END)
            for t in range(TT):
                for half in range(2):
                    dst = acc[:, t, half * 512:(half + 1) * 512]
                    last = nc.vector.tensor_tensor(dst, dst, ps[:, 2 * t + half, :], ALU.add)
                last.then_inc(res_added, 1)
            dve.wait_ge(f_loaded, 16)
            for t in range(TT):
                n = 2 * TT + 1 + t
                dve.wait_ge(f_r, t + 1)
                nc.vector.scalar_tensor_tensor(acc[:, t, :], acc[:, t, :], rstd[:, n:n + 1], fgain[:, :], ALU.mult, ALU.mult).then_inc(f_done, 1)

        @block.tensor
        def _(pe):
            def three(out_ap, stat, mov, first=True, last=True):
                for i, (s_, m_) in enumerate(((stat[0], mov[0]), (stat[0], mov[1]), (stat[1], mov[0]))):
                    ins = nc.tensor.matmul(out_ap, s_, m_, start=first and i == 0, stop=last and i == 2)
                return ins

            def project(u, bank, width=SEQ, cols=slice(0, SEQ), at=0):
                for k in range(KD):
                    ws = (w_h[:, u, k * P:(k + 1) * P], w_l[:, u, k * P:(k + 1) * P])
                    ins = three(ps[:, bank, at:at + width], ws, (xt_h[:, k, cols], xt_l[:, k, cols]), k == 0, k == KD - 1)
                return ins

            def norm_tile(n):
                rows = META if n == TT else P
                pe.wait_ge(nt_xn, n + 1)
                if n >= 2:
                    pe.wait_ge(nt_f, n - 1)
                for k in range(KD):
                    bank = 2 * (n % 2) + k // 4
                    at = (k % 4) * P
                    ins = nc.tensor.transpose(ps[:, bank, at:at + rows], xn[0:rows, n % 2, k * P:(k + 1) * P], ident[0:rows, 0:rows])
                ins.then_inc(nt_tr, 1)

            pe.wait_ge(c_loaded, 64)
            for n in range(TT + 1):
                norm_tile(n)

            pe.wait_ge(t_loaded, 32)
            pe.wait_ge(nt_lo, TT + 1)
            pe.wait_ge(wg_split, 1)
            for bank, g0, cols in ((4, 0, slice(0, SEQ)), (5, MH, slice(0, SEQ)), (6, 0, slice(SEQ, TOK)), (7, MH, slice(SEQ, TOK))):
                for k in range(KD):
                    at = k * 2 * MH + g0
                    ins = three(ps[0:MH, bank, 0:cols.stop - cols.start], (wg_h[:, at:at + MH], wg_l[:, at:at + MH]),
                                (xt_h[:, k, cols], xt_l[:, k, cols]), k == 0, k == KD - 1)
            ins.then_inc(g_mm, 1)

            for h in range(NH + 1):
                is_m = h < MH
                g, gp = h - 1, (h - 1) % 2
                hp = h % 2

                def block_of(s):
                    b = 4 * h + s
                    pe.wait_ge(w_lo, b + 1)
                    if b >= 2:
                        pe.wait_ge(pj_ev, b - 1)
                    return b

                if h < NH:
                    b = block_of(0)
                    project(b % RING, 0).then_inc(w_used, 1)
                if h == 0:
                    pe.wait_ge(g_u, 1)
                    for j in range(TT):
                        nc.tensor.transpose(ps[:, 4, j * MH:(j + 1) * MH], decay[0:MH, TOK + META + j * P:TOK + META + (j + 1) * P], ident[0:MH, 0:MH])
                    nc.tensor.transpose(ps[0:META, 4, TT * MH:(TT + 1) * MH], decay[0:MH, TOK:TOK + META], ident[0:MH, 0:MH]).then_inc(g_ut, 1)
                if h >= 1:
                    pe.wait_ge(vt_ev, g + 1)
                    if g >= 1:
                        pe.wait_ge(rstd_done, g)
                    if g < MH:
                        pe.wait_ge(d_done, g + 1)
                    else:
                        pe.wait_ge(rope_done, g - MH + 1)
                    for j, (bank, at) in enumerate(((3, 0), (4, 0), (6, 0), (4, COLS[1]))):
                        nc.tensor.matmul(ps[:, bank, at:at + COLS[j]], kT[:, gp, j * P:(j + 1) * P], qT[:, gp, j * P:SEQ], start=True, stop=True)
                    nc.tensor.matmul(ps[0:META, 5, :], kT[:, gp, SEQ:TOK], qT[:, gp, :], start=True, stop=True).then_inc(s_done, 1)
                if h < NH:
                    b = block_of(1)
                    project(b % RING, 1)
                    if h > MH:
                        pe.wait_ge(rope_done, h - MH)
                    project(b % RING, 2, META, slice(SEQ, TOK), 0).then_inc(w_used, 1)
                if h >= 1:
                    pe.wait_ge(p_done, g + 1)

                    def over_keys(bank, meta_stat, stats):
                        ins = nc.tensor.matmul(ps[:, bank, :], meta_stat, probs[0:META, S_AT[TT]:S_WIDTH], start=True, stop=False)
                        for j in range(TT):
                            ins = nc.tensor.matmul(ps[:, bank, j * P:SEQ], stats[j], probs[:, S_AT[j]:S_AT[j + 1]],
                                                   start=False, stop=j == TT - 1)
                        return ins

                    if g < MH:
                        over_keys(3, table_cols(T_ONE, P, META), [table_cols(T_ONE, P)] * TT)
                    over_keys(7, v_meta[:, gp, :], [v_tok[:, gp, j * P:(j + 1) * P] for j in range(TT)]).then_inc(pv_done, 1)
                if h < NH:
                    b = block_of(2)
                    project(b % RING, 0)
                    pe.wait_ge(pj_ev, 4 * h + 2)
                    project(b % RING, 2, META, slice(SEQ, TOK), META).then_inc(w_used, 1)
                if h >= 1:
                    pe.wait_ge(x_ready, g + 1)
                    nc.tensor.matmul(ps[:, 4, :], table_cols(T_MEAN, P), hx[:, :], start=True, stop=True).then_inc(mean_done, 1)
                if h < NH:
                    b = block_of(3)
                    project(b % RING, 1).then_inc(w_used, 1)
                if h >= 1:
                    pe.wait_ge(sq_ready, g + 1)
                    nc.tensor.matmul(ps[:, 3, :], table_cols(T_MEAN, P), hsq[:, :], start=True, stop=True).then_inc(var_done, 1)
                if h < NH:
                    if is_m:
                        if h == 0:
                            pe.wait_ge(g_u, 1)
                        for bank, row in ((5, 0), (6, 1)):
                            ins = nc.tensor.matmul(ps[:, bank, :], table[0:MH, T_SEL + h * P:T_SEL + (h + 1) * P], gm[:, row, META:TOK],
                                                   start=True, stop=True)
                        ins.then_inc(bc_done, 1)
                    else:
                        pe.wait_ge(pj_ev, 4 * h + 3)
                        swap = table_cols(T_SWAP, P)
                        nc.tensor.matmul(ps[:, 5, :], swap, q_raw[:, :], start=True, stop=True)
                        nc.tensor.matmul(ps[:, 6, :], swap, k_raw[:, 0:SEQ], start=True, stop=True)
                        nc.tensor.matmul(ps[:, 2, 32:32 + META], swap, k_raw[:, SEQ:TOK], start=True, stop=True).then_inc(sw_done, 1)
                    pe.wait_ge(pj_ev, 4 * h + 3)
                    if h == 0:
                        pe.wait_ge(g_ready, 1)
                    for j in range(TT):
                        nc.tensor.transpose(ps[:, 7, j * P:(j + 1) * P], vT[:, j * P:(j + 1) * P], ident[:, :])
                    nc.tensor.transpose(ps[0:META, 4, 0:P], vT[:, SEQ:TOK], ident[:, :]).then_inc(vt_done, 1)

            def add_rows(u, slot, first, last, order=range(TT), before={}):
                for t in order:
                    if t in before:
                        before[t]()
                    cols = slice(t * P, (t + 1) * P)
                    for i, (y_, w_) in enumerate(((y_h, w_h), (y_h, w_l), (y_l, w_h))):
                        for half in range(2):
                            ins = nc.tensor.matmul(ps[:, 2 * t + half, :], y_[:, slot, cols], w_[:, u, half * 512:(half + 1) * 512],
                                                   start=first and i == 0, stop=last and i == 2)
                return ins

            pe.wait_ge(y_lo, NH)
            for j in range(KD):
                pe.wait_ge(w_lo, B_OUT + j + 1)
                add_rows(j % RING, j, j == 0, j == KD - 1).then_inc(w_used, 1)

            pe.wait_ge(mix_added, TT)
            for n in range(TT + 1, 2 * TT + 1):
                norm_tile(n)
            pe.wait_ge(nt_lo, 2 * TT + 1)

            def query(i, u0, first=False):
                for p in range(2):
                    pe.wait_ge(w_lo, i * 2 + (B_QUERY + p + 1))
                    if not first:
                        pe.wait_ge(qx_ready, i * 2 + (p - 1))
                    project(u0 + p, p).then_inc(w_used, 1)
                for p in range(2):
                    pe.wait_ge(qx_ready, i * 2 + (p + 1))
                    if not first:
                        pe.wait_ge(sc_ev, i * 2 + (p - 1))
                    for t in range(TT):
                        ins = nc.tensor.matmul(ps[:, 2 + p, t * P:(t + 1) * P], qx[:, p, t * P:(t + 1) * P], keys_t[:, p, :],
                                               start=True, stop=True)
                    ins.then_inc(sc_done, 1)

            query(0, 0, first=True)
            query(1, 2)
            with pe.Fori(1, PH // 2) as i2:
                for half in range(2):
                    query(i2 * 2 + half, 2 * half)

            def down_tile(q, u, first=False, between={}):
                pe.wait_ge(w_lo, q * RING + (B_DOWN + u + 1))
                if not first:
                    pe.wait_ge(a_ready, q * RING + (u - 1))
                for k in range(KD):
                    ws = (w_h[:, u, k * P:(k + 1) * P], w_l[:, u, k * P:(k + 1) * P])
                    ins = three(ps[:, u % 2, :], ws, (xt_h[:, k, 0:SEQ], xt_l[:, k, 0:SEQ]), k == 0, k == KD - 1)
                    if k in between:
                        between[k]()
                ins.then_inc(w_used, 1)

            for u in range(RING):
                down_tile(0, u, first=u < 2)
            with pe.Fori(0, TT) as r:
                with pe.Fori(0, PLAIN // RING) as i:
                    for u in range(RING):
                        down_tile(r * ((PLAIN + BUILD) // RING) + i + PRE // RING, u)
                pe.wait_ge(route_ready, r + 1)
                for i in range(3):
                    ins = nc.tensor.transpose(ps[:, 4, i * P:(i + 1) * P], route[:, i, :], ident[:, :])
                ins.then_inc(route_tr, 1)
                def gate_batch(n):
                    pe.wait_ge(oh_ready, r * (P // BATCH) + (n + 1))
                    if n >= 2:
                        pe.wait_ge(g_ev, r * (P // BATCH) + (n - 1))
                    for c in range(BATCH):
                        for part in (1, 2):
                            ins = nc.tensor.matmul(ps[:, 2 + n % 2, c * P:(c + 1) * P], onehot[:, n % 2, 0, c, :],
                                                   onehot[:, n % 2, part, c, :], start=part == 1, stop=part == 2)
                    ins.then_inc(gm_done, 1)

                for i in range(BUILD // RING):
                    for u in range(RING):
                        n0 = (i * RING + u) * PER_TILE
                        step = KD // PER_TILE
                        between = {step * (k + 1) - 2: (lambda n=n0 + k: gate_batch(n)) for k in range(PER_TILE)}
                        down_tile(r * ((PLAIN + BUILD) // RING) + (PLAIN + PRE) // RING + i, u, between=between)
            with pe.Fori(0, POST // RING) as i:
                for u in range(RING):
                    down_tile(i + (P - POST) // RING, u)

            pe.wait_ge(g_ev, TT * P // BATCH)

            def up_tile(q, u, first=False, last=False):
                pe.wait_ge(w_lo, q * RING + (B_UP + u + 1))
                pe.wait_ge(ga_lo, q * RING + (u + 1))
                if first:
                    add_rows(u, u, first, last, order=(1, 2, 3, 0),
                             before={0: lambda: pe.wait_ge(a_ready, P)}).then_inc(w_used, 1)
                else:
                    add_rows(u, u, first, last).then_inc(w_used, 1)

            for u in range(RING):
                up_tile(0, u, first=u == 0)
            with pe.Fori(1, P // RING - 1) as q:
                for u in range(RING):
                    up_tile(q, u)
            for u in range(RING):
                up_tile(P // RING - 1, u, last=u == RING - 1)


def _tables():
    import numpy as np
    tab = np.zeros((P, T_END), np.float32)
    pos = np.concatenate([np.arange(META, META + SEQ), np.arange(META)]).astype(np.float32)
    half = P // 2
    inv = (np.float32(10000.0) ** (-np.arange(half, dtype=np.float32) / np.float32(half))).astype(np.float32)
    ang = (pos[None, :] * inv[:, None]).astype(np.float32)
    cos, sin = np.cos(ang.astype(np.float64)), np.sin(ang.astype(np.float64))
    tab[:, T_COS:T_COS + TOK] = np.concatenate([cos, cos], 0)
    tab[:, T_SIN:T_SIN + TOK] = np.concatenate([-sin, sin], 0)
    gap = np.arange(TOK)[None, :] - np.arange(P)[:, None]
    for h in range(RH):
        lg = math.log1p(-2.0 ** (-5.0 - h))
        tab[:, T_DEC + h * TOK:T_DEC + (h + 1) * TOK] = np.where(gap >= 0, np.exp(lg * np.maximum(gap, 0)), 0.0)
    for m in range(P):
        tab[(m + half) % P, T_SWAP + m] = 1.0
    tab[:, T_ONE:T_ONE + P] = 1.0
    tab[:, T_MEAN:T_MEAN + P] = 1.0 / P
    for h in range(MH):
        tab[h, T_SEL + h * P:T_SEL + (h + 1) * P] = 1.0
    return tab

def kernel(x, meta_tokens, norm1_w, w_in, gate_bias, m_norm_w, r_norm_w, w_out, norm2_w,
           peer_w_query, peer_sub_keys, peer_w_down, peer_w_up, final_norm_w):
    import numpy as np
    import concourse.bacc as bacc
    from concourse.bass_utils import run_bass_kernel_spmd

    def columns(w):
        w = np.asarray(w)
        n = w.shape[1] // P
        return w.reshape(KD, P, n, P).transpose(2, 1, 0, 3).reshape(n, P, D)

    w_in0 = np.asarray(w_in)[0]
    head_cols = [part * MH * P + h * P for h in range(MH) for part in range(4)]
    head_cols += [(4 + part) * RH * P + h * P for h in range(RH) for part in range(4)]
    by_head = np.concatenate([w_in0[:, c:c + P] for c in head_cols], axis=1)
    down = np.asarray(peer_w_down)[0].reshape(P, P, KD, P).transpose(1, 3, 2, 0).reshape(P, P, D)
    up = np.asarray(peer_w_up)[0].reshape(P, P, D).transpose(1, 0, 2)
    arrays = {
        "x": np.asarray(x),
        "meta": np.asarray(meta_tokens),
        "w_blocks": np.concatenate([columns(by_head), np.asarray(w_out)[0].reshape(KD, P, D),
                                    columns(np.asarray(peer_w_query)[0]), down, up], axis=0),
        "w_gates": w_in0[:, 4 * (MH + RH) * P:].reshape(KD, P, 2 * MH).transpose(1, 0, 2).reshape(P, KD * 2 * MH),
        "gate_bias": np.asarray(gate_bias).reshape(2, MH).T,
        "gains": np.concatenate([np.asarray(norm1_w).reshape(KD, P), np.asarray(norm2_w).reshape(KD, P),
                                 np.asarray(m_norm_w).reshape(MH, P), np.asarray(r_norm_w).reshape(RH, P)], axis=0).T,
        "final_gain": np.broadcast_to(np.asarray(final_norm_w)[None], (P, D)),
        "keys": np.asarray(peer_sub_keys)[0].transpose(2, 0, 1),
        "ident": np.eye(P, dtype=np.float32),
        "table": _tables(),
    }
    nc = bacc.Bacc("TRN2", target_bir_lowering=False, num_devices=1)
    args = {}
    for name in arrays:
        arrays[name] = np.ascontiguousarray(arrays[name])
        args[name] = nc.dram_tensor("in_" + name, arrays[name].shape, F32, kind="ExternalInput").ap()
    out = nc.dram_tensor("out_dram", (1, SEQ, D), F32, kind="ExternalOutput").ap()
    mixer_peer_kernel(nc, args["x"], args["meta"], args["w_blocks"], args["w_gates"], args["gate_bias"],
                      args["gains"], args["final_gain"], args["keys"], args["ident"], args["table"], out)
    r = run_bass_kernel_spmd(nc, [{"in_" + n: a for n, a in arrays.items()}], core_ids=[0])
    return r.results[0]["out_dram"]
```

```python
import math
from contextlib import ExitStack

import concourse.bass as bass
from concourse import mybir

F32 = mybir.dt.float32
F32R = mybir.dt.float32r
F16 = mybir.dt.float16
U32 = mybir.dt.uint32
ALU = mybir.AluOpType
ACT = mybir.ActivationFunctionType
AX = mybir.AxisListType

P = 128
D = 1024
KD = D // P
SEQ = 512
META = 16
TOK = SEQ + META
TT = SEQ // P
MH, RH = 4, 4
NH = MH + RH
PH = 8
TOPK = 16
EPS = 1e-6
SCALE = P ** -0.5
GSCALE = 4096.0

B_OUT = 4 * NH
B_OUT2 = B_OUT + 4
B_QUERY = B_OUT + KD
B_DOWN = B_QUERY + 2 * PH
B_UP = B_DOWN + P
B_END = B_UP + P
RING = 4
LEAD = 2

PRE = 4
PLAIN = 12
BUILD = 16
POST = P - PRE - TT * (PLAIN + BUILD)
PIECES = 8
BATCH = 4
PER_TILE = P // BATCH // BUILD

FIRST = 272
REST = TOK - FIRST
F_ROW = 32
G_ROWS = F_ROW + MH

COLS = [SEQ - P * j for j in range(TT)]
S_AT = [sum(COLS[:j]) for j in range(TT + 1)]
S_WIDTH = S_AT[TT] + SEQ

T_COS, T_SIN, T_DEC = 0, TOK, 2 * TOK
T_SWAP = T_DEC + RH * TOK
T_ONE = T_SWAP + P
T_MEAN = T_ONE + P
T_SEL = T_MEAN + P
T_END = T_SEL + MH * P


def mixer_peer_kernel(nc, x, meta, w_blocks, w_gates, gate_bias, gains, final_gain, keys, ident_in, table_in, out):
    a_dram = nc.dram_tensor("act_scratch", (P, P, SEQ), F32, kind="Internal").ap()
    g_dram = nc.dram_tensor("gate_scratch", (P, P, SEQ), F32, kind="Internal").ap()

    ctx = ExitStack()
    with ctx:
        def sb(name, shape, dt=F32, scope=ctx):
            return scope.enter_context(nc.sbuf_tensor(name, shape, dt))

        def sem(name):
            return ctx.enter_context(nc.semaphore(name))

        raw = sb("raw", [P, RING, D])
        w_h = sb("w_h", [P, RING, D], F32R)
        w_l = sb("w_l", [P, RING, D], F32R)
        xt_h = sb("xt_h", [P, KD, TOK], F32R)
        xt_l = sb("xt_l", [P, KD, TOK], F32R)
        acc = sb("acc", [P, TT, D])
        ident = sb("ident", [P, P])
        keys_t = sb("keys_t", [P, 2, P])
        gain = sb("gain", [P, 2 * KD + NH])
        sums = sb("sums", [P, 16])
        rstd = sb("rstd", [P, 16])
        fence_cell = sb("fence_cell", [P, 5])

        with ExitStack() as region:
            xn = sb("xn", [P, 2, D], scope=region)
            ntmp = sb("ntmp", [P, 2, KD, P], scope=region)
            junk = sb("junk", [P, D], scope=region)
            mt = sb("mt", [META, D], scope=region)
        with ExitStack() as region:
            topv = sb("topv", [P, TT, 2, PH, TOPK], scope=region)
            topi = sb("topi", [P, TT, 2, PH, TOPK], scope=region)
            cand = sb("cand", [P, PH, TOPK * TOPK], scope=region)
            tv = sb("tv", [P, PH, TOPK], scope=region)
            ti = sb("ti", [P, PH * TOPK], U32, scope=region)
            tj = sb("tj", [P, 2, PH * TOPK], U32, scope=region)
            tf = sb("tf", [P, 2, PH * TOPK], scope=region)
            dist = sb("dist", [P, PH, TOPK], scope=region)
            expd = sb("expd", [P, PH, TOPK], scope=region)
            den8 = sb("den8", [P, 2, PH], scope=region)
            route = sb("route", [P, 3, PH * TOPK], scope=region)
            eq = sb("eq", [P, PH * TOPK, TOPK], F16, scope=region)
            pick = sb("pick", [P, PH, TOPK, TOPK], F16, scope=region)
            gh16 = sb("gh16", [P, P], F16, scope=region)
            route_t = sb("route_t", [P, 3, P], scope=region)
        y_h = sb("y_h", [P, KD, SEQ], F32R)
        y_l = sb("y_l", [P, KD, SEQ], F32R)

        with ExitStack() as region:
            table = sb("table", [P, T_END], scope=region)
            qT = sb("qT", [P, 2, SEQ], scope=region)
            kT = sb("kT", [P, 2, TOK], scope=region)
            vT = sb("vT", [P, TOK], scope=region)
            v_tok = sb("v_tok", [P, 2, TT * P], scope=region)
            v_meta = sb("v_meta", [META, 2, P], scope=region)
            og = sb("og", [P, 2, SEQ], scope=region)
            eg = sb("eg", [P, SEQ], scope=region)
            decay = sb("decay", [P, S_WIDTH], scope=region)
            probs = sb("probs", [P, S_WIDTH], scope=region)
            floor = sb("floor", [P, SEQ], scope=region)
            hden = sb("hden", [P, SEQ], scope=region)
            hx = sb("hx", [P, SEQ], scope=region)
            hxc = sb("hxc", [P, SEQ], scope=region)
            hsq = sb("hsq", [P, SEQ], scope=region)
            hy = sb("hy", [P, SEQ], scope=region)
            q_raw = sb("q_raw", [P, SEQ], scope=region)
            k_raw = sb("k_raw", [P, TOK], scope=region)
            rot = sb("rot", [P, TOK], scope=region)
            gm = sb("gm", [MH, 2, TOK], scope=region)
            u_col = sb("u_col", [P, TT + 1, MH], scope=region)
            wg = sb("wg", [P, KD * G_ROWS], scope=region)
            wg_h = sb("wg_h", [P, KD * G_ROWS], F32R, scope=region)
            wg_l = sb("wg_l", [P, KD * G_ROWS], F32R, scope=region)
            gb = sb("gb", [G_ROWS, 1], scope=region)
        with ExitStack() as region:
            qx = sb("qx", [P, 2, SEQ], scope=region)
            sc = sb("sc", [P, 2, TT, P], scope=region)
            t8v = sb("t8v", [P, TT, 2, TOPK], scope=region)
            t8i = sb("t8i", [P, TT, 2, TOPK], U32, scope=region)
            sc_rest = sb("sc_rest", [P, 2, TT, P], scope=region)
            xn2 = sb("xn2", [P, 2, D], scope=region)
            ntmp2 = sb("ntmp2", [P, 2, KD, P], scope=region)
            junk_n2 = sb("junk_n2", [P, D], scope=region)
        with ExitStack() as region:
            gchunk = sb("gchunk", [P, P, P], scope=region)
            onehot = sb("onehot", [P, 2, 3, BATCH, P], F16, scope=region)
            a_out = sb("a_out", [P, 2, SEQ], scope=region)
            iota16 = sb("iota16", [P, P], F16, scope=region)
            gate_h = sb("gate_h", [P, P], scope=region)
            gate_l = sb("gate_l", [P, P], scope=region)
        with ExitStack() as region:
            a_in = sb("a_in", [P, RING, SEQ], scope=region)
            g_in = sb("g_in", [P, RING, SEQ], scope=region)
            ga = sb("ga", [P, 2, SEQ], scope=region)
            fgain = sb("fgain", [P, D], scope=region)
            junk2 = sb("junk2", [P, D], scope=region)

        ps = ctx.enter_context(nc.psum_tensor("ps", [P, 8, 512], F32))

        w_loaded = [sem(f"w_loaded{i}") for i in range(RING)]
        w_hi, w_lo, w_used = sem("w_hi"), sem("w_lo"), sem("w_used")
        x_loaded = [sem(f"x_loaded{i}") for i in range(TT + 1)]
        c_loaded = sem("c_loaded")
        t_loaded = sem("t_loaded")
        nt_r, nt_xn, nt_tr, nt_f, nt_hi, nt_lo = (sem(n) for n in ("nt_r", "nt_xn", "nt_tr", "nt_f", "nt_hi", "nt_lo"))
        act_own, dve_own = sem("act_own"), sem("dve_own")
        wg_split_h, wg_split = sem("wg_split_h"), sem("wg_split")
        g_mm, g_an, g_ln, g_u, g_ut, g_ready = (sem(n) for n in ("g_mm", "g_an", "g_ln", "g_u", "g_ut", "g_ready"))
        pj_ev, s_done, p_done, pv_done, den_abs = (sem(n) for n in ("pj_ev", "s_done", "p_done", "pv_done", "den_abs"))
        x_ready, mean_done, xc_ready, sq_ready, var_done, rstd_done = (sem(n) for n in ("x_ready", "mean_done", "xc_ready", "sq_ready", "var_done", "rstd_done"))
        y_ready, y_hi, y_lo, o_exp = (sem(n) for n in ("y_ready", "y_hi", "y_lo", "o_exp"))
        vt_done, vt_ev, bc_done, d_done, masked, sw_done, rope_done = (sem(n) for n in ("vt_done", "vt_ev", "bc_done", "d_done", "masked", "sw_done", "rope_done"))
        rows_done, mix_added = sem("rows_done"), sem("mix_added")
        qx_ready, sc_done, sc_ev, sc_used = (sem(n) for n in ("qx_ready", "sc_done", "sc_ev", "sc_used"))
        iota_ready = sem("iota_ready")
        chunk_free, dist_ready, exp_ready, route_ready, route_tr, oh_ready, gm_done, g_ev = (
            sem(n) for n in ("chunk_free", "dist_ready", "exp_ready", "route_ready", "route_tr", "oh_ready", "gm_done", "g_ev"))
        a_ready = sem("a_ready")
        a_stored = [sem(f"a_stored{i}") for i in range(2)]
        ag_loaded = [sem(f"ag_loaded{i}") for i in range(RING)]
        ga_done, ga_hi, ga_lo = (sem(n) for n in ("ga_done", "ga_hi", "ga_lo"))
        up_rows_done, f_loaded, res_added, f_r, f_done, stored = (sem(n) for n in ("up_rows_done", "f_loaded", "res_added", "f_r", "f_done", "stored"))

        block = ctx.enter_context(nc.Block())

        def table_cols(at, n, rows=P):
            return table[0:rows, at:at + n]

        def norm_bank(n):
            return 2 * (n % 2) if n <= TT else 2 * (n - TT - 1)

        @block.sync
        def _(sp):
            def known(v):
                return v if isinstance(v, int) else sp.snap(v)

            def load_weights(q, u):
                b = known(q * RING + u)
                free = known(q * RING + (u - RING + 1))
                if isinstance(q, int) and q * RING + u < RING:
                    sp.dma_start(raw[:, u, :], w_blocks[b, :, :]).then_inc(w_loaded[u], 16)
                    return
                if isinstance(q, int):
                    src = w_blocks[b, :, :]
                else:
                    src = w_blocks[bass.ds(b, 1), :, :].rearrange("o p n -> p (o n)")
                sp.wait_ge(w_lo, free)
                sp.dma_start(raw[:, u, :], src).then_inc(w_loaded[u], 16)

            for t in range(TT):
                sp.dma_start(acc[:, t, :], x[0, t * P:(t + 1) * P, :]).then_inc(x_loaded[t], 16)
                if t == 0:
                    sp.dma_start(gain[:, :], gains).then_inc(c_loaded, 16)
                    sp.dma_start(ident[:, :], ident_in).then_inc(c_loaded, 16)
            sp.dma_start(mt[:, :], meta).then_inc(x_loaded[TT], 16)
            sp.dma_start(wg[:, :], w_gates).then_inc(c_loaded, 16)
            sp.dma_start(gb[:, :], gate_bias).then_inc(c_loaded, 16)
            for u in range(RING):
                load_weights(0, u)
            sp.dma_start(table[:, :], table_in).then_inc(t_loaded, 16)
            sp.dma_start(keys_t[:, :, :], keys).then_inc(t_loaded, 16)
            with sp.Fori(1, (B_DOWN + PRE) // RING) as q:
                for u in range(RING):
                    load_weights(q, u)

            def store_act(q, u):
                n = known(q * RING + u)
                ready = known(q * RING + (u + 1))
                sp.wait_ge(a_ready, ready)
                if isinstance(q, int):
                    dst = a_dram[n, :, :]
                else:
                    dst = a_dram[bass.ds(n, 1), :, :].rearrange("o p t -> p (o t)")
                sp.dma_start(dst, a_out[:, u % 2, :]).then_inc(a_stored[u % 2], 16)

            g_view = g_dram.rearrange("j p t -> p j t")

            def store_chunk(r, piece):
                js = slice(piece * P // PIECES, (piece + 1) * P // PIECES)
                if piece == 0:
                    sp.wait_ge(g_ev, known(r * (P // BATCH) + P // BATCH))
                cols = slice(r * P, (r + 1) * P) if isinstance(r, int) else bass.ds(known(r * P), P)
                sp.dma_start(g_view[:, js, cols], gchunk[:, js, :]).then_inc(chunk_free, 16)

            def down_unit(q, chunk=None, piece0=0):
                for u in range(RING):
                    b_unit = q + (B_DOWN // RING + (u + 6) // RING)
                    load_weights(b_unit, (u + 6) % RING)
                    if chunk is not None and piece0 + u < PIECES:
                        store_chunk(chunk, piece0 + u)
                    store_act(q, u)

            for u in range(2):
                load_weights((B_DOWN + PRE) // RING, u)
            with sp.Fori(0, (PRE + PLAIN + BUILD) // RING) as i:
                down_unit(i)
            with sp.Fori(1, TT) as r:
                at = r * ((PLAIN + BUILD) // RING) + PRE // RING
                for i in range(PLAIN // RING):
                    down_unit(at + i, r - 1, i * RING)
                with sp.Fori(0, BUILD // RING) as i:
                    down_unit(at + i + PLAIN // RING)

            def load_ag(q, u, first=False):
                n = known(q * RING + u)
                free = known(q * RING + (u - RING + 1))
                if isinstance(q, int):
                    a_src, g_src = a_dram[n, :, :], g_dram[n, :, :]
                else:
                    a_src = a_dram[bass.ds(n, 1), :, :].rearrange("o p t -> p (o t)")
                    g_src = g_dram[bass.ds(n, 1), :, :].rearrange("o p t -> p (o t)")
                if not first:
                    sp.wait_ge(ga_done, free)
                sp.dma_start(a_in[:, u, :], a_src).then_inc(ag_loaded[u], 16)
                sp.dma_start(g_in[:, u, :], g_src).then_inc(ag_loaded[u], 16)

            for i in range(POST // RING - 1):
                down_unit((P - POST) // RING + i, TT - 1, i * RING)
            sp.wait_ge(chunk_free, 1 + 16 * PIECES * TT)
            for slot in range(2):
                sp.wait_ge(a_stored[slot], 16 * (P - RING) // 2)
            for u in range(RING):
                load_ag(0, u, first=True)
            down_unit(P // RING - 1)
            for slot in range(2):
                sp.wait_ge(a_stored[slot], 16 * P // 2)
            sp.dma_start(fgain[:, :], final_gain).then_inc(f_loaded, 16)
            def up_unit(q, weights=True):
                for u in range(RING):
                    if weights or u < RING - 6 % RING:
                        load_weights(q + (B_UP // RING + (u + 6) // RING), (u + 6) % RING)
                    load_ag(q + 1, u)

            with sp.Fori(0, P // RING - 2) as q:
                up_unit(q)
            up_unit(P // RING - 2, weights=False)
            for t in range(TT):
                sp.wait_ge(f_done, t + 1)
                sp.dma_start(out[0, t * P:(t + 1) * P, :], acc[:, t, :]).then_inc(stored, 16)
            sp.wait_ge(stored, 16 * TT)

        @block.gpsimd
        def _(pool):
            def split_low(q, u):
                pool.wait_ge(w_hi, q * RING + (u + 1))
                nc.gpsimd.tensor_tensor(w_l[:, u, :], raw[:, u, :], w_h[:, u, :].bitcast(F32), ALU.subtract).then_inc(w_lo, 1)

            for b in range(LEAD):
                split_low(0, b)
            for h in range(NH + 1):
                for s in range(4):
                    if h < NH:
                        b = 4 * h + s + LEAD
                        split_low(b // RING, b % RING)
                    if s == 0 and 1 <= h <= MH:
                        pool.wait_ge(d_done, h)
                        for j in range(TT):
                            blk = decay[:, S_AT[j]:S_AT[j] + P]
                            last = nc.gpsimd.affine_select(out=blk, in_=blk, compare_op=ALU.is_ge, fill=0.0, base=0,
                                                           pattern=[[1, P]], channel_multiplier=-1)
                        last.then_inc(masked, 1)
            for b in range(B_OUT + LEAD, B_QUERY):
                split_low(b // RING, b % RING)
            pool.wait_ge(y_lo, NH)
            nc.gpsimd.iota(iota16[:, :], [[1, P]], base=0, channel_multiplier=0,
                           allow_small_or_imprecise_dtypes=True).then_inc(iota_ready, 1)
            with pool.Fori(B_QUERY // RING, B_DOWN // RING) as q:
                for u in range(RING):
                    split_low(q, u)
            with pool.Fori(B_DOWN // RING, B_END // RING) as q:
                for u in range(RING):
                    split_low(q, u)

        @block.scalar
        def _(act):
            own = [0]

            def link(ins):
                own[0] += 1
                ins.then_inc(act_own, 1)
                act.wait_ge(act_own, own[0])

            def split_high(q, u, first=False):
                act.wait_ge(w_loaded[u], q * 16 + 16)
                if not first:
                    act.wait_ge(w_used, q * RING + (u - RING + 1))
                nc.scalar.copy(w_h[:, u, :], raw[:, u, :]).then_inc(w_hi, 1)

            def high(b):
                split_high(b // RING, b % RING, first=b < RING)

            def inv_rms(src, n, scratch, ready, rows=P):
                link(nc.scalar.activation(scratch, src, ACT.Square, accum_out=sums[0:rows, n:n + 1]))
                link(nc.scalar.activation(sums[0:rows, n:n + 1], sums[0:rows, n:n + 1], ACT.Ln, bias=EPS, scale=1.0 / D))
                nc.scalar.activation(rstd[0:rows, n:n + 1], sums[0:rows, n:n + 1], ACT.Exp, scale=-0.5).then_inc(ready, 1)

            def high_xt(n):
                t = n if n <= TT else n - TT - 1
                cols = slice(t * P, t * P + P) if n != TT else slice(SEQ, TOK)
                width = P if n != TT else META
                tmp = ntmp if n <= TT else ntmp2
                act.wait_ge(nt_f, n + 1)
                nc.scalar.copy(xt_h[:, :, cols], tmp[:, n % 2, :, 0:width]).then_inc(nt_hi, 1)

            nc.scalar.preload_act_table_set("natural_log_exp_and_others")

            for n in range(TT + 1):
                act.wait_ge(x_loaded[n], 16)
                src = acc[:, n, :] if n < TT else mt[:, :]
                rows = P if n < TT else META
                inv_rms(src, n, junk[0:rows, :], nt_r, rows)
                if n == TT:
                    act.wait_ge(c_loaded, 64)
                    nc.scalar.copy(wg_h[:, :], wg[:, :]).then_inc(wg_split_h, 1)
                if n >= 2:
                    high_xt(n - 2)
            high(0)
            high_xt(TT - 1)
            high(1)
            high_xt(TT)

            act.wait_ge(g_an, 1)
            link(nc.scalar.activation(hxc[0:MH, :], hx[0:MH, :], ACT.Exp))
            link(nc.scalar.activation(hxc[0:MH, 0:SEQ], hxc[0:MH, 0:SEQ], ACT.Ln, bias=1.0))
            act.wait_ge(g_an, 2)
            link(nc.scalar.activation(rot[0:MH, 0:META], rot[0:MH, 0:META], ACT.Exp))
            nc.scalar.activation(rot[0:MH, 0:META], rot[0:MH, 0:META], ACT.Ln, bias=1.0).then_inc(g_ln, 1)

            for h in range(NH + 1):
                is_m = h < MH
                pair = h % 2
                if h < NH:
                    high(4 * h + LEAD)
                if h >= 1:
                    g = h - 1
                    act.wait_ge(vt_done, g + 1)
                    if g >= 2:
                        act.wait_ge(pv_done, g - 1)
                    nc.scalar.copy(v_tok[:, g % 2, :], ps[:, 7, :])
                    nc.scalar.copy(v_meta[:, g % 2, :], ps[0:META, 4, 0:P]).then_inc(vt_ev, 1)
                    if g < MH:
                        act.wait_ge(bc_done, g + 1)
                        act.wait_ge(g_ready, 1)
                        if g >= 1:
                            act.wait_ge(p_done, g)
                            act.wait_ge(x_ready, g)
                        for j in range(TT):
                            nc.scalar.activation(decay[:, S_AT[j]:S_AT[j + 1]], ps[:, 5, P * j:SEQ], ACT.Exp,
                                                 bias=u_col[:, j, g:g + 1], scale=-1.0)
                        nc.scalar.activation(decay[0:META, S_AT[TT]:S_WIDTH], ps[0:META, 5, :], ACT.Exp,
                                             bias=u_col[0:META, TT, g:g + 1], scale=-1.0)
                        nc.scalar.activation(floor[:, :], ps[:, 6, :], ACT.Exp, scale=-1.0).then_inc(d_done, 1)
                    if g >= 1:
                        act.wait_ge(y_ready, g)
                        nc.scalar.copy(y_h[:, g - 1, :], hy[:, :]).then_inc(y_hi, 1)
                if h == NH:
                    for b in range(B_OUT + LEAD, B_OUT2):
                        high(b)
                if h < NH:
                    act.wait_ge(w_used, 4 * h + 1)
                    if is_m:
                        if h >= 2:
                            act.wait_ge(s_done, h - 1)
                        nc.scalar.copy(qT[:, pair, :], ps[:, 0, :]).then_inc(pj_ev, 1)
                    else:
                        if h > MH:
                            act.wait_ge(rope_done, h - MH)
                        nc.scalar.copy(q_raw[:, :], ps[:, 0, :]).then_inc(pj_ev, 1)
                    high(4 * h + 1 + LEAD)
                    act.wait_ge(w_used, 4 * h + 2)
                    dst = kT[:, pair, :] if is_m else k_raw[:, :]
                    nc.scalar.copy(dst[:, 0:FIRST], ps[:, 1, 0:FIRST])
                    nc.scalar.copy(dst[:, FIRST:TOK], ps[:, 2, 0:REST]).then_inc(pj_ev, 1)
                if h >= 1:
                    g = h - 1
                    act.wait_ge(pv_done, g + 1)
                    if g < MH:
                        nc.scalar.activation(hden[:, :], ps[:, 3, :], ACT.Abs).then_inc(den_abs, 1)
                    else:
                        nc.scalar.copy(hx[:, :], ps[:, 7, :]).then_inc(x_ready, 1)
                if h < NH:
                    high(4 * h + 2 + LEAD)
                    act.wait_ge(w_used, 4 * h + 3)
                    nc.scalar.copy(vT[:, 0:FIRST], ps[:, 0, 0:FIRST])
                    nc.scalar.copy(vT[:, FIRST:TOK], ps[:, 2, REST:2 * REST]).then_inc(pj_ev, 1)
                if h >= 1:
                    act.wait_ge(xc_ready, h)
                    nc.scalar.activation(hsq[:, :], hxc[:, :], ACT.Square).then_inc(sq_ready, 1)
                if h < NH:
                    high(4 * h + 3 + LEAD)
                    act.wait_ge(w_used, 4 * h + 4)
                    if h >= 2:
                        act.wait_ge(y_ready, h - 1)
                    if is_m:
                        nc.scalar.activation(og[:, pair, :], ps[:, 1, :], ACT.Exp, scale=-1.0).then_inc(pj_ev, 1)
                    else:
                        nc.scalar.copy(og[:, pair, :], ps[:, 1, :]).then_inc(pj_ev, 1)
                        act.wait_ge(pj_ev, 4 * h + 4)
                        nc.scalar.activation(eg[:, :], og[:, pair, :], ACT.Exp, scale=-1.0).then_inc(o_exp, 1)
                if h >= 1:
                    act.wait_ge(var_done, h)
                    link(nc.scalar.activation(hsq[:, :], ps[:, 3, :], ACT.Ln, bias=EPS))
                    nc.scalar.activation(hsq[:, :], hsq[:, :], ACT.Exp, scale=-0.5).then_inc(rstd_done, 1)
            act.wait_ge(y_ready, NH)
            nc.scalar.copy(y_h[:, NH - 1, :], hy[:, :]).then_inc(y_hi, 1)
            for b in range(B_OUT2, B_QUERY):
                high(b)

            for n in range(TT + 1, 2 * TT + 1):
                act.wait_ge(mix_added, n - TT)
                inv_rms(acc[:, n - TT - 1, :], n, junk_n2[:, :], nt_r)
                if n >= TT + 2:
                    high_xt(n - 1)
                if n == 2 * TT - 1:
                    for b in range(B_QUERY, B_QUERY + LEAD):
                        high(b)
            high_xt(2 * TT)

            def query(i, first=False):
                for p in range(2):
                    act.wait_ge(w_used, i * 2 + (B_QUERY + p + 1))
                    if not first:
                        act.wait_ge(sc_done, i * 2 + (p - 1))
                    nc.scalar.copy(qx[:, p, :], ps[:, p, :]).then_inc(qx_ready, 1)
                for p in range(2):
                    act.wait_ge(sc_done, i * 2 + (p + 1))
                    if not first:
                        act.wait_ge(sc_used, i * 2 + (p - 1))
                    nc.scalar.copy(sc[:, p, :, :], ps[:, 2 + p, :].rearrange("p (t n) -> p t n", t=TT)).then_inc(sc_ev, 1)

            for i in range(2):
                high(B_QUERY + 2 * i + LEAD)
                high(B_QUERY + 2 * i + 1 + LEAD)
                query(i, first=i == 0)
            with act.Fori(1, PH // 2) as i2:
                for half in range(2):
                    for p in range(2):
                        split_high(i2 + (B_QUERY // RING + half), (2 * half + p + LEAD) % RING)
                    query(i2 * 2 + half)

            def gelu(q, u, first=False):
                act.wait_ge(w_used, q * RING + (B_DOWN + u + 1))
                if not first:
                    act.wait_ge(a_stored[u % 2], q * 32 + 16 * (u // 2))
                nc.scalar.activation(a_out[:, u % 2, :], ps[:, u % 2, :], ACT.Gelu).then_inc(a_ready, 1)

            def down_tile(q, u, first=False):
                split_high(q + (B_DOWN // RING + (u + LEAD) // RING), (u + LEAD) % RING)
                gelu(q, u, first)

            for u in range(RING):
                down_tile(0, u, first=u < 2)
            with act.Fori(0, TT) as r:
                with act.Fori(0, PLAIN // RING - 1) as i:
                    for u in range(RING):
                        down_tile(r * ((PLAIN + BUILD) // RING) + i + PRE // RING, u)
                act.wait_ge(dist_ready, r + 1)
                nc.scalar.activation(expd[:, :, :], dist[:, :, :], ACT.Exp).then_inc(exp_ready, 1)
                for u in range(RING):
                    down_tile(r * ((PLAIN + BUILD) // RING) + (PLAIN + PRE) // RING - 1, u)
                act.wait_ge(chunk_free, r * (16 * PIECES) + 1)
                for i in range(BUILD // RING):
                    for u in range(RING):
                        down_tile(r * ((PLAIN + BUILD) // RING) + (PLAIN + PRE) // RING + i, u)
                        for k in range(PER_TILE):
                            n = (i * RING + u) * PER_TILE + k
                            act.wait_ge(gm_done, r * (P // BATCH) + (n + 1))
                            nc.scalar.activation(gchunk[:, :, n * BATCH:(n + 1) * BATCH].rearrange("p j t -> p t j"),
                                                 ps[:, 2 + n % 2, :].rearrange("p (t j) -> p t j", t=BATCH),
                                                 ACT.Copy, scale=1.0 / GSCALE).then_inc(g_ev, 1)
            with act.Fori(0, POST // RING - 1) as i:
                for u in range(RING):
                    down_tile(i + (P - POST) // RING, u)

            def high_ga(q, u, first=False):
                act.wait_ge(ga_done, q * RING + (u + 1))
                if not first:
                    act.wait_ge(w_used, q * RING + (B_UP + u - RING + 1))
                nc.scalar.copy(y_h[:, u, :], ga[:, u % 2, :]).then_inc(ga_hi, 1)

            for u in range(RING):
                down_tile(P // RING - 1, u)
                if u >= LEAD:
                    high_ga(0, u - LEAD, first=True)

            def up_tile(q, u):
                split_high(q + (B_UP // RING + (u + LEAD) // RING), (u + LEAD) % RING)
                high_ga(q + (u + LEAD) // RING, (u + LEAD) % RING, first=isinstance(q, int) and q == 0 and u < LEAD)

            for u in range(RING):
                up_tile(0, u)
            with act.Fori(1, P // RING - 1) as q:
                for u in range(RING):
                    up_tile(q, u)
            for u in range(RING - LEAD):
                up_tile(P // RING - 1, u)

            nc.scalar.preload_act_table_set("natural_log_exp_and_others")
            for t in range(TT):
                act.wait_ge(res_added, t + 1)
                inv_rms(acc[:, t, :], 2 * TT + 1 + t, junk2[:, :], f_r)

        @block.vector
        def _(dve):
            own = [0]

            def link(ins):
                own[0] += 1
                ins.then_inc(dve_own, 1)
                dve.wait_ge(dve_own, own[0])

            def scale_rows(n):
                src = acc[:, n, :] if n < TT else (mt[:, :] if n == TT else acc[:, n - TT - 1, :])
                rows = META if n == TT else P
                dve.wait_ge(nt_r, n + 1)
                if n >= 2:
                    dve.wait_ge(nt_tr, n - 1)
                nc.vector.tensor_scalar((xn if n <= TT else xn2)[0:rows, n % 2, :], src, rstd[0:rows, n:n + 1], None, ALU.mult).then_inc(nt_xn, 1)

            def apply_gain(n):
                width = META if n == TT else P
                g0 = 0 if n <= TT else KD
                dve.wait_ge(nt_tr, n + 1)
                if n >= 2:
                    dve.wait_ge(nt_lo, n - 1)
                bank = norm_bank(n)
                src = ps[:, bank:bank + 2, :].rearrange("p b (k c) -> p (b k) c", c=P)
                nc.vector.tensor_tensor((ntmp if n <= TT else ntmp2)[:, n % 2, :, 0:width], src[:, :, 0:width],
                                        gain[:, g0:g0 + KD].unsqueeze(2).broadcast_to([P, KD, width]),
                                        ALU.mult).then_inc(nt_f, 1)

            def low_xt(n):
                t = n if n <= TT else n - TT - 1
                cols = slice(t * P, t * P + P) if n != TT else slice(SEQ, TOK)
                width = P if n != TT else META
                dve.wait_ge(nt_hi, n + 1)
                tmp = ntmp if n <= TT else ntmp2
                nc.vector.tensor_tensor(xt_l[:, :, cols], tmp[:, n % 2, :, 0:width], xt_h[:, :, cols].bitcast(F32),
                                        ALU.subtract).then_inc(nt_lo, 1)

            dve.wait_ge(c_loaded, 64)
            for n in range(TT + 1):
                scale_rows(n)
                if n == TT:
                    dve.wait_ge(wg_split_h, 1)
                    nc.vector.tensor_tensor(wg_l[:, :], wg[:, :], wg_h[:, :].bitcast(F32), ALU.subtract).then_inc(wg_split, 1)
                if n >= 1:
                    apply_gain(n - 1)
                if n >= 2:
                    low_xt(n - 2)
            apply_gain(TT)
            low_xt(TT - 1)
            low_xt(TT)

            dve.wait_ge(t_loaded, 32)
            gi, gf, gl = (probs[0:MH, k * TOK:(k + 1) * TOK] for k in range(3))
            gs, gu, g1 = (decay[0:MH, k * TOK:(k + 1) * TOK] for k in range(3))
            dve.wait_ge(g_mm, 1)
            for gate, row in ((gi, 0), (gf, F_ROW)):
                rows = slice(row, row + MH)
                for dst, bank, cols in ((slice(META, META + FIRST), 4, slice(0, FIRST)),
                                        (slice(META + FIRST, TOK), 5, slice(0, SEQ - FIRST)),
                                        (slice(0, META), 5, slice(SEQ - FIRST, REST))):
                    last = nc.vector.tensor_scalar(gate[:, dst], ps[rows, bank, cols], gb[rows, :], None, ALU.add)
            link(last)
            nc.vector.scalar_tensor_tensor(hx[0:MH, :], gf[:, META:TOK], -1.0, gf[:, META:TOK], ALU.mult, ALU.min).then_inc(g_an, 1)
            nc.vector.scalar_tensor_tensor(rot[0:MH, 0:META], gf[:, 0:META], -1.0, gf[:, 0:META], ALU.mult, ALU.min).then_inc(g_an, 1)
            link(nc.vector.memset(g1, 1.0))
            dve.wait_ge(g_ln, 1)
            link(nc.vector.scalar_tensor_tensor(gl[:, META:TOK], gf[:, META:TOK], 0.0, hxc[0:MH, :], ALU.min, ALU.subtract))
            link(nc.vector.scalar_tensor_tensor(gl[:, 0:META], gf[:, 0:META], 0.0, rot[0:MH, 0:META], ALU.min, ALU.subtract))
            link(nc.vector.tensor_tensor_scan(gs, g1, gl, 0.0, ALU.mult, ALU.add))
            link(nc.vector.tensor_tensor(gu, gi, gs, ALU.subtract))
            link(nc.vector.tensor_tensor_scan(gm[:, 0, :], g1, gu, 0.0, ALU.mult, ALU.max))
            nc.vector.tensor_tensor(gm[:, 1, :], gm[:, 0, :], gs, ALU.add).then_inc(g_u, 1)
            dve.wait_ge(g_ut, 1)
            nc.vector.tensor_copy(u_col[:, 0:TT, :], ps[:, 3, 0:TT * MH].rearrange("p (t h) -> p t h", h=MH))
            nc.vector.tensor_copy(u_col[0:META, TT, :], ps[0:META, 3, TT * MH:(TT + 1) * MH]).then_inc(g_ready, 1)

            for h in range(NH + 1):
                if h >= 1:
                    g = h - 1
                    gp = g % 2
                    if g >= MH:
                        dve.wait_ge(sw_done, g - MH + 1)
                        if g >= 2:
                            dve.wait_ge(s_done, g - 1)
                        cos, sin = table_cols(T_COS, TOK), table_cols(T_SIN, TOK)
                        link(nc.vector.tensor_tensor(rot[:, 0:SEQ], ps[:, 5, :], sin[:, 0:SEQ], ALU.mult))
                        link(nc.vector.tensor_tensor(qT[:, gp, :], q_raw[:, :], cos[:, 0:SEQ], ALU.mult))
                        link(nc.vector.tensor_tensor(qT[:, gp, :], qT[:, gp, :], rot[:, 0:SEQ], ALU.add))
                        nc.vector.tensor_tensor(rot[:, 0:SEQ], ps[:, 6, :], sin[:, 0:SEQ], ALU.mult)
                        link(nc.vector.tensor_tensor(rot[:, SEQ:TOK], ps[:, 2, 0:META], sin[:, SEQ:TOK], ALU.mult))
                        link(nc.vector.tensor_tensor(kT[:, gp, :], k_raw[:, :], cos, ALU.mult))
                        nc.vector.tensor_tensor(kT[:, gp, :], kT[:, gp, :], rot[:, :], ALU.add).then_inc(rope_done, 1)
                    if g >= MH:
                        dve.wait_ge(o_exp, g - MH + 1)
                        link(nc.vector.tensor_scalar(eg[:, :], eg[:, :], 1.0, None, ALU.add))
                        link(nc.vector.reciprocal(eg[:, :], eg[:, :]))
                        link(nc.vector.tensor_tensor(og[:, gp, :], og[:, gp, :], eg[:, :], ALU.mult))
                    if g >= 1:
                        dve.wait_ge(y_hi, g)
                        nc.vector.tensor_tensor(y_l[:, g - 1, :], hy[:, :], y_h[:, g - 1, :].bitcast(F32), ALU.subtract).then_inc(y_lo, 1)
                    dve.wait_ge(s_done, g + 1)
                    if g < MH:
                        dve.wait_ge(masked, g + 1)
                    if g >= 1:
                        dve.wait_ge(pv_done, g)
                    where = [(3, 0), (4, 0), (6, 0), (4, COLS[1])]
                    for j in range(TT):
                        bank, at = where[j]
                        w = COLS[j]
                        dec = decay[:, S_AT[j]:S_AT[j + 1]] if g < MH else table_cols(T_DEC + (g - MH) * TOK, w)
                        nc.vector.scalar_tensor_tensor(probs[:, S_AT[j]:S_AT[j + 1]], ps[:, bank, at:at + w], SCALE, dec,
                                                       ALU.mult, ALU.mult)
                    dec = decay[0:META, S_AT[TT]:S_WIDTH] if g < MH else table_cols(T_DEC + (g - MH) * TOK + META, SEQ, META)
                    nc.vector.scalar_tensor_tensor(probs[0:META, S_AT[TT]:S_WIDTH], ps[0:META, 5, :], SCALE, dec,
                                                   ALU.mult, ALU.mult).then_inc(p_done, 1)
                    if g < MH:
                        dve.wait_ge(den_abs, g + 1)
                        link(nc.vector.tensor_tensor(hden[:, :], hden[:, :], floor[:, :], ALU.max))
                        dve.wait_ge(pj_ev, 4 * g + 4)
                        link(nc.vector.scalar_tensor_tensor(hden[:, :], og[:, gp, :], 1.0, hden[:, :], ALU.add, ALU.mult))
                        link(nc.vector.reciprocal(hden[:, :], hden[:, :]))
                        nc.vector.tensor_tensor(hx[:, :], ps[:, 7, :], hden[:, :], ALU.mult).then_inc(x_ready, 1)
                    dve.wait_ge(mean_done, g + 1)
                    nc.vector.tensor_tensor(hxc[:, :], hx[:, :], ps[:, 4, :], ALU.subtract).then_inc(xc_ready, 1)
                    dve.wait_ge(rstd_done, g + 1)
                    head_gain = gain[:, 2 * KD + g:2 * KD + g + 1]
                    if g < MH:
                        nc.vector.scalar_tensor_tensor(hy[:, :], hxc[:, :], head_gain, hsq[:, :], ALU.mult, ALU.mult).then_inc(y_ready, 1)
                    else:
                        link(nc.vector.scalar_tensor_tensor(hxc[:, :], hxc[:, :], head_gain, hsq[:, :], ALU.mult, ALU.mult))
                        nc.vector.tensor_tensor(hy[:, :], hxc[:, :], og[:, gp, :], ALU.mult).then_inc(y_ready, 1)
            dve.wait_ge(y_hi, NH)
            nc.vector.tensor_tensor(y_l[:, NH - 1, :], hy[:, :], y_h[:, NH - 1, :].bitcast(F32), ALU.subtract).then_inc(y_lo, 1)

            def add_sums(t, done, last_used, added):
                if t < TT - 1:
                    dve.wait_ge(done, t + 1)
                else:
                    dve.wait_ge(w_used, last_used)
                for half in range(2):
                    dst = acc[:, t, half * 512:(half + 1) * 512]
                    last = nc.vector.tensor_tensor(dst, dst, ps[:, 2 * t + half, :], ALU.add)
                last.then_inc(added, 1)

            for t in range(TT):
                add_sums(t, rows_done, B_QUERY, mix_added)
                scale_rows(TT + 1 + t)
                if t >= 1:
                    apply_gain(TT + t)
                    low_xt(TT + t)
            apply_gain(2 * TT)
            low_xt(2 * TT)

            link(nc.vector.memset(fence_cell[:, 0:1], 0.0))

            def fence(semaphore, value, cell=0):
                dve.wait_ge(semaphore, value)
                nc.vector.tensor_copy(fence_cell[:, 1 + cell:2 + cell], fence_cell[:, 0:1])

            class Steps:

                def __init__(self, index, size):
                    self.index, self.size, self.start, self.n = index, size, own[0], 0

                def step(self, ins):
                    self.n += 1
                    ins.then_inc(dve_own, 1)

                def value(self):
                    return self.index * self.size + (self.start + self.n)

                def end(self, times):
                    assert self.n == self.size
                    own[0] += self.size * times

            with dve.Fori(0, PH) as h:
                steps = Steps(h, 8)
                for p in range(2):
                    fence(sc_ev, h * 2 + (p + 1), 1 + p)
                    for t in range(TT):
                        last = nc.vector.max(t8v[:, t, p, 0:8], sc[:, p, t, :])
                    steps.step(last)
                    fence(dve_own, steps.value())
                    for t in range(TT):
                        nc.vector.max_index(t8i[:, t, p, 0:8], t8v[:, t, p, 0:8], sc[:, p, t, :])
                    for t in range(TT):
                        last = nc.vector.match_replace(sc_rest[:, p, t, :], t8v[:, t, p, 0:8], sc[:, p, t, :], -3.0e38)
                    steps.step(last)
                    fence(dve_own, steps.value())
                    for t in range(TT):
                        last = nc.vector.max(t8v[:, t, p, 8:16], sc_rest[:, p, t, :])
                    steps.step(last)
                    fence(dve_own, steps.value())
                    for t in range(TT):
                        last = nc.vector.max_index(t8i[:, t, p, 8:16], t8v[:, t, p, 8:16], sc_rest[:, p, t, :])
                    last.then_inc(sc_used, 1)
                fence(sc_used, h * 2 + 2)
                steps.step(nc.vector.tensor_copy(topv[:, :, :, bass.ds(h, 1), :].rearrange("p t s o k -> p t s (o k)"), t8v[:, :, :, :]))
                steps.step(nc.vector.tensor_copy(topi[:, :, :, bass.ds(h, 1), :].rearrange("p t s o k -> p t s (o k)"), t8i[:, :, :, :]))
                fence(dve_own, steps.value())
            steps.end(PH)
            link(nc.vector.tensor_copy(fence_cell[:, 4:5], fence_cell[:, 0:1]))
            nc.vector.tensor_copy(fence_cell[:, 4:5], fence_cell[:, 0:1]).then_inc(chunk_free, 1)
            dve.wait_ge(iota_ready, 1)

            with dve.Fori(0, TT) as r:
                steps = Steps(r, 19)
                step = steps.step

                def behind():
                    dve.wait_ge(dve_own, steps.value())

                def of_tile(tops, s):
                    return tops[:, bass.ds(r, 1), s, :, :].rearrange("p o h k -> p (o h) k")

                cand4 = cand[:, :, :].rearrange("p h (a b) -> p h a b", b=TOPK)
                step(nc.vector.tensor_tensor(cand4, of_tile(topv, 0).unsqueeze(3).broadcast_to([P, PH, TOPK, TOPK]),
                                             of_tile(topv, 1).unsqueeze(2).broadcast_to([P, PH, TOPK, TOPK]), ALU.add))
                fence(dve_own, steps.value())
                for h in range(PH):
                    last = nc.vector.max(tv[:, h, 0:8], cand[:, h, :])
                step(last)
                fence(dve_own, steps.value())
                for h in range(PH):
                    last = nc.vector.max_index(ti[:, h * TOPK:h * TOPK + 8], tv[:, h, 0:8], cand[:, h, :])
                step(last)
                fence(dve_own, steps.value())
                for h in range(PH):
                    last = nc.vector.match_replace(cand[:, h, :], tv[:, h, 0:8], cand[:, h, :], -3.0e38)
                step(last)
                fence(dve_own, steps.value())
                for h in range(PH):
                    last = nc.vector.max(tv[:, h, 8:16], cand[:, h, :])
                step(last)
                fence(dve_own, steps.value())
                nc.vector.tensor_tensor(dist[:, :, :], tv[:, :, :], tv[:, :, 0:1].broadcast_to([P, PH, TOPK]),
                                        ALU.subtract).then_inc(dist_ready, 1)
                for h in range(PH):
                    last = nc.vector.max_index(ti[:, h * TOPK + 8:(h + 1) * TOPK], tv[:, h, 8:16], cand[:, h, :])
                step(last)
                behind()
                nc.vector.tensor_scalar(tj[:, 0, :], ti[:, :], 4, None, ALU.logical_shift_right)
                step(nc.vector.tensor_scalar(tj[:, 1, :], ti[:, :], 15, None, ALU.bitwise_and))
                behind()
                step(nc.vector.tensor_copy(tf[:, :, :], tj[:, :, :]))
                for s in range(2):
                    behind()
                    step(nc.vector.tensor_tensor(eq[:, :, :], tf[:, s, :].unsqueeze(2).broadcast_to([P, P, TOPK]),
                                                 iota16[:, 0:TOPK].unsqueeze(1).broadcast_to([P, P, TOPK]), ALU.is_equal))
                    behind()
                    step(nc.vector.tensor_tensor(pick[:, :, :, :], eq[:, :, :].rearrange("p (h k) a -> p h k a", h=PH),
                                                 of_tile(topi, s).unsqueeze(2).broadcast_to([P, PH, TOPK, TOPK]), ALU.mult))
                    behind()
                    step(nc.vector.tensor_reduce(route[:, s, :], pick[:, :, :, :].rearrange("p h k a -> p (h k) a"), AX.X, ALU.add))
                dve.wait_ge(exp_ready, r + 1)
                step(nc.vector.tensor_reduce(den8[:, 0, :], expd[:, :, :], AX.X, ALU.add))
                behind()
                step(nc.vector.reciprocal(den8[:, 1, :], den8[:, 0, :]))
                behind()
                nc.vector.scalar_tensor_tensor(route[:, 2, :].rearrange("p (h k) -> p h k", h=PH), expd[:, :, :], GSCALE,
                                               den8[:, 1, :].unsqueeze(2).broadcast_to([P, PH, TOPK]), ALU.mult, ALU.mult).then_inc(route_ready, 1)
                dve.wait_ge(route_tr, r + 1)
                nc.vector.tensor_copy(route_t[:, :, :], ps[:, 4, 0:3 * P].rearrange("p (i t) -> p i t", i=3))
                step(nc.vector.tensor_copy(gh16[:, :], ps[:, 4, 2 * P:3 * P]))
                behind()
                step(nc.vector.tensor_copy(gate_h[:, :], gh16[:, :]))
                behind()
                step(nc.vector.tensor_tensor(gate_l[:, :], route_t[:, 2, :], gate_h[:, :], ALU.subtract))
                behind()
                for n in range(P // BATCH):
                    slot = n % 2
                    if n >= 2:
                        dve.wait_ge(gm_done, r * (P // BATCH) + (n - 1))
                    for c in range(BATCH):
                        t = n * BATCH + c
                        nc.vector.tensor_scalar(onehot[:, slot, 0, c, :], iota16[:, :], route_t[:, 0, t:t + 1], None, ALU.is_equal)
                        nc.vector.tensor_scalar(onehot[:, slot, 1, c, :], iota16[:, :], route_t[:, 1, t:t + 1], gate_h[:, t:t + 1],
                                                ALU.is_equal, ALU.mult)
                        last = nc.vector.tensor_scalar(onehot[:, slot, 2, c, :], iota16[:, :], route_t[:, 1, t:t + 1], gate_l[:, t:t + 1],
                                                       ALU.is_equal, ALU.mult)
                    last.then_inc(oh_ready, 1)
            steps.end(TT)

            def weigh(q, u, first=False):
                dve.wait_ge(ag_loaded[u], q * 32 + 32)
                if not first:
                    dve.wait_ge(ga_lo, q * RING + (u - 1))
                nc.vector.tensor_tensor(ga[:, u % 2, :], a_in[:, u, :], g_in[:, u, :], ALU.mult).then_inc(ga_done, 1)
                dve.wait_ge(ga_hi, q * RING + (u + 1))
                nc.vector.tensor_tensor(y_l[:, u, :], ga[:, u % 2, :], y_h[:, u, :].bitcast(F32), ALU.subtract).then_inc(ga_lo, 1)

            for u in range(RING):
                weigh(0, u, first=u < 2)
            with dve.Fori(1, P // RING) as q:
                for u in range(RING):
                    weigh(q, u)

            dve.wait_ge(f_loaded, 16)
            for t in range(TT):
                add_sums(t, up_rows_done, B_END, res_added)
                n = 2 * TT + 1 + t
                dve.wait_ge(f_r, t + 1)
                nc.vector.scalar_tensor_tensor(acc[:, t, :], acc[:, t, :], rstd[:, n:n + 1], fgain[:, :], ALU.mult, ALU.mult).then_inc(f_done, 1)

        @block.tensor
        def _(pe):
            def three(out_ap, stat, mov, first=True, last=True):
                for i, (s_, m_) in enumerate(((stat[0], mov[0]), (stat[0], mov[1]), (stat[1], mov[0]))):
                    ins = nc.tensor.matmul(out_ap, s_, m_, start=first and i == 0, stop=last and i == 2)
                return ins

            def project(u, bank, width=SEQ, cols=slice(0, SEQ), at=0):
                for k in range(KD):
                    ws = (w_h[:, u, k * P:(k + 1) * P], w_l[:, u, k * P:(k + 1) * P])
                    ins = three(ps[:, bank, at:at + width], ws, (xt_h[:, k, cols], xt_l[:, k, cols]), k == 0, k == KD - 1)
                return ins

            def norm_tile(n):
                rows = META if n == TT else P
                pe.wait_ge(nt_xn, n + 1)
                if n >= 2:
                    pe.wait_ge(nt_f, n - 1)
                for k in range(KD):
                    bank = norm_bank(n) + k // 4
                    at = (k % 4) * P
                    ins = nc.tensor.transpose(ps[:, bank, at:at + rows], (xn if n <= TT else xn2)[0:rows, n % 2, k * P:(k + 1) * P], ident[0:rows, 0:rows])
                ins.then_inc(nt_tr, 1)

            pe.wait_ge(c_loaded, 64)
            for n in range(TT + 1):
                norm_tile(n)

            pe.wait_ge(t_loaded, 32)
            pe.wait_ge(nt_lo, TT + 1)
            pe.wait_ge(wg_split, 1)
            for bank, cols in ((4, slice(0, FIRST)), (5, slice(FIRST, TOK))):
                for k in range(KD):
                    at = k * G_ROWS
                    ins = three(ps[0:G_ROWS, bank, 0:cols.stop - cols.start], (wg_h[:, at:at + G_ROWS], wg_l[:, at:at + G_ROWS]),
                                (xt_h[:, k, cols], xt_l[:, k, cols]), k == 0, k == KD - 1)
            ins.then_inc(g_mm, 1)

            def out_rows(j, banks):
                u = (B_OUT + j) % RING
                for bank in banks:
                    cols = slice((bank // 2) * P, (bank // 2 + 1) * P)
                    ins = three(ps[:, bank, :], (y_h[:, j, cols], y_l[:, j, cols]),
                                tuple(w_[:, u, (bank % 2) * 512:(bank % 2 + 1) * 512] for w_ in (w_h, w_l)), j == 0, j == KD - 1)
                return ins

            for h in range(NH + 1):
                is_m = h < MH
                g, gp = h - 1, (h - 1) % 2
                hp = h % 2

                def block_of(s):
                    b = 4 * h + s
                    pe.wait_ge(w_lo, b + 1)
                    if b >= 2:
                        pe.wait_ge(pj_ev, b - 1)
                    return b

                if h < NH:
                    b = block_of(0)
                    project(b % RING, 0).then_inc(w_used, 1)
                if h == NH:
                    pe.wait_ge(pj_ev, 4 * NH)
                    pe.wait_ge(y_lo, 4)
                    for j in range(4):
                        pe.wait_ge(w_lo, B_OUT + j + 1)
                        out_rows(j, (0, 1))
                if h >= 1:
                    pe.wait_ge(vt_ev, g + 1)
                    if g >= 1:
                        pe.wait_ge(rstd_done, g)
                    if g < MH:
                        pe.wait_ge(d_done, g + 1)
                    else:
                        pe.wait_ge(rope_done, g - MH + 1)
                    for j, (bank, at) in enumerate(((3, 0), (4, 0), (6, 0), (4, COLS[1]))):
                        nc.tensor.matmul(ps[:, bank, at:at + COLS[j]], kT[:, gp, j * P:(j + 1) * P], qT[:, gp, j * P:SEQ], start=True, stop=True)
                    nc.tensor.matmul(ps[0:META, 5, :], kT[:, gp, SEQ:TOK], qT[:, gp, :], start=True, stop=True).then_inc(s_done, 1)
                if h < NH:
                    b = block_of(1)
                    project(b % RING, 1, FIRST, slice(0, FIRST))
                    if h > MH:
                        pe.wait_ge(rope_done, h - MH)
                    project(b % RING, 2, REST, slice(FIRST, TOK), 0).then_inc(w_used, 1)
                if h == NH:
                    for j in range(4):
                        out_rows(j, (2,))
                if h >= 1:
                    pe.wait_ge(p_done, g + 1)

                    def over_keys(bank, meta_stat, stats):
                        ins = nc.tensor.matmul(ps[:, bank, :], meta_stat, probs[0:META, S_AT[TT]:S_WIDTH], start=True, stop=False)
                        for j in range(TT):
                            ins = nc.tensor.matmul(ps[:, bank, j * P:SEQ], stats[j], probs[:, S_AT[j]:S_AT[j + 1]],
                                                   start=False, stop=j == TT - 1)
                        return ins

                    if g < MH:
                        over_keys(3, table_cols(T_ONE, P, META), [table_cols(T_ONE, P)] * TT)
                    over_keys(7, v_meta[:, gp, :], [v_tok[:, gp, j * P:(j + 1) * P] for j in range(TT)]).then_inc(pv_done, 1)
                if h < NH:
                    b = block_of(2)
                    project(b % RING, 0, FIRST, slice(0, FIRST))
                    pe.wait_ge(pj_ev, 4 * h + 2)
                    project(b % RING, 2, REST, slice(FIRST, TOK), REST).then_inc(w_used, 1)
                if h == NH:
                    for j in range(2):
                        out_rows(j, (5,))
                if h >= 1:
                    pe.wait_ge(x_ready, g + 1)
                    nc.tensor.matmul(ps[:, 4, :], table_cols(T_MEAN, P), hx[:, :], start=True, stop=True).then_inc(mean_done, 1)
                if h < NH:
                    b = block_of(3)
                    project(b % RING, 1).then_inc(w_used, 1)
                if h == NH:
                    for j in range(4):
                        if j >= 2:
                            out_rows(j, (5,))
                    out_rows(0, (6,))
                if h >= 1:
                    pe.wait_ge(sq_ready, g + 1)
                    nc.tensor.matmul(ps[:, 3, :], table_cols(T_MEAN, P), hsq[:, :], start=True, stop=True).then_inc(var_done, 1)
                if h < NH:
                    if is_m:
                        if h == 0:
                            pe.wait_ge(g_u, 1)
                            for j in range(TT):
                                nc.tensor.transpose(ps[:, 3, j * MH:(j + 1) * MH],
                                                    decay[0:MH, TOK + META + j * P:TOK + META + (j + 1) * P], ident[0:MH, 0:MH])
                            nc.tensor.transpose(ps[0:META, 3, TT * MH:(TT + 1) * MH], decay[0:MH, TOK:TOK + META],
                                                ident[0:MH, 0:MH]).then_inc(g_ut, 1)
                        for bank, row in ((5, 0), (6, 1)):
                            ins = nc.tensor.matmul(ps[:, bank, :], table[0:MH, T_SEL + h * P:T_SEL + (h + 1) * P], gm[:, row, META:TOK],
                                                   start=True, stop=True)
                        ins.then_inc(bc_done, 1)
                    else:
                        pe.wait_ge(pj_ev, 4 * h + 3)
                        swap = table_cols(T_SWAP, P)
                        nc.tensor.matmul(ps[:, 5, :], swap, q_raw[:, :], start=True, stop=True)
                        nc.tensor.matmul(ps[:, 6, :], swap, k_raw[:, 0:SEQ], start=True, stop=True)
                        nc.tensor.matmul(ps[:, 2, 0:META], swap, k_raw[:, SEQ:TOK], start=True, stop=True).then_inc(sw_done, 1)
                    pe.wait_ge(pj_ev, 4 * h + 3)
                    for j in range(TT):
                        nc.tensor.transpose(ps[:, 7, j * P:(j + 1) * P], vT[:, j * P:(j + 1) * P], ident[:, :])
                    nc.tensor.transpose(ps[0:META, 4, 0:P], vT[:, SEQ:TOK], ident[:, :]).then_inc(vt_done, 1)

            def add_rows(u, slot, first, last, order=range(TT), before={}):
                for t in order:
                    if t in before:
                        before[t]()
                    cols = slice(t * P, (t + 1) * P)
                    for i, (y_, w_) in enumerate(((y_h, w_h), (y_h, w_l), (y_l, w_h))):
                        for half in range(2):
                            ins = nc.tensor.matmul(ps[:, 2 * t + half, :], y_[:, slot, cols], w_[:, u, half * 512:(half + 1) * 512],
                                                   start=first and i == 0, stop=last and i == 2)
                return ins

            for j in range(1, 4):
                out_rows(j, (6,))
            for j in range(4):
                out_rows(j, (7,))
            pe.wait_ge(rstd_done, NH)
            for j in range(4):
                out_rows(j, (3, 4)).then_inc(w_used, 1)
            for t in range(TT):
                for j in range(4, KD):
                    if t == 0:
                        pe.wait_ge(w_lo, B_OUT + j + 1)
                        if j == KD - 1:
                            pe.wait_ge(y_lo, NH)
                    ins = out_rows(j, (2 * t, 2 * t + 1))
                    if t == TT - 1:
                        ins.then_inc(w_used, 1)
                    elif j == KD - 1:
                        ins.then_inc(rows_done, 1)
                if t >= 1:
                    norm_tile(TT + t)

            half = SEQ // 2
            pe.wait_ge(nt_lo, TT + 3)
            for p in range(2):
                pe.wait_ge(w_lo, B_QUERY + p + 1)
                project(p, p, half, slice(0, half))
            norm_tile(2 * TT)
            pe.wait_ge(nt_lo, 2 * TT + 1)

            def query(i, u0, first=False):
                for p in range(2):
                    pe.wait_ge(w_lo, i * 2 + (B_QUERY + p + 1))
                    if not first:
                        pe.wait_ge(qx_ready, i * 2 + (p - 1))
                    if first:
                        project(u0 + p, p, half, slice(half, SEQ), half).then_inc(w_used, 1)
                    else:
                        project(u0 + p, p).then_inc(w_used, 1)
                for p in range(2):
                    pe.wait_ge(qx_ready, i * 2 + (p + 1))
                    if not first:
                        pe.wait_ge(sc_ev, i * 2 + (p - 1))
                    for t in range(TT):
                        ins = nc.tensor.matmul(ps[:, 2 + p, t * P:(t + 1) * P], qx[:, p, t * P:(t + 1) * P], keys_t[:, p, :],
                                               start=True, stop=True)
                    ins.then_inc(sc_done, 1)

            query(0, 0, first=True)
            query(1, 2)
            with pe.Fori(1, PH // 2) as i2:
                for half in range(2):
                    query(i2 * 2 + half, 2 * half)

            def down_tile(q, u, first=False, between={}):
                pe.wait_ge(w_lo, q * RING + (B_DOWN + u + 1))
                if not first:
                    pe.wait_ge(a_ready, q * RING + (u - 1))
                for k in range(KD):
                    ws = (w_h[:, u, k * P:(k + 1) * P], w_l[:, u, k * P:(k + 1) * P])
                    ins = three(ps[:, u % 2, :], ws, (xt_h[:, k, 0:SEQ], xt_l[:, k, 0:SEQ]), k == 0, k == KD - 1)
                    if k in between:
                        between[k]()
                ins.then_inc(w_used, 1)

            for u in range(RING):
                down_tile(0, u, first=u < 2)
            with pe.Fori(0, TT) as r:
                with pe.Fori(0, PLAIN // RING - 1) as i:
                    for u in range(RING):
                        down_tile(r * ((PLAIN + BUILD) // RING) + i + PRE // RING, u)

                def turn_routing():
                    pe.wait_ge(route_ready, r + 1)
                    for i in range(3):
                        ins = nc.tensor.transpose(ps[:, 4, i * P:(i + 1) * P], route[:, i, :], ident[:, :])
                    ins.then_inc(route_tr, 1)

                for u in range(RING):
                    down_tile(r * ((PLAIN + BUILD) // RING) + (PLAIN + PRE) // RING - 1, u,
                              between={0: turn_routing} if u == RING - 2 else {})

                def gate_batch(n):
                    pe.wait_ge(oh_ready, r * (P // BATCH) + (n + 1))
                    if n >= 2:
                        pe.wait_ge(g_ev, r * (P // BATCH) + (n - 1))
                    for c in range(BATCH):
                        for part in (1, 2):
                            ins = nc.tensor.matmul(ps[:, 2 + n % 2, c * P:(c + 1) * P], onehot[:, n % 2, 0, c, :],
                                                   onehot[:, n % 2, part, c, :], start=part == 1, stop=part == 2)
                    ins.then_inc(gm_done, 1)

                for i in range(BUILD // RING):
                    for u in range(RING):
                        n0 = (i * RING + u) * PER_TILE
                        step = KD // PER_TILE
                        between = {step * (k + 1) - 2: (lambda n=n0 + k: gate_batch(n)) for k in range(PER_TILE)}
                        down_tile(r * ((PLAIN + BUILD) // RING) + (PLAIN + PRE) // RING + i, u, between=between)
            with pe.Fori(0, POST // RING) as i:
                for u in range(RING):
                    down_tile(i + (P - POST) // RING, u)

            pe.wait_ge(g_ev, TT * P // BATCH)

            def up_tile(q, u, first=False, last=False):
                pe.wait_ge(w_lo, q * RING + (B_UP + u + 1))
                pe.wait_ge(ga_lo, q * RING + (u + 1))
                if first:
                    add_rows(u, u, first, last, order=(1, 2, 3, 0),
                             before={0: lambda: pe.wait_ge(a_ready, P)}).then_inc(w_used, 1)
                else:
                    add_rows(u, u, first, last).then_inc(w_used, 1)

            for u in range(RING):
                up_tile(0, u, first=u == 0)
            with pe.Fori(1, P // RING - 1) as q:
                for u in range(RING):
                    up_tile(q, u)
            for t in range(TT):
                for u in range(RING):
                    if t == 0:
                        pe.wait_ge(w_lo, B_END - RING + u + 1)
                        pe.wait_ge(ga_lo, P - RING + u + 1)
                    ins = add_rows(u, u, False, u == RING - 1, order=(t,))
                    if t == TT - 1:
                        ins.then_inc(w_used, 1)
                    elif u == RING - 1:
                        ins.then_inc(up_rows_done, 1)


def _tables():
    import numpy as np
    tab = np.zeros((P, T_END), np.float32)
    pos = np.concatenate([np.arange(META, META + SEQ), np.arange(META)]).astype(np.float32)
    half = P // 2
    inv = (np.float32(10000.0) ** (-np.arange(half, dtype=np.float32) / np.float32(half))).astype(np.float32)
    ang = (pos[None, :] * inv[:, None]).astype(np.float32)
    cos, sin = np.cos(ang.astype(np.float64)), np.sin(ang.astype(np.float64))
    tab[:, T_COS:T_COS + TOK] = np.concatenate([cos, cos], 0)
    tab[:, T_SIN:T_SIN + TOK] = np.concatenate([-sin, sin], 0)
    gap = np.arange(TOK)[None, :] - np.arange(P)[:, None]
    for h in range(RH):
        lg = math.log1p(-2.0 ** (-5.0 - h))
        tab[:, T_DEC + h * TOK:T_DEC + (h + 1) * TOK] = np.where(gap >= 0, np.exp(lg * np.maximum(gap, 0)), 0.0)
    for m in range(P):
        tab[(m + half) % P, T_SWAP + m] = 1.0
    tab[:, T_ONE:T_ONE + P] = 1.0
    tab[:, T_MEAN:T_MEAN + P] = 1.0 / P
    for h in range(MH):
        tab[h, T_SEL + h * P:T_SEL + (h + 1) * P] = 1.0
    return tab

def kernel(x, meta_tokens, norm1_w, w_in, gate_bias, m_norm_w, r_norm_w, w_out, norm2_w,
           peer_w_query, peer_sub_keys, peer_w_down, peer_w_up, final_norm_w):
    import numpy as np
    import concourse.bacc as bacc
    from concourse.bass_utils import run_bass_kernel_spmd

    def columns(w):
        w = np.asarray(w)
        n = w.shape[1] // P
        return w.reshape(KD, P, n, P).transpose(2, 1, 0, 3).reshape(n, P, D)

    def gate_rows(g):
        rows = np.zeros(g.shape[:-1] + (G_ROWS,), g.dtype)
        rows[..., :MH] = g[..., :MH]
        rows[..., F_ROW:] = g[..., MH:]
        return rows

    w_in0 = np.asarray(w_in)[0]
    head_cols = [part * MH * P + h * P for h in range(MH) for part in range(4)]
    head_cols += [(4 + part) * RH * P + h * P for h in range(RH) for part in range(4)]
    by_head = np.concatenate([w_in0[:, c:c + P] for c in head_cols], axis=1)
    down = np.asarray(peer_w_down)[0].reshape(P, P, KD, P).transpose(1, 3, 2, 0).reshape(P, P, D)
    up = np.asarray(peer_w_up)[0].reshape(P, P, D).transpose(1, 0, 2)
    arrays = {
        "x": np.asarray(x),
        "meta": np.asarray(meta_tokens),
        "w_blocks": np.concatenate([columns(by_head), np.asarray(w_out)[0].reshape(KD, P, D),
                                    columns(np.asarray(peer_w_query)[0]), down, up], axis=0),
        "w_gates": gate_rows(w_in0[:, 4 * (MH + RH) * P:]).reshape(KD, P, G_ROWS).transpose(1, 0, 2).reshape(P, KD * G_ROWS),
        "gate_bias": gate_rows(np.asarray(gate_bias)).reshape(G_ROWS, 1),
        "gains": np.concatenate([np.asarray(norm1_w).reshape(KD, P), np.asarray(norm2_w).reshape(KD, P),
                                 np.asarray(m_norm_w).reshape(MH, P), np.asarray(r_norm_w).reshape(RH, P)], axis=0).T,
        "final_gain": np.broadcast_to(np.asarray(final_norm_w)[None], (P, D)),
        "keys": np.asarray(peer_sub_keys)[0].transpose(2, 0, 1),
        "ident": np.eye(P, dtype=np.float32),
        "table": _tables(),
    }
    nc = bacc.Bacc("TRN2", target_bir_lowering=False, num_devices=1)
    args = {}
    for name in arrays:
        arrays[name] = np.ascontiguousarray(arrays[name])
        args[name] = nc.dram_tensor("in_" + name, arrays[name].shape, F32, kind="ExternalInput").ap()
    out = nc.dram_tensor("out_dram", (1, SEQ, D), F32, kind="ExternalOutput").ap()
    mixer_peer_kernel(nc, args["x"], args["meta"], args["w_blocks"], args["w_gates"], args["gate_bias"],
                      args["gains"], args["final_gain"], args["keys"], args["ident"], args["table"], out)
    r = run_bass_kernel_spmd(nc, [{"in_" + n: a for n, a in arrays.items()}], core_ids=[0])
    return r.results[0]["out_dram"]
```

```python
import math
from contextlib import ExitStack

import concourse.bass as bass
from concourse import mybir

F32 = mybir.dt.float32
F32R = mybir.dt.float32r
F16 = mybir.dt.float16
U32 = mybir.dt.uint32
ALU = mybir.AluOpType
ACT = mybir.ActivationFunctionType
AX = mybir.AxisListType

P = 128
D = 1024
KD = D // P
SEQ = 512
META = 16
TOK = SEQ + META
TT = SEQ // P
MH, RH = 4, 4
NH = MH + RH
PH = 8
TOPK = 16
EPS = 1e-6
SCALE = P ** -0.5
GSCALE = 4096.0

B_OUT = 4 * NH
B_OUT2 = B_OUT + 4
B_QUERY = B_OUT + KD
B_DOWN = B_QUERY + 2 * PH
B_UP = B_DOWN + P
B_END = B_UP + P
RING = 4
LEAD = 2

PRE = 4
PLAIN = 12
BUILD = 16
POST = P - PRE - TT * (PLAIN + BUILD)
PIECES = 16
BATCH = 4
PER_TILE = P // BATCH // BUILD

FIRST = 272
REST = TOK - FIRST
F_ROW = 32
G_ROWS = F_ROW + MH

KT = TT + 1
ROWS = [P] * TT + [TOK - TT * P]
T0 = [max(0, j * P - META) for j in range(KT)]
COLS = [SEQ - t0 for t0 in T0]
S_AT = [sum(COLS[:j]) for j in range(KT + 1)]
S_BANK = [(3, 0), (4, 0), (6, 0), (6, COLS[2]), (4, COLS[1])]
XS = slice(META, TOK)

NORM_OF = [0, 1, TT, 2, 3] + list(range(TT))
NORM_ROWS = [META if t == TT else P for t in NORM_OF]
NORM_COLS = [slice(0, META) if t == TT else slice(META + t * P, META + (t + 1) * P) for t in NORM_OF]

T_COS, T_SIN, T_DEC = 0, TOK, 2 * TOK
T_SWAP = T_DEC + RH * TOK
T_ONE = T_SWAP + P
T_MEAN = T_ONE + P
T_SEL = T_MEAN + P
T_END = T_SEL + MH * P


def mixer_peer_kernel(nc, x, meta, w_blocks, w_gates, gate_bias, gains, final_gain, keys, ident_in, table_in, out):
    a_dram = nc.dram_tensor("act_scratch", (P, P, SEQ), F32, kind="Internal").ap()
    g_dram = nc.dram_tensor("gate_scratch", (P, P, SEQ), F32, kind="Internal").ap()

    ctx = ExitStack()
    with ctx:
        def sb(name, shape, dt=F32, scope=ctx):
            return scope.enter_context(nc.sbuf_tensor(name, shape, dt))

        def sem(name):
            return ctx.enter_context(nc.semaphore(name))

        raw = sb("raw", [P, RING, D])
        w_h = sb("w_h", [P, RING, D], F32R)
        w_l = sb("w_l", [P, RING, D], F32R)
        xt_h = sb("xt_h", [P, KD, TOK], F32R)
        xt_l = sb("xt_l", [P, KD, TOK], F32R)
        acc = sb("acc", [P, TT, D])
        ident = sb("ident", [P, P])
        keys_t = sb("keys_t", [P, 2, P])
        gain = sb("gain", [P, 2 * KD + NH])
        sums = sb("sums", [P, 16])
        rstd = sb("rstd", [P, 16])
        fence_cell = sb("fence_cell", [P, 5])

        with ExitStack() as region:
            xn = sb("xn", [P, 2, D], scope=region)
            ntmp = sb("ntmp", [P, 2, KD, P], scope=region)
            junk = sb("junk", [P, D], scope=region)
            mt = sb("mt", [META, D], scope=region)
            wg = sb("wg", [P, KD * G_ROWS], scope=region)
            wg_h = sb("wg_h", [P, KD * G_ROWS], F32R, scope=region)
            wg_l = sb("wg_l", [P, KD * G_ROWS], F32R, scope=region)
            gb = sb("gb", [G_ROWS, 1], scope=region)
            gm = sb("gm", [MH, 2, TOK], scope=region)
        with ExitStack() as region:
            topv = sb("topv", [P, TT, 2, PH, TOPK], scope=region)
            topi = sb("topi", [P, TT, 2, PH, TOPK], scope=region)
            cand = sb("cand", [P, PH, TOPK * TOPK], scope=region)
            tv = sb("tv", [P, PH, TOPK], scope=region)
            ti = sb("ti", [P, PH * TOPK], U32, scope=region)
            tj = sb("tj", [P, 2, PH * TOPK], U32, scope=region)
            tf = sb("tf", [P, 2, PH * TOPK], scope=region)
            dist = sb("dist", [P, PH, TOPK], scope=region)
            expd = sb("expd", [P, PH, TOPK], scope=region)
            den8 = sb("den8", [P, 2, PH], scope=region)
            route = sb("route", [P, 3, PH * TOPK], scope=region)
            eq = sb("eq", [P, PH * TOPK, TOPK], F16, scope=region)
            pick = sb("pick", [P, PH, TOPK, TOPK], F16, scope=region)
            gh16 = sb("gh16", [P, P], F16, scope=region)
            route_t = sb("route_t", [P, 3, P], scope=region)
        y_h = sb("y_h", [P, KD, SEQ], F32R)
        y_l = sb("y_l", [P, KD, SEQ], F32R)

        with ExitStack() as region:
            table = sb("table", [P, T_END], scope=region)
            qT = sb("qT", [P, 2, SEQ], scope=region)
            kT = sb("kT", [P, 2, TOK], scope=region)
            vT = sb("vT", [P, TOK], scope=region)
            v_tok = sb("v_tok", [P, 2, TT * P], scope=region)
            v_last = sb("v_last", [ROWS[TT], 2, P], scope=region)
            og = sb("og", [P, 2, SEQ], scope=region)
            decay = sb("decay", [P, S_AT[KT]], scope=region)
            probs = sb("probs", [P, S_AT[KT]], scope=region)
            hden = sb("hden", [P, SEQ], scope=region)
            eg = hden
            hx = sb("hx", [P, SEQ], scope=region)
            hxc = sb("hxc", [P, SEQ], scope=region)
            hsq = sb("hsq", [P, SEQ], scope=region)
            hy = sb("hy", [P, SEQ], scope=region)
            q_raw = sb("q_raw", [P, SEQ], scope=region)
            k_raw = sb("k_raw", [P, TOK], scope=region)
            rot = sb("rot", [P, TOK], scope=region)
            floor = rot[:, 0:SEQ]
            part_h = sb("part_h", [P, SEQ], F32R, scope=region)
            part_l = sb("part_l", [P, SEQ], F32R, scope=region)
            mean_r = sb("mean_r", [P, P], F32R, scope=region)
            sel_r = sb("sel_r", [MH, MH * P], F32R, scope=region)
            gm_h = sb("gm_h", [MH, 2, SEQ], F32R, scope=region)
            gm_l = sb("gm_l", [MH, 2, SEQ], F32R, scope=region)
            u_col = sb("u_col", [P, TT + 1, MH], scope=region)
        with ExitStack() as region:
            qx = sb("qx", [P, 2, SEQ], scope=region)
            sc = sb("sc", [P, 2, TT, P], scope=region)
            t8v = sb("t8v", [P, TT, 2, TOPK], scope=region)
            t8i = sb("t8i", [P, TT, 2, TOPK], U32, scope=region)
            sc_rest = sb("sc_rest", [P, 2, TT, P], scope=region)
            xn2 = sb("xn2", [P, 2, D], scope=region)
            ntmp2 = sb("ntmp2", [P, 2, KD, P], scope=region)
            junk_n2 = sb("junk_n2", [P, D], scope=region)
        with ExitStack() as region:
            gchunk = sb("gchunk", [P, P, P], scope=region)
            onehot = sb("onehot", [P, 2, 3, BATCH, P], F16, scope=region)
            a_out = sb("a_out", [P, 2, SEQ], scope=region)
            iota16 = sb("iota16", [P, P], F16, scope=region)
            gate_h = sb("gate_h", [P, P], scope=region)
            gate_l = sb("gate_l", [P, P], scope=region)
        with ExitStack() as region:
            a_in = sb("a_in", [P, RING, SEQ], scope=region)
            g_in = sb("g_in", [P, RING, SEQ], scope=region)
            ga = sb("ga", [P, 2, SEQ], scope=region)
            fgain = sb("fgain", [P, D], scope=region)
            junk2 = sb("junk2", [P, D], scope=region)

        ps = ctx.enter_context(nc.psum_tensor("ps", [P, 8, 512], F32))

        w_loaded = [sem(f"w_loaded{i}") for i in range(RING)]
        w_hi, w_lo, w_used = sem("w_hi"), sem("w_lo"), sem("w_used")
        x_loaded = [sem(f"x_loaded{i}") for i in range(TT + 1)]
        c_loaded, wg_loaded = sem("c_loaded"), sem("wg_loaded")
        t_loaded = sem("t_loaded")
        nt_r, nt_xn, nt_tr, nt_f, nt_hi, nt_lo = (sem(n) for n in ("nt_r", "nt_xn", "nt_tr", "nt_f", "nt_hi", "nt_lo"))
        act_own, dve_own = sem("act_own"), sem("dve_own")
        wg_split_h, wg_split = sem("wg_split_h"), sem("wg_split")
        const_ready, gm_hi, gm_lo = sem("const_ready"), sem("gm_hi"), sem("gm_lo")
        x_hi, x_lo, sq_hi, sq_lo = (sem(n) for n in ("x_hi", "x_lo", "sq_hi", "sq_lo"))
        g_mm, g_an, g_ln, g_u, g_ut, g_ready = (sem(n) for n in ("g_mm", "g_an", "g_ln", "g_u", "g_ut", "g_ready"))
        pj_ev, s_done, p_done, den_done, pv_done, den_abs = (
            sem(n) for n in ("pj_ev", "s_done", "p_done", "den_done", "pv_done", "den_abs"))
        x_ready, mean_done, xc_ready, sq_ready, var_done, rstd_done = (sem(n) for n in ("x_ready", "mean_done", "xc_ready", "sq_ready", "var_done", "rstd_done"))
        y_ready, y_hi, y_lo, o_exp = (sem(n) for n in ("y_ready", "y_hi", "y_lo", "o_exp"))
        vt_done, vt_ev, bc_done, d_done, masked, sw_done, rope_done = (sem(n) for n in ("vt_done", "vt_ev", "bc_done", "d_done", "masked", "sw_done", "rope_done"))
        rows_done, mix_added = sem("rows_done"), sem("mix_added")
        qx_ready, sc_done, sc_ev, sc_used = (sem(n) for n in ("qx_ready", "sc_done", "sc_ev", "sc_used"))
        iota_ready = sem("iota_ready")
        chunk_free, dist_ready, exp_ready, route_ready, route_tr, oh_ready, gm_done, g_ev = (
            sem(n) for n in ("chunk_free", "dist_ready", "exp_ready", "route_ready", "route_tr", "oh_ready", "gm_done", "g_ev"))
        a_ready = sem("a_ready")
        a_stored = [sem(f"a_stored{i}") for i in range(2)]
        ag_loaded = [sem(f"ag_loaded{i}") for i in range(RING)]
        ga_done, ga_hi, ga_lo = (sem(n) for n in ("ga_done", "ga_hi", "ga_lo"))
        up_rows_done, f_loaded, res_added, f_r, f_done, stored = (sem(n) for n in ("up_rows_done", "f_loaded", "res_added", "f_r", "f_done", "stored"))

        block = ctx.enter_context(nc.Block())

        def table_cols(at, n, rows=P):
            return table[0:rows, at:at + n]

        def norm_bank(n):
            return 2 * (n % 2) if n <= TT else 2 * (n - TT - 1)

        @block.sync
        def _(sp):
            def known(v):
                return v if isinstance(v, int) else sp.snap(v)

            def load_weights(q, u):
                b = known(q * RING + u)
                free = known(q * RING + (u - RING + 1))
                if isinstance(q, int) and q * RING + u < RING:
                    sp.dma_start(raw[:, u, :], w_blocks[b, :, :]).then_inc(w_loaded[u], 16)
                    return
                if isinstance(q, int):
                    src = w_blocks[b, :, :]
                else:
                    src = w_blocks[bass.ds(b, 1), :, :].rearrange("o p n -> p (o n)")
                sp.wait_ge(w_lo, free)
                sp.dma_start(raw[:, u, :], src).then_inc(w_loaded[u], 16)

            for t in range(TT):
                sp.dma_start(acc[:, t, :], x[0, t * P:(t + 1) * P, :]).then_inc(x_loaded[t], 16)
                if t == 0:
                    sp.dma_start(gain[:, :], gains).then_inc(c_loaded, 16)
                    sp.dma_start(ident[:, :], ident_in).then_inc(c_loaded, 16)
                if t == 1:
                    sp.dma_start(mt[:, :], meta).then_inc(x_loaded[TT], 16)
                    sp.dma_start(wg[:, :], w_gates).then_inc(wg_loaded, 16)
                    sp.dma_start(gb[:, :], gate_bias).then_inc(wg_loaded, 16)
            for u in range(RING):
                load_weights(0, u)
            sp.dma_start(table[:, :], table_in).then_inc(t_loaded, 16)
            sp.dma_start(keys_t[:, :, :], keys).then_inc(t_loaded, 16)
            with sp.Fori(1, (B_DOWN + PRE) // RING) as q:
                for u in range(RING):
                    load_weights(q, u)

            def store_act(q, u):
                n = known(q * RING + u)
                ready = known(q * RING + (u + 1))
                sp.wait_ge(a_ready, ready)
                if isinstance(q, int):
                    dst = a_dram[n, :, :]
                else:
                    dst = a_dram[bass.ds(n, 1), :, :].rearrange("o p t -> p (o t)")
                sp.dma_start(dst, a_out[:, u % 2, :]).then_inc(a_stored[u % 2], 16)

            g_view = g_dram.rearrange("j p t -> p j t")

            def store_chunk(r, piece):
                js = slice(piece * P // PIECES, (piece + 1) * P // PIECES)
                if piece == 0:
                    sp.wait_ge(g_ev, known(r * (P // BATCH) + P // BATCH))
                cols = slice(r * P, (r + 1) * P) if isinstance(r, int) else bass.ds(known(r * P), P)
                sp.dma_start(g_view[:, js, cols], gchunk[:, js, :]).then_inc(chunk_free, 16)

            def down_unit(q, chunk=None, i=0, tiles=PLAIN):
                for u in range(RING):
                    b_unit = q + (B_DOWN // RING + (u + 6) // RING)
                    load_weights(b_unit, (u + 6) % RING)
                    if chunk is not None:
                        tile = i * RING + u
                        for piece in range(tile * PIECES // tiles, (tile + 1) * PIECES // tiles):
                            store_chunk(chunk, piece)
                    store_act(q, u)

            for u in range(2):
                load_weights((B_DOWN + PRE) // RING, u)
            with sp.Fori(0, (PRE + PLAIN + BUILD) // RING) as i:
                down_unit(i)
            with sp.Fori(1, TT) as r:
                at = r * ((PLAIN + BUILD) // RING) + PRE // RING
                for i in range(PLAIN // RING):
                    down_unit(at + i, r - 1, i)
                with sp.Fori(0, BUILD // RING) as i:
                    down_unit(at + i + PLAIN // RING)

            def load_ag(q, u, first=False):
                n = known(q * RING + u)
                free = known(q * RING + (u - RING + 1))
                if isinstance(q, int):
                    a_src, g_src = a_dram[n, :, :], g_dram[n, :, :]
                else:
                    a_src = a_dram[bass.ds(n, 1), :, :].rearrange("o p t -> p (o t)")
                    g_src = g_dram[bass.ds(n, 1), :, :].rearrange("o p t -> p (o t)")
                if not first:
                    sp.wait_ge(ga_done, free)
                sp.dma_start(a_in[:, u, :], a_src).then_inc(ag_loaded[u], 16)
                sp.dma_start(g_in[:, u, :], g_src).then_inc(ag_loaded[u], 16)

            for i in range(POST // RING - 1):
                down_unit((P - POST) // RING + i, TT - 1, i, POST - RING)
            sp.wait_ge(chunk_free, 1 + 16 * PIECES * TT)
            for slot in range(2):
                sp.wait_ge(a_stored[slot], 16 * (P - RING) // 2)
            for u in range(RING):
                load_ag(0, u, first=True)
            down_unit(P // RING - 1)
            for slot in range(2):
                sp.wait_ge(a_stored[slot], 16 * P // 2)
            sp.dma_start(fgain[:, :], final_gain).then_inc(f_loaded, 16)
            def up_unit(q, weights=True):
                for u in range(RING):
                    if weights or u < RING - 6 % RING:
                        load_weights(q + (B_UP // RING + (u + 6) // RING), (u + 6) % RING)
                    load_ag(q + 1, u)

            with sp.Fori(0, P // RING - 2) as q:
                up_unit(q)
            up_unit(P // RING - 2, weights=False)
            for t in range(TT):
                for half in range(2):
                    cols = slice(half * 512, (half + 1) * 512)
                    sp.wait_ge(f_done, 2 * t + half + 1)
                    sp.dma_start(out[0, t * P:(t + 1) * P, cols], acc[:, t, cols]).then_inc(stored, 16)
            sp.wait_ge(stored, 16 * 2 * TT)

        @block.gpsimd
        def _(pool):
            def split_low(q, u):
                pool.wait_ge(w_hi, q * RING + (u + 1))
                nc.gpsimd.tensor_tensor(w_l[:, u, :], raw[:, u, :], w_h[:, u, :].bitcast(F32), ALU.subtract).then_inc(w_lo, 1)

            for n in range(TT):
                cols = NORM_COLS[n]
                pool.wait_ge(nt_hi, n + 1)
                nc.gpsimd.tensor_tensor(xt_l[:, :, cols], ntmp[:, n % 2, :, 0:NORM_ROWS[n]], xt_h[:, :, cols].bitcast(F32),
                                        ALU.subtract).then_inc(nt_lo, 1)
            for b in range(LEAD):
                split_low(0, b)
            pool.wait_ge(t_loaded, 32)
            nc.gpsimd.tensor_copy(mean_r[:, :], table_cols(T_MEAN, P))
            nc.gpsimd.tensor_copy(sel_r[:, :], table_cols(T_SEL, MH * P, MH)).then_inc(const_ready, 1)
            for h in range(NH + 1):
                for s in range(4):
                    if h < NH:
                        b = 4 * h + s + LEAD
                        split_low(b // RING, b % RING)
                    if s == 0 and 1 <= h <= MH:
                        pool.wait_ge(d_done, h)
                        for j in range(KT):
                            late = META if j == 0 else 0
                            blk = decay[0:ROWS[j], S_AT[j]:S_AT[j] + ROWS[j] - late]
                            last = nc.gpsimd.affine_select(out=blk, in_=blk, compare_op=ALU.is_ge, fill=0.0, base=late,
                                                           pattern=[[1, ROWS[j] - late]], channel_multiplier=-1)
                        last.then_inc(masked, 1)
            for b in range(B_OUT + LEAD, B_QUERY):
                split_low(b // RING, b % RING)
            pool.wait_ge(y_lo, NH)
            nc.gpsimd.iota(iota16[:, :], [[1, P]], base=0, channel_multiplier=0,
                           allow_small_or_imprecise_dtypes=True).then_inc(iota_ready, 1)
            with pool.Fori(B_QUERY // RING, B_DOWN // RING) as q:
                for u in range(RING):
                    split_low(q, u)
            with pool.Fori(B_DOWN // RING, B_END // RING) as q:
                for u in range(RING):
                    split_low(q, u)

        @block.scalar
        def _(act):
            own = [0]

            def link(ins):
                own[0] += 1
                ins.then_inc(act_own, 1)
                act.wait_ge(act_own, own[0])

            def split_high(q, u, first=False):
                act.wait_ge(w_loaded[u], q * 16 + 16)
                if not first:
                    act.wait_ge(w_used, q * RING + (u - RING + 1))
                nc.scalar.copy(w_h[:, u, :], raw[:, u, :]).then_inc(w_hi, 1)

            def high(b):
                split_high(b // RING, b % RING, first=b < RING)

            def inv_rms(src, n, scratch, ready, rows=P):
                link(nc.scalar.activation(scratch, src, ACT.Square, accum_out=sums[0:rows, n:n + 1]))
                link(nc.scalar.activation(sums[0:rows, n:n + 1], sums[0:rows, n:n + 1], ACT.Ln, bias=EPS, scale=1.0 / D))
                nc.scalar.activation(rstd[0:rows, n:n + 1], sums[0:rows, n:n + 1], ACT.Exp, scale=-0.5).then_inc(ready, 1)

            def high_xt(n):
                tmp = ntmp if n <= TT else ntmp2
                act.wait_ge(nt_f, n + 1)
                nc.scalar.copy(xt_h[:, :, NORM_COLS[n]], tmp[:, n % 2, :, 0:NORM_ROWS[n]]).then_inc(nt_hi, 1)

            nc.scalar.preload_act_table_set("natural_log_exp_and_others")

            for n in range(TT + 1):
                t, rows = NORM_OF[n], NORM_ROWS[n]
                act.wait_ge(x_loaded[t], 16)
                src = acc[:, t, :] if t < TT else mt[:, :]
                inv_rms(src, n, junk[0:rows, :], nt_r, rows)
                if t == TT:
                    act.wait_ge(wg_loaded, 32)
                    nc.scalar.copy(wg_h[:, :], wg[:, :]).then_inc(wg_split_h, 1)
                if n >= 2:
                    high_xt(n - 2)
            high_xt(TT - 1)
            high_xt(TT)
            high(0)
            high(1)

            act.wait_ge(g_an, 1)
            link(nc.scalar.activation(hxc[0:MH, :], hx[0:MH, :], ACT.Exp))
            link(nc.scalar.activation(hxc[0:MH, 0:SEQ], hxc[0:MH, 0:SEQ], ACT.Ln, bias=1.0))
            act.wait_ge(g_an, 2)
            link(nc.scalar.activation(rot[0:MH, 0:META], rot[0:MH, 0:META], ACT.Exp))
            nc.scalar.activation(rot[0:MH, 0:META], rot[0:MH, 0:META], ACT.Ln, bias=1.0).then_inc(g_ln, 1)

            def split_gm():
                act.wait_ge(g_u, 1)
                nc.scalar.copy(gm_h[:, :, :], gm[:, :, XS]).then_inc(gm_hi, 1)

            for h in range(NH + 1):
                is_m = h < MH
                pair = h % 2
                if h < NH:
                    high(4 * h + LEAD)
                if h >= 1:
                    g = h - 1
                    act.wait_ge(vt_done, g + 1)
                    if g >= 2:
                        act.wait_ge(pv_done, g - 1)
                    nc.scalar.copy(v_tok[:, g % 2, :], ps[:, 7, :])
                    nc.scalar.copy(v_last[:, g % 2, :], ps[0:ROWS[TT], 4, 0:P]).then_inc(vt_ev, 1)
                    if g < MH:
                        act.wait_ge(bc_done, g + 1)
                        act.wait_ge(g_ready, 1)
                        if g >= 1:
                            act.wait_ge(p_done, g)
                            act.wait_ge(x_ready, g)
                        for j in range(KT):
                            nc.scalar.activation(decay[0:ROWS[j], S_AT[j]:S_AT[j + 1]], ps[0:ROWS[j], 5, T0[j]:SEQ], ACT.Exp,
                                                 bias=u_col[0:ROWS[j], j, g:g + 1], scale=-1.0)
                        nc.scalar.activation(floor[:, :], ps[:, 6, :], ACT.Exp, scale=-1.0).then_inc(d_done, 1)
                    if g >= 1:
                        act.wait_ge(y_ready, g)
                        nc.scalar.copy(y_h[:, g - 1, :], hy[:, :]).then_inc(y_hi, 1)
                if h < NH:
                    act.wait_ge(w_used, 4 * h + 1)
                    if is_m:
                        if h >= 2:
                            act.wait_ge(s_done, h - 1)
                        nc.scalar.copy(qT[:, pair, :], ps[:, 0, :]).then_inc(pj_ev, 1)
                    else:
                        if h > MH:
                            act.wait_ge(rope_done, h - MH)
                        nc.scalar.copy(q_raw[:, :], ps[:, 0, :]).then_inc(pj_ev, 1)
                    high(4 * h + 1 + LEAD)
                    act.wait_ge(w_used, 4 * h + 2)
                    dst = kT[:, pair, :] if is_m else k_raw[:, :]
                    nc.scalar.copy(dst[:, 0:FIRST], ps[:, 1, 0:FIRST])
                    nc.scalar.copy(dst[:, FIRST:TOK], ps[:, 2, 0:REST]).then_inc(pj_ev, 1)
                if h >= 1:
                    g = h - 1
                    if g < MH:
                        act.wait_ge(den_done, g + 1)
                        nc.scalar.activation(hden[:, :], ps[:, 3, :], ACT.Abs).then_inc(den_abs, 1)
                    else:
                        act.wait_ge(pv_done, g + 1)
                        nc.scalar.copy(part_h[:, :], ps[:, 7, :]).then_inc(x_hi, 1)
                        nc.scalar.copy(hx[:, :], ps[:, 7, :]).then_inc(x_ready, 1)
                if h < NH:
                    high(4 * h + 2 + LEAD)
                    if h == 0:
                        split_gm()
                    act.wait_ge(w_used, 4 * h + 3)
                    nc.scalar.copy(vT[:, 0:FIRST], ps[:, 0, 0:FIRST])
                    nc.scalar.copy(vT[:, FIRST:TOK], ps[:, 2, REST:2 * REST]).then_inc(pj_ev, 1)
                if h >= 1:
                    act.wait_ge(xc_ready, h)
                    nc.scalar.activation(hsq[:, :], hxc[:, :], ACT.Square).then_inc(sq_ready, 1)
                    act.wait_ge(sq_ready, h)
                    nc.scalar.copy(part_h[:, :], hsq[:, :]).then_inc(sq_hi, 1)
                if h < NH:
                    high(4 * h + 3 + LEAD)
                if h == NH - 1:
                    high(B_OUT + LEAD)
                if h < NH:
                    act.wait_ge(w_used, 4 * h + 4)
                    if h >= 2:
                        act.wait_ge(y_ready, h - 1)
                    if is_m:
                        nc.scalar.activation(og[:, pair, :], ps[:, 1, :], ACT.Exp, scale=-1.0).then_inc(pj_ev, 1)
                    else:
                        nc.scalar.copy(og[:, pair, :], ps[:, 1, :]).then_inc(pj_ev, 1)
                        act.wait_ge(pj_ev, 4 * h + 4)
                        nc.scalar.activation(eg[:, :], og[:, pair, :], ACT.Exp, scale=-1.0).then_inc(o_exp, 1)
                if h == NH - 1:
                    high(B_OUT + LEAD + 1)
                if h >= 1:
                    act.wait_ge(var_done, h)
                    link(nc.scalar.activation(hsq[:, :], ps[:, 3, :], ACT.Ln, bias=EPS))
                    nc.scalar.activation(hsq[:, :], hsq[:, :], ACT.Exp, scale=-0.5).then_inc(rstd_done, 1)
            act.wait_ge(y_ready, NH)
            nc.scalar.copy(y_h[:, NH - 1, :], hy[:, :]).then_inc(y_hi, 1)
            for b in range(B_OUT2, B_QUERY):
                high(b)

            for n in range(TT + 1, 2 * TT + 1):
                act.wait_ge(mix_added, n - TT)
                inv_rms(acc[:, n - TT - 1, :], n, junk_n2[:, :], nt_r)
                if n == 2 * TT - 1:
                    high(B_QUERY)
                if n >= TT + 2:
                    high_xt(n - 1)
                if n == 2 * TT - 1:
                    high(B_QUERY + 1)
            high_xt(2 * TT)

            def query(i, first=False):
                for p in range(2):
                    act.wait_ge(w_used, i * 2 + (B_QUERY + p + 1))
                    if not first:
                        act.wait_ge(sc_done, i * 2 + (p - 1))
                    nc.scalar.copy(qx[:, p, :], ps[:, p, :]).then_inc(qx_ready, 1)
                for p in range(2):
                    act.wait_ge(sc_done, i * 2 + (p + 1))
                    if not first:
                        act.wait_ge(sc_used, i * 2 + (p - 1))
                    nc.scalar.copy(sc[:, p, :, :], ps[:, 2 + p, :].rearrange("p (t n) -> p t n", t=TT)).then_inc(sc_ev, 1)

            for i in range(2):
                high(B_QUERY + 2 * i + LEAD)
                high(B_QUERY + 2 * i + 1 + LEAD)
                query(i, first=i == 0)
            with act.Fori(1, PH // 2) as i2:
                for half in range(2):
                    for p in range(2):
                        split_high(i2 + (B_QUERY // RING + half), (2 * half + p + LEAD) % RING)
                    query(i2 * 2 + half)

            def gelu(q, u, first=False):
                act.wait_ge(w_used, q * RING + (B_DOWN + u + 1))
                if not first:
                    act.wait_ge(a_stored[u % 2], q * 32 + 16 * (u // 2))
                nc.scalar.activation(a_out[:, u % 2, :], ps[:, u % 2, :], ACT.Gelu).then_inc(a_ready, 1)

            def down_tile(q, u, first=False):
                split_high(q + (B_DOWN // RING + (u + LEAD) // RING), (u + LEAD) % RING)
                gelu(q, u, first)

            for u in range(RING):
                down_tile(0, u, first=u < 2)
            with act.Fori(0, TT) as r:
                with act.Fori(0, PLAIN // RING - 1) as i:
                    for u in range(RING):
                        down_tile(r * ((PLAIN + BUILD) // RING) + i + PRE // RING, u)
                act.wait_ge(dist_ready, r + 1)
                nc.scalar.activation(expd[:, :, :], dist[:, :, :], ACT.Exp).then_inc(exp_ready, 1)
                for u in range(RING):
                    down_tile(r * ((PLAIN + BUILD) // RING) + (PLAIN + PRE) // RING - 1, u)
                act.wait_ge(chunk_free, r * (16 * PIECES) + 1)
                for i in range(BUILD // RING):
                    for u in range(RING):
                        down_tile(r * ((PLAIN + BUILD) // RING) + (PLAIN + PRE) // RING + i, u)
                        for k in range(PER_TILE):
                            n = (i * RING + u) * PER_TILE + k
                            act.wait_ge(gm_done, r * (P // BATCH) + (n + 1))
                            nc.scalar.activation(gchunk[:, :, n * BATCH:(n + 1) * BATCH].rearrange("p j t -> p t j"),
                                                 ps[:, 2 + n % 2, :].rearrange("p (t j) -> p t j", t=BATCH),
                                                 ACT.Copy, scale=1.0 / GSCALE).then_inc(g_ev, 1)
            with act.Fori(0, POST // RING - 1) as i:
                for u in range(RING):
                    down_tile(i + (P - POST) // RING, u)

            def high_ga(q, u, first=False):
                act.wait_ge(ga_done, q * RING + (u + 1))
                if not first:
                    act.wait_ge(w_used, q * RING + (B_UP + u - RING + 1))
                nc.scalar.copy(y_h[:, u, :], ga[:, u % 2, :]).then_inc(ga_hi, 1)

            for u in range(RING):
                down_tile(P // RING - 1, u)
                if u >= LEAD:
                    high_ga(0, u - LEAD, first=True)

            def up_tile(q, u):
                split_high(q + (B_UP // RING + (u + LEAD) // RING), (u + LEAD) % RING)
                high_ga(q + (u + LEAD) // RING, (u + LEAD) % RING, first=isinstance(q, int) and q == 0 and u < LEAD)

            for u in range(RING):
                up_tile(0, u)
            with act.Fori(1, P // RING - 1) as q:
                for u in range(RING):
                    up_tile(q, u)
            for u in range(RING - LEAD):
                up_tile(P // RING - 1, u)

            nc.scalar.preload_act_table_set("natural_log_exp_and_others")
            for t in range(TT):
                act.wait_ge(res_added, t + 1)
                inv_rms(acc[:, t, :], 2 * TT + 1 + t, junk2[:, :], f_r)

        @block.vector
        def _(dve):
            own = [0]

            def link(ins):
                own[0] += 1
                ins.then_inc(dve_own, 1)
                dve.wait_ge(dve_own, own[0])

            def scale_rows(n):
                t, rows = NORM_OF[n], NORM_ROWS[n]
                src = acc[:, t, :] if t < TT else mt[:, :]
                dve.wait_ge(nt_r, n + 1)
                if n >= 2:
                    dve.wait_ge(nt_tr, n - 1)
                nc.vector.tensor_scalar((xn if n <= TT else xn2)[0:rows, n % 2, :], src, rstd[0:rows, n:n + 1], None, ALU.mult).then_inc(nt_xn, 1)

            def apply_gain(n):
                width = NORM_ROWS[n]
                g0 = 0 if n <= TT else KD
                dve.wait_ge(nt_tr, n + 1)
                if n >= 2:
                    dve.wait_ge(nt_lo, n - 1)
                bank = norm_bank(n)
                src = ps[:, bank:bank + 2, :].rearrange("p b (k c) -> p (b k) c", c=P)
                nc.vector.tensor_tensor((ntmp if n <= TT else ntmp2)[:, n % 2, :, 0:width], src[:, :, 0:width],
                                        gain[:, g0:g0 + KD].unsqueeze(2).broadcast_to([P, KD, width]),
                                        ALU.mult).then_inc(nt_f, 1)

            def low_xt(n):
                cols = NORM_COLS[n]
                tmp = ntmp if n <= TT else ntmp2
                dve.wait_ge(nt_hi, n + 1)
                nc.vector.tensor_tensor(xt_l[:, :, cols], tmp[:, n % 2, :, :], xt_h[:, :, cols].bitcast(F32),
                                        ALU.subtract).then_inc(nt_lo, 1)

            dve.wait_ge(c_loaded, 32)
            for n in range(TT + 1):
                scale_rows(n)
                if NORM_OF[n] == TT:
                    dve.wait_ge(wg_split_h, 1)
                    nc.vector.tensor_tensor(wg_l[:, :], wg[:, :], wg_h[:, :].bitcast(F32), ALU.subtract).then_inc(wg_split, 1)
                if n >= 1:
                    apply_gain(n - 1)
            apply_gain(TT)
            dve.wait_ge(nt_lo, TT)
            low_xt(TT)

            gi, gf = (probs[0:MH, k * TOK:(k + 1) * TOK] for k in range(2))
            gs, gu = (decay[0:MH, k * TOK:(k + 1) * TOK] for k in range(2))
            gl, g1 = k_raw[0:MH, :], kT[0:MH, 1, :]
            dve.wait_ge(g_mm, 1)
            dve.wait_ge(wg_loaded, 32)
            for gate, row in ((gi, 0), (gf, F_ROW)):
                rows = slice(row, row + MH)
                for dst, bank in ((slice(0, FIRST), 4), (slice(FIRST, TOK), 5)):
                    last = nc.vector.tensor_scalar(gate[:, dst], ps[rows, bank, 0:dst.stop - dst.start], gb[rows, :], None, ALU.add)
            link(last)
            nc.vector.scalar_tensor_tensor(hx[0:MH, :], gf[:, META:TOK], -1.0, gf[:, META:TOK], ALU.mult, ALU.min).then_inc(g_an, 1)
            nc.vector.scalar_tensor_tensor(rot[0:MH, 0:META], gf[:, 0:META], -1.0, gf[:, 0:META], ALU.mult, ALU.min).then_inc(g_an, 1)
            link(nc.vector.memset(g1, 1.0))
            dve.wait_ge(g_ln, 1)
            link(nc.vector.scalar_tensor_tensor(gl[:, META:TOK], gf[:, META:TOK], 0.0, hxc[0:MH, :], ALU.min, ALU.subtract))
            link(nc.vector.scalar_tensor_tensor(gl[:, 0:META], gf[:, 0:META], 0.0, rot[0:MH, 0:META], ALU.min, ALU.subtract))
            link(nc.vector.tensor_tensor_scan(gs, g1, gl, 0.0, ALU.mult, ALU.add))
            link(nc.vector.tensor_tensor(gu, gi, gs, ALU.subtract))
            link(nc.vector.tensor_tensor_scan(gm[:, 0, :], g1, gu, 0.0, ALU.mult, ALU.max))
            nc.vector.tensor_tensor(gm[:, 1, :], gm[:, 0, :], gs, ALU.add).then_inc(g_u, 1)
            dve.wait_ge(g_ut, 1)
            nc.vector.tensor_copy(u_col[:, 0:TT, :], ps[:, 3, 0:TT * MH].rearrange("p (t h) -> p t h", h=MH))
            dve.wait_ge(gm_hi, 1)
            nc.vector.tensor_tensor(gm_l[:, :, :], gm[:, :, XS], gm_h[:, :, :].bitcast(F32), ALU.subtract).then_inc(gm_lo, 1)
            nc.vector.tensor_copy(u_col[0:ROWS[TT], TT, :], ps[0:ROWS[TT], 3, TT * MH:(TT + 1) * MH]).then_inc(g_ready, 1)

            dve.wait_ge(t_loaded, 32)
            for h in range(NH + 1):
                if h >= 1:
                    g = h - 1
                    gp = g % 2
                    if g >= MH:
                        dve.wait_ge(sw_done, g - MH + 1)
                        if g >= 2:
                            dve.wait_ge(s_done, g - 1)
                        cos, sin = table_cols(T_COS, TOK), table_cols(T_SIN, TOK)
                        link(nc.vector.tensor_tensor(rot[:, 0:SEQ], ps[:, 5, :], sin[:, XS], ALU.mult))
                        link(nc.vector.tensor_tensor(qT[:, gp, :], q_raw[:, :], cos[:, XS], ALU.mult))
                        link(nc.vector.tensor_tensor(qT[:, gp, :], qT[:, gp, :], rot[:, 0:SEQ], ALU.add))
                        nc.vector.tensor_tensor(rot[:, 0:SEQ], ps[:, 6, :], sin[:, 0:SEQ], ALU.mult)
                        link(nc.vector.tensor_tensor(rot[:, SEQ:TOK], ps[:, 2, 0:META], sin[:, SEQ:TOK], ALU.mult))
                        link(nc.vector.tensor_tensor(kT[:, gp, :], k_raw[:, :], cos, ALU.mult))
                        nc.vector.tensor_tensor(kT[:, gp, :], kT[:, gp, :], rot[:, :], ALU.add).then_inc(rope_done, 1)
                    if g >= 1:
                        dve.wait_ge(y_hi, g)
                        nc.vector.tensor_tensor(y_l[:, g - 1, :], hy[:, :], y_h[:, g - 1, :].bitcast(F32), ALU.subtract).then_inc(y_lo, 1)
                    dve.wait_ge(s_done, g + 1)
                    if g < MH:
                        dve.wait_ge(masked, g + 1)
                    if g >= 1:
                        dve.wait_ge(pv_done, g)
                    for j in range(KT):
                        bank, at = S_BANK[j]
                        rows, w = ROWS[j], COLS[j]
                        if g < MH:
                            dec = decay[0:rows, S_AT[j]:S_AT[j + 1]]
                        else:
                            dec = table_cols(T_DEC + (g - MH) * TOK + (META if j == 0 else 0), w, rows)
                        last = nc.vector.scalar_tensor_tensor(probs[0:rows, S_AT[j]:S_AT[j + 1]], ps[0:rows, bank, at:at + w], SCALE, dec,
                                                              ALU.mult, ALU.mult)
                    last.then_inc(p_done, 1)
                    if g >= MH:
                        dve.wait_ge(o_exp, g - MH + 1)
                        link(nc.vector.tensor_scalar(eg[:, :], eg[:, :], 1.0, None, ALU.add))
                        link(nc.vector.reciprocal(eg[:, :], eg[:, :]))
                        link(nc.vector.tensor_tensor(og[:, gp, :], og[:, gp, :], eg[:, :], ALU.mult))
                    if g < MH:
                        dve.wait_ge(den_abs, g + 1)
                        link(nc.vector.tensor_tensor(hden[:, :], hden[:, :], floor[:, :], ALU.max))
                        dve.wait_ge(pj_ev, 4 * g + 4)
                        link(nc.vector.scalar_tensor_tensor(hden[:, :], og[:, gp, :], 1.0, hden[:, :], ALU.add, ALU.mult))
                        link(nc.vector.reciprocal(hden[:, :], hden[:, :]))
                        dve.wait_ge(pv_done, g + 1)
                        nc.vector.tensor_tensor(hx[:, :], ps[:, 7, :], hden[:, :], ALU.mult).then_inc(x_ready, 1)
                    if g >= MH:
                        dve.wait_ge(x_ready, g + 1)
                        dve.wait_ge(x_hi, g - MH + 1)
                        nc.vector.tensor_tensor(part_l[:, :], hx[:, :], part_h[:, :].bitcast(F32), ALU.subtract).then_inc(x_lo, 1)
                    dve.wait_ge(mean_done, g + 1)
                    nc.vector.tensor_tensor(hxc[:, :], hx[:, :], ps[:, 4, :], ALU.subtract).then_inc(xc_ready, 1)
                    dve.wait_ge(sq_hi, g + 1)
                    nc.vector.tensor_tensor(part_l[:, :], hsq[:, :], part_h[:, :].bitcast(F32), ALU.subtract).then_inc(sq_lo, 1)
                    dve.wait_ge(rstd_done, g + 1)
                    head_gain = gain[:, 2 * KD + g:2 * KD + g + 1]
                    if g < MH:
                        nc.vector.scalar_tensor_tensor(hy[:, :], hxc[:, :], head_gain, hsq[:, :], ALU.mult, ALU.mult).then_inc(y_ready, 1)
                    else:
                        link(nc.vector.scalar_tensor_tensor(hxc[:, :], hxc[:, :], head_gain, hsq[:, :], ALU.mult, ALU.mult))
                        nc.vector.tensor_tensor(hy[:, :], hxc[:, :], og[:, gp, :], ALU.mult).then_inc(y_ready, 1)
            dve.wait_ge(y_hi, NH)
            nc.vector.tensor_tensor(y_l[:, NH - 1, :], hy[:, :], y_h[:, NH - 1, :].bitcast(F32), ALU.subtract).then_inc(y_lo, 1)

            def add_sums(t, done, last_used, added, by_half=False):
                for half in range(2):
                    if t < TT - 1 or (by_half and half == 0):
                        dve.wait_ge(done, t + 1)
                    else:
                        dve.wait_ge(w_used, last_used)
                    dst = acc[:, t, half * 512:(half + 1) * 512]
                    last = nc.vector.tensor_tensor(dst, dst, ps[:, 2 * t + half, :], ALU.add)
                last.then_inc(added, 1)

            for t in range(TT):
                add_sums(t, rows_done, B_QUERY, mix_added)
                if t >= 1:
                    apply_gain(TT + t)
                scale_rows(TT + 1 + t)
                if t >= 1:
                    low_xt(TT + t)
            apply_gain(2 * TT)
            low_xt(2 * TT)

            link(nc.vector.memset(fence_cell[:, 0:1], 0.0))

            def fence(semaphore, value, cell=0):
                dve.wait_ge(semaphore, value)
                nc.vector.tensor_copy(fence_cell[:, 1 + cell:2 + cell], fence_cell[:, 0:1])

            class Steps:

                def __init__(self, index, size):
                    self.index, self.size, self.start, self.n = index, size, own[0], 0

                def step(self, ins):
                    self.n += 1
                    ins.then_inc(dve_own, 1)

                def value(self):
                    return self.index * self.size + (self.start + self.n)

                def end(self, times):
                    assert self.n == self.size
                    own[0] += self.size * times

            with dve.Fori(0, PH) as h:
                steps = Steps(h, 8)
                for p in range(2):
                    fence(sc_ev, h * 2 + (p + 1), 1 + p)
                    for t in range(TT):
                        last = nc.vector.max(t8v[:, t, p, 0:8], sc[:, p, t, :])
                    steps.step(last)
                    fence(dve_own, steps.value())
                    for t in range(TT):
                        nc.vector.max_index(t8i[:, t, p, 0:8], t8v[:, t, p, 0:8], sc[:, p, t, :])
                    for t in range(TT):
                        last = nc.vector.match_replace(sc_rest[:, p, t, :], t8v[:, t, p, 0:8], sc[:, p, t, :], -3.0e38)
                    steps.step(last)
                    fence(dve_own, steps.value())
                    for t in range(TT):
                        last = nc.vector.max(t8v[:, t, p, 8:16], sc_rest[:, p, t, :])
                    steps.step(last)
                    fence(dve_own, steps.value())
                    for t in range(TT):
                        last = nc.vector.max_index(t8i[:, t, p, 8:16], t8v[:, t, p, 8:16], sc_rest[:, p, t, :])
                    last.then_inc(sc_used, 1)
                fence(sc_used, h * 2 + 2)
                steps.step(nc.vector.tensor_copy(topv[:, :, :, bass.ds(h, 1), :].rearrange("p t s o k -> p t s (o k)"), t8v[:, :, :, :]))
                steps.step(nc.vector.tensor_copy(topi[:, :, :, bass.ds(h, 1), :].rearrange("p t s o k -> p t s (o k)"), t8i[:, :, :, :]))
                fence(dve_own, steps.value())
            steps.end(PH)
            link(nc.vector.tensor_copy(fence_cell[:, 4:5], fence_cell[:, 0:1]))
            nc.vector.tensor_copy(fence_cell[:, 4:5], fence_cell[:, 0:1]).then_inc(chunk_free, 1)
            dve.wait_ge(iota_ready, 1)

            with dve.Fori(0, TT) as r:
                steps = Steps(r, 19)
                step = steps.step

                def behind():
                    dve.wait_ge(dve_own, steps.value())

                def of_tile(tops, s):
                    return tops[:, bass.ds(r, 1), s, :, :].rearrange("p o h k -> p (o h) k")

                cand4 = cand[:, :, :].rearrange("p h (a b) -> p h a b", b=TOPK)
                step(nc.vector.tensor_tensor(cand4, of_tile(topv, 0).unsqueeze(3).broadcast_to([P, PH, TOPK, TOPK]),
                                             of_tile(topv, 1).unsqueeze(2).broadcast_to([P, PH, TOPK, TOPK]), ALU.add))
                fence(dve_own, steps.value())
                for h in range(PH):
                    last = nc.vector.max(tv[:, h, 0:8], cand[:, h, :])
                step(last)
                fence(dve_own, steps.value())
                for h in range(PH):
                    last = nc.vector.max_index(ti[:, h * TOPK:h * TOPK + 8], tv[:, h, 0:8], cand[:, h, :])
                step(last)
                fence(dve_own, steps.value())
                for h in range(PH):
                    last = nc.vector.match_replace(cand[:, h, :], tv[:, h, 0:8], cand[:, h, :], -3.0e38)
                step(last)
                fence(dve_own, steps.value())
                for h in range(PH):
                    last = nc.vector.max(tv[:, h, 8:16], cand[:, h, :])
                step(last)
                fence(dve_own, steps.value())
                nc.vector.tensor_tensor(dist[:, :, :], tv[:, :, :], tv[:, :, 0:1].broadcast_to([P, PH, TOPK]),
                                        ALU.subtract).then_inc(dist_ready, 1)
                for h in range(PH):
                    last = nc.vector.max_index(ti[:, h * TOPK + 8:(h + 1) * TOPK], tv[:, h, 8:16], cand[:, h, :])
                step(last)
                behind()
                nc.vector.tensor_scalar(tj[:, 0, :], ti[:, :], 4, None, ALU.logical_shift_right)
                step(nc.vector.tensor_scalar(tj[:, 1, :], ti[:, :], 15, None, ALU.bitwise_and))
                behind()
                step(nc.vector.tensor_copy(tf[:, :, :], tj[:, :, :]))
                for s in range(2):
                    behind()
                    step(nc.vector.tensor_tensor(eq[:, :, :], tf[:, s, :].unsqueeze(2).broadcast_to([P, P, TOPK]),
                                                 iota16[:, 0:TOPK].unsqueeze(1).broadcast_to([P, P, TOPK]), ALU.is_equal))
                    behind()
                    step(nc.vector.tensor_tensor(pick[:, :, :, :], eq[:, :, :].rearrange("p (h k) a -> p h k a", h=PH),
                                                 of_tile(topi, s).unsqueeze(2).broadcast_to([P, PH, TOPK, TOPK]), ALU.mult))
                    behind()
                    step(nc.vector.tensor_reduce(route[:, s, :], pick[:, :, :, :].rearrange("p h k a -> p (h k) a"), AX.X, ALU.add))
                dve.wait_ge(exp_ready, r + 1)
                step(nc.vector.tensor_reduce(den8[:, 0, :], expd[:, :, :], AX.X, ALU.add))
                behind()
                step(nc.vector.reciprocal(den8[:, 1, :], den8[:, 0, :]))
                behind()
                nc.vector.scalar_tensor_tensor(route[:, 2, :].rearrange("p (h k) -> p h k", h=PH), expd[:, :, :], GSCALE,
                                               den8[:, 1, :].unsqueeze(2).broadcast_to([P, PH, TOPK]), ALU.mult, ALU.mult).then_inc(route_ready, 1)
                dve.wait_ge(route_tr, r + 1)
                nc.vector.tensor_copy(route_t[:, :, :], ps[:, 4, 0:3 * P].rearrange("p (i t) -> p i t", i=3))
                step(nc.vector.tensor_copy(gh16[:, :], ps[:, 4, 2 * P:3 * P]))
                behind()
                step(nc.vector.tensor_copy(gate_h[:, :], gh16[:, :]))
                behind()
                step(nc.vector.tensor_tensor(gate_l[:, :], route_t[:, 2, :], gate_h[:, :], ALU.subtract))
                behind()
                for n in range(P // BATCH):
                    slot = n % 2
                    if n >= 2:
                        dve.wait_ge(gm_done, r * (P // BATCH) + (n - 1))
                    for c in range(BATCH):
                        t = n * BATCH + c
                        nc.vector.tensor_scalar(onehot[:, slot, 0, c, :], iota16[:, :], route_t[:, 0, t:t + 1], None, ALU.is_equal)
                        nc.vector.tensor_scalar(onehot[:, slot, 1, c, :], iota16[:, :], route_t[:, 1, t:t + 1], gate_h[:, t:t + 1],
                                                ALU.is_equal, ALU.mult)
                        last = nc.vector.tensor_scalar(onehot[:, slot, 2, c, :], iota16[:, :], route_t[:, 1, t:t + 1], gate_l[:, t:t + 1],
                                                       ALU.is_equal, ALU.mult)
                    last.then_inc(oh_ready, 1)
            steps.end(TT)

            def weigh(q, u, first=False):
                dve.wait_ge(ag_loaded[u], q * 32 + 32)
                if not first:
                    dve.wait_ge(ga_lo, q * RING + (u - 1))
                nc.vector.tensor_tensor(ga[:, u % 2, :], a_in[:, u, :], g_in[:, u, :], ALU.mult).then_inc(ga_done, 1)
                dve.wait_ge(ga_hi, q * RING + (u + 1))
                nc.vector.tensor_tensor(y_l[:, u, :], ga[:, u % 2, :], y_h[:, u, :].bitcast(F32), ALU.subtract).then_inc(ga_lo, 1)

            for u in range(RING):
                weigh(0, u, first=u < 2)
            with dve.Fori(1, P // RING) as q:
                for u in range(RING):
                    weigh(q, u)

            dve.wait_ge(f_loaded, 16)
            for t in range(TT):
                add_sums(t, up_rows_done, B_END, res_added, by_half=True)
                n = 2 * TT + 1 + t
                dve.wait_ge(f_r, t + 1)
                for half in range(2):
                    cols = slice(half * 512, (half + 1) * 512)
                    nc.vector.scalar_tensor_tensor(acc[:, t, cols], acc[:, t, cols], rstd[:, n:n + 1], fgain[:, cols],
                                                   ALU.mult, ALU.mult).then_inc(f_done, 1)

        @block.tensor
        def _(pe):
            def three(out_ap, stat, mov, first=True, last=True):
                for i, (s_, m_) in enumerate(((stat[0], mov[0]), (stat[0], mov[1]), (stat[1], mov[0]))):
                    ins = nc.tensor.matmul(out_ap, s_, m_, start=first and i == 0, stop=last and i == 2)
                return ins

            def project(u, bank, width=SEQ, cols=XS, at=0):
                for k in range(KD):
                    ws = (w_h[:, u, k * P:(k + 1) * P], w_l[:, u, k * P:(k + 1) * P])
                    ins = three(ps[:, bank, at:at + width], ws, (xt_h[:, k, cols], xt_l[:, k, cols]), k == 0, k == KD - 1)
                return ins

            def norm_tile(n):
                rows = NORM_ROWS[n]
                pe.wait_ge(nt_xn, n + 1)
                if n >= 2:
                    pe.wait_ge(nt_f, n - 1)
                for k in range(KD):
                    bank = norm_bank(n) + k // 4
                    at = (k % 4) * P
                    ins = nc.tensor.transpose(ps[:, bank, at:at + rows], (xn if n <= TT else xn2)[0:rows, n % 2, k * P:(k + 1) * P], ident[0:rows, 0:rows])
                ins.then_inc(nt_tr, 1)

            pe.wait_ge(c_loaded, 32)
            for n in range(TT + 1):
                norm_tile(n)

            pe.wait_ge(wg_split, 1)
            for bank, cols in ((4, slice(0, FIRST)), (5, slice(FIRST, TOK))):
                pe.wait_ge(nt_lo, 3 if bank == 4 else TT + 1)
                for k in range(KD):
                    at = k * G_ROWS
                    ins = three(ps[0:G_ROWS, bank, 0:cols.stop - cols.start], (wg_h[:, at:at + G_ROWS], wg_l[:, at:at + G_ROWS]),
                                (xt_h[:, k, cols], xt_l[:, k, cols]), k == 0, k == KD - 1)
            ins.then_inc(g_mm, 1)

            def by_constant(bank, constant, high_part, low_part):
                nc.tensor.matmul(ps[:, bank, :], constant, high_part, start=True, stop=False)
                return nc.tensor.matmul(ps[:, bank, :], constant, low_part, start=False, stop=True)

            def out_rows(j, banks):
                u = (B_OUT + j) % RING
                for bank in banks:
                    cols = slice((bank // 2) * P, (bank // 2 + 1) * P)
                    ins = three(ps[:, bank, :], (y_h[:, j, cols], y_l[:, j, cols]),
                                tuple(w_[:, u, (bank % 2) * 512:(bank % 2 + 1) * 512] for w_ in (w_h, w_l)), j == 0, j == KD - 1)
                return ins

            for h in range(NH + 1):
                is_m = h < MH
                g, gp = h - 1, (h - 1) % 2
                hp = h % 2

                def block_of(s):
                    b = 4 * h + s
                    pe.wait_ge(w_lo, b + 1)
                    if b >= 2:
                        pe.wait_ge(pj_ev, b - 1)
                    return b

                if h < NH:
                    b = block_of(0)
                    project(b % RING, 0).then_inc(w_used, 1)
                if h == NH:
                    pe.wait_ge(pj_ev, 4 * NH)
                    pe.wait_ge(y_lo, 4)
                    for j in range(4):
                        pe.wait_ge(w_lo, B_OUT + j + 1)
                        out_rows(j, (0, 1))
                if h >= 1:
                    pe.wait_ge(vt_ev, g + 1)
                    if g >= 1:
                        pe.wait_ge(rstd_done, g)
                    if g < MH:
                        pe.wait_ge(d_done, g + 1)
                    else:
                        pe.wait_ge(rope_done, g - MH + 1)
                    for j in range(KT):
                        bank, at = S_BANK[j]
                        ins = nc.tensor.matmul(ps[0:ROWS[j], bank, at:at + COLS[j]], kT[:, gp, j * P:j * P + ROWS[j]], qT[:, gp, T0[j]:SEQ],
                                               start=True, stop=True)
                    ins.then_inc(s_done, 1)
                if h < NH:
                    b = block_of(1)
                    project(b % RING, 1, FIRST, slice(0, FIRST))
                    if h > MH:
                        pe.wait_ge(rope_done, h - MH)
                    project(b % RING, 2, REST, slice(FIRST, TOK), 0).then_inc(w_used, 1)
                if h == NH:
                    for j in range(4):
                        out_rows(j, (2,))
                if h >= 1:
                    pe.wait_ge(p_done, g + 1)

                    def over_keys(bank, stats):
                        for j in range(KT):
                            ins = nc.tensor.matmul(ps[:, bank, T0[j]:SEQ], stats[j], probs[0:ROWS[j], S_AT[j]:S_AT[j + 1]],
                                                   start=j == 0, stop=j == KT - 1)
                        return ins

                    if g < MH:
                        over_keys(3, [table_cols(T_ONE, P, rows) for rows in ROWS]).then_inc(den_done, 1)
                    over_keys(7, [v_tok[:, gp, j * P:(j + 1) * P] for j in range(TT)] + [v_last[:, gp, :]]).then_inc(pv_done, 1)
                if h < NH:
                    b = block_of(2)
                    project(b % RING, 0, FIRST, slice(0, FIRST))
                    pe.wait_ge(pj_ev, 4 * h + 2)
                    project(b % RING, 2, REST, slice(FIRST, TOK), REST).then_inc(w_used, 1)
                if h == NH:
                    for j in range(2):
                        out_rows(j, (5,))
                if h >= 1:
                    pe.wait_ge(x_ready, g + 1)
                    if g < MH:
                        nc.tensor.matmul(ps[:, 4, :], table_cols(T_MEAN, P), hx[:, :], start=True, stop=True).then_inc(mean_done, 1)
                    else:
                        pe.wait_ge(x_lo, g - MH + 1)
                        by_constant(4, mean_r[:, :], part_h[:, :], part_l[:, :]).then_inc(mean_done, 1)
                if h < NH:
                    b = block_of(3)
                    project(b % RING, 1).then_inc(w_used, 1)
                if h == NH:
                    for j in range(2, 4):
                        out_rows(j, (5,))
                    out_rows(0, (6,))
                if h >= 1:
                    pe.wait_ge(sq_lo, g + 1)
                    by_constant(3, mean_r[:, :], part_h[:, :], part_l[:, :]).then_inc(var_done, 1)
                if h < NH:
                    if is_m:
                        if h == 0:
                            pe.wait_ge(t_loaded, 32)
                            pe.wait_ge(const_ready, 1)
                            pe.wait_ge(g_u, 1)
                            for j in range(TT):
                                nc.tensor.transpose(ps[:, 3, j * MH:(j + 1) * MH],
                                                    decay[0:MH, TOK + j * P:TOK + (j + 1) * P], ident[0:MH, 0:MH])
                            nc.tensor.transpose(ps[0:ROWS[TT], 3, TT * MH:(TT + 1) * MH], decay[0:MH, TOK + TT * P:2 * TOK],
                                                ident[0:MH, 0:MH]).then_inc(g_ut, 1)
                            pe.wait_ge(gm_lo, 1)
                        for bank, row in ((5, 0), (6, 1)):
                            ins = by_constant(bank, sel_r[:, h * P:(h + 1) * P], gm_h[:, row, :], gm_l[:, row, :])
                        ins.then_inc(bc_done, 1)
                    else:
                        pe.wait_ge(pj_ev, 4 * h + 3)
                        swap = table_cols(T_SWAP, P)
                        nc.tensor.matmul(ps[:, 5, :], swap, q_raw[:, :], start=True, stop=True)
                        nc.tensor.matmul(ps[:, 6, :], swap, k_raw[:, 0:SEQ], start=True, stop=True)
                        nc.tensor.matmul(ps[:, 2, 0:META], swap, k_raw[:, SEQ:TOK], start=True, stop=True).then_inc(sw_done, 1)
                    pe.wait_ge(pj_ev, 4 * h + 3)
                    for j in range(TT):
                        nc.tensor.transpose(ps[:, 7, j * P:(j + 1) * P], vT[:, j * P:(j + 1) * P], ident[:, :])
                    nc.tensor.transpose(ps[0:META, 4, 0:P], vT[:, SEQ:TOK], ident[:, :]).then_inc(vt_done, 1)

            def add_rows(u, slot, first, last, order=range(TT), before={}, halves=(0, 1)):
                for t in order:
                    if t in before:
                        before[t]()
                    cols = slice(t * P, (t + 1) * P)
                    for i, (y_, w_) in enumerate(((y_h, w_h), (y_h, w_l), (y_l, w_h))):
                        for half in halves:
                            ins = nc.tensor.matmul(ps[:, 2 * t + half, :], y_[:, slot, cols], w_[:, u, half * 512:(half + 1) * 512],
                                                   start=first and i == 0, stop=last and i == 2)
                return ins

            for j in range(1, 4):
                out_rows(j, (6,))
            pe.wait_ge(rstd_done, NH)
            for j in range(4):
                out_rows(j, (7, 3, 4)).then_inc(w_used, 1)
            for t in range(TT):
                for j in range(4, KD):
                    if t == 0:
                        pe.wait_ge(w_lo, B_OUT + j + 1)
                        if j == KD - 1:
                            pe.wait_ge(y_lo, NH)
                    ins = out_rows(j, (2 * t, 2 * t + 1))
                    if t == TT - 1:
                        ins.then_inc(w_used, 1)
                    elif j == KD - 1:
                        ins.then_inc(rows_done, 1)
                if t >= 1:
                    norm_tile(TT + t)

            half = SEQ // 2
            pe.wait_ge(nt_lo, TT + 3)
            for p in range(2):
                pe.wait_ge(w_lo, B_QUERY + p + 1)
                project(p, p, half, slice(META, META + half))
                if p == 0:
                    norm_tile(2 * TT)
            pe.wait_ge(nt_lo, 2 * TT + 1)

            def query(i, u0, first=False):
                for p in range(2):
                    pe.wait_ge(w_lo, i * 2 + (B_QUERY + p + 1))
                    if not first:
                        pe.wait_ge(qx_ready, i * 2 + (p - 1))
                    if first:
                        project(u0 + p, p, half, slice(META + half, TOK), half).then_inc(w_used, 1)
                    else:
                        project(u0 + p, p).then_inc(w_used, 1)
                for p in range(2):
                    pe.wait_ge(qx_ready, i * 2 + (p + 1))
                    if not first:
                        pe.wait_ge(sc_ev, i * 2 + (p - 1))
                    for t in range(TT):
                        ins = nc.tensor.matmul(ps[:, 2 + p, t * P:(t + 1) * P], qx[:, p, t * P:(t + 1) * P], keys_t[:, p, :],
                                               start=True, stop=True)
                    ins.then_inc(sc_done, 1)

            query(0, 0, first=True)
            query(1, 2)
            with pe.Fori(1, PH // 2) as i2:
                for half in range(2):
                    query(i2 * 2 + half, 2 * half)

            def down_tile(q, u, first=False, between={}):
                pe.wait_ge(w_lo, q * RING + (B_DOWN + u + 1))
                if not first:
                    pe.wait_ge(a_ready, q * RING + (u - 1))
                for k in range(KD):
                    ws = (w_h[:, u, k * P:(k + 1) * P], w_l[:, u, k * P:(k + 1) * P])
                    ins = three(ps[:, u % 2, :], ws, (xt_h[:, k, XS], xt_l[:, k, XS]), k == 0, k == KD - 1)
                    if k in between:
                        between[k]()
                ins.then_inc(w_used, 1)

            for u in range(RING):
                down_tile(0, u, first=u < 2)
            with pe.Fori(0, TT) as r:
                with pe.Fori(0, PLAIN // RING - 1) as i:
                    for u in range(RING):
                        down_tile(r * ((PLAIN + BUILD) // RING) + i + PRE // RING, u)

                def turn_routing():
                    pe.wait_ge(route_ready, r + 1)
                    for i in range(3):
                        ins = nc.tensor.transpose(ps[:, 4, i * P:(i + 1) * P], route[:, i, :], ident[:, :])
                    ins.then_inc(route_tr, 1)

                for u in range(RING):
                    down_tile(r * ((PLAIN + BUILD) // RING) + (PLAIN + PRE) // RING - 1, u,
                              between={0: turn_routing} if u == RING - 2 else {})

                def gate_batch(n):
                    pe.wait_ge(oh_ready, r * (P // BATCH) + (n + 1))
                    if n >= 2:
                        pe.wait_ge(g_ev, r * (P // BATCH) + (n - 1))
                    for c in range(BATCH):
                        for part in (1, 2):
                            ins = nc.tensor.matmul(ps[:, 2 + n % 2, c * P:(c + 1) * P], onehot[:, n % 2, 0, c, :],
                                                   onehot[:, n % 2, part, c, :], start=part == 1, stop=part == 2)
                    ins.then_inc(gm_done, 1)

                for i in range(BUILD // RING):
                    for u in range(RING):
                        n0 = (i * RING + u) * PER_TILE
                        step = KD // PER_TILE
                        between = {step * (k + 1) - 2: (lambda n=n0 + k: gate_batch(n)) for k in range(PER_TILE)}
                        down_tile(r * ((PLAIN + BUILD) // RING) + (PLAIN + PRE) // RING + i, u, between=between)
            with pe.Fori(0, POST // RING) as i:
                for u in range(RING):
                    down_tile(i + (P - POST) // RING, u)

            pe.wait_ge(g_ev, TT * P // BATCH)

            def up_tile(q, u, first=False, last=False):
                pe.wait_ge(w_lo, q * RING + (B_UP + u + 1))
                pe.wait_ge(ga_lo, q * RING + (u + 1))
                if first:
                    add_rows(u, u, first, last, order=(1, 2, 3, 0),
                             before={0: lambda: pe.wait_ge(a_ready, P)}).then_inc(w_used, 1)
                else:
                    add_rows(u, u, first, last).then_inc(w_used, 1)

            for u in range(RING):
                up_tile(0, u, first=u == 0)
            with pe.Fori(1, P // RING - 1) as q:
                for u in range(RING):
                    up_tile(q, u)
            for t in range(TT - 1):
                for u in range(RING):
                    if t == 0:
                        pe.wait_ge(w_lo, B_END - RING + u + 1)
                        pe.wait_ge(ga_lo, P - RING + u + 1)
                    ins = add_rows(u, u, False, u == RING - 1, order=(t,))
                ins.then_inc(up_rows_done, 1)
            for u in range(RING):
                ins = add_rows(u, u, False, u == RING - 1, order=(TT - 1,), halves=(0,))
            ins.then_inc(up_rows_done, 1)
            for u in range(RING):
                add_rows(u, u, False, u == RING - 1, order=(TT - 1,), halves=(1,)).then_inc(w_used, 1)


def _tables():
    import numpy as np
    tab = np.zeros((P, T_END), np.float32)
    pos = np.arange(TOK).astype(np.float32)
    half = P // 2
    inv = (np.float32(10000.0) ** (-np.arange(half, dtype=np.float32) / np.float32(half))).astype(np.float32)
    ang = (pos[None, :] * inv[:, None]).astype(np.float32)
    cos, sin = np.cos(ang.astype(np.float64)), np.sin(ang.astype(np.float64))
    tab[:, T_COS:T_COS + TOK] = np.concatenate([cos, cos], 0)
    tab[:, T_SIN:T_SIN + TOK] = np.concatenate([-sin, sin], 0)
    gap = np.arange(TOK)[None, :] - np.arange(P)[:, None]
    for h in range(RH):
        lg = math.log1p(-2.0 ** (-5.0 - h))
        tab[:, T_DEC + h * TOK:T_DEC + (h + 1) * TOK] = np.where(gap >= 0, np.exp(lg * np.maximum(gap, 0)), 0.0)
    for m in range(P):
        tab[(m + half) % P, T_SWAP + m] = 1.0
    tab[:, T_ONE:T_ONE + P] = 1.0
    tab[:, T_MEAN:T_MEAN + P] = 1.0 / P
    for h in range(MH):
        tab[h, T_SEL + h * P:T_SEL + (h + 1) * P] = 1.0
    return tab

def kernel(x, meta_tokens, norm1_w, w_in, gate_bias, m_norm_w, r_norm_w, w_out, norm2_w,
           peer_w_query, peer_sub_keys, peer_w_down, peer_w_up, final_norm_w):
    import numpy as np
    import concourse.bacc as bacc
    from concourse.bass_utils import run_bass_kernel_spmd

    def columns(w):
        w = np.asarray(w)
        n = w.shape[1] // P
        return w.reshape(KD, P, n, P).transpose(2, 1, 0, 3).reshape(n, P, D)

    def gate_rows(g):
        rows = np.zeros(g.shape[:-1] + (G_ROWS,), g.dtype)
        rows[..., :MH] = g[..., :MH]
        rows[..., F_ROW:] = g[..., MH:]
        return rows

    w_in0 = np.asarray(w_in)[0]
    head_cols = [part * MH * P + h * P for h in range(MH) for part in range(4)]
    head_cols += [(4 + part) * RH * P + h * P for h in range(RH) for part in range(4)]
    by_head = np.concatenate([w_in0[:, c:c + P] for c in head_cols], axis=1)
    down = np.asarray(peer_w_down)[0].reshape(P, P, KD, P).transpose(1, 3, 2, 0).reshape(P, P, D)
    up = np.asarray(peer_w_up)[0].reshape(P, P, D).transpose(1, 0, 2)
    arrays = {
        "x": np.asarray(x),
        "meta": np.asarray(meta_tokens),
        "w_blocks": np.concatenate([columns(by_head), np.asarray(w_out)[0].reshape(KD, P, D),
                                    columns(np.asarray(peer_w_query)[0]), down, up], axis=0),
        "w_gates": gate_rows(w_in0[:, 4 * (MH + RH) * P:]).reshape(KD, P, G_ROWS).transpose(1, 0, 2).reshape(P, KD * G_ROWS),
        "gate_bias": gate_rows(np.asarray(gate_bias)).reshape(G_ROWS, 1),
        "gains": np.concatenate([np.asarray(norm1_w).reshape(KD, P), np.asarray(norm2_w).reshape(KD, P),
                                 np.asarray(m_norm_w).reshape(MH, P), np.asarray(r_norm_w).reshape(RH, P)], axis=0).T,
        "final_gain": np.broadcast_to(np.asarray(final_norm_w)[None], (P, D)),
        "keys": np.asarray(peer_sub_keys)[0].transpose(2, 0, 1),
        "ident": np.eye(P, dtype=np.float32),
        "table": _tables(),
    }
    nc = bacc.Bacc("TRN2", target_bir_lowering=False, num_devices=1)
    args = {}
    for name in arrays:
        arrays[name] = np.ascontiguousarray(arrays[name])
        args[name] = nc.dram_tensor("in_" + name, arrays[name].shape, F32, kind="ExternalInput").ap()
    out = nc.dram_tensor("out_dram", (1, SEQ, D), F32, kind="ExternalOutput").ap()
    mixer_peer_kernel(nc, args["x"], args["meta"], args["w_blocks"], args["w_gates"], args["gate_bias"],
                      args["gains"], args["final_gain"], args["keys"], args["ident"], args["table"], out)
    r = run_bass_kernel_spmd(nc, [{"in_" + n: a for n, a in arrays.items()}], core_ids=[0])
    return r.results[0]["out_dram"]
```
